# Optimizing a Trainium2 kernel written in Bass

```python
import math
import jax, jax.numpy as jnp
from jax import lax
import numpy as np

D_MODEL = 1024
BATCH = 1
SEQ = 256
DEPTH = 2

N_A = DEPTH // 2
N_B = DEPTH - N_A

D_FF = 2816

D_RNN = 1280
N_GATE_BLOCKS = 5
GATE_BW = D_RNN // N_GATE_BLOCKS
CONV_WIDTH = 4
LRU_C = 8.0

N_HEADS = 16
HEAD_DIM = D_MODEL // N_HEADS
DILATION_PAIRS = ((128, 1), (512, 4), (2048, 16))
N_GROUPS = len(DILATION_PAIRS)

DEEPNORM_ALPHA = float((2 * DEPTH) ** 0.25)
DEEPNORM_BETA = float((8 * DEPTH) ** -0.25)

LN_EPS = 1e-5
NEG_INF = -1e30


def layer_norm(x, g, b):
    xf = x.astype(jnp.float32)
    mu = jnp.mean(xf, axis=-1, keepdims=True)
    xc = xf - mu
    var = jnp.mean(xc * xc, axis=-1, keepdims=True)
    y = xc * lax.rsqrt(var + LN_EPS) * g.astype(jnp.float32) + b.astype(jnp.float32)
    return y.astype(x.dtype)

def swiglu(x, w_in, w_out):
    gate, up = jnp.split(x @ w_in, 2, axis=-1)
    return (jax.nn.silu(gate) * up) @ w_out

def causal_depthwise_conv(u, w, b):
    r = u.shape[-1]
    rhs = w.astype(u.dtype)[:, None, :]
    y = lax.conv_general_dilated(
        u, rhs, window_strides=(1,), padding=[(CONV_WIDTH - 1, 0)],
        dimension_numbers=("NWC", "WIO", "NWC"), feature_group_count=r)
    return y + b.astype(u.dtype)

def rg_lru(u, gate_w, gate_b, lam):
    uf = u.astype(jnp.float32)
    bsz, s, r = uf.shape
    ublk = uf.reshape(bsz, s, N_GATE_BLOCKS, GATE_BW)
    gates = jnp.einsum("bsnc,gncd->gbsnd", ublk, gate_w.astype(jnp.float32)).reshape(2, bsz, s, r)
    gates = gates + gate_b.astype(jnp.float32)[:, None, None, :]
    rec_gate = jax.nn.sigmoid(gates[0])
    in_gate = jax.nn.sigmoid(gates[1])
    log_a = -LRU_C * rec_gate * jax.nn.softplus(-lam.astype(jnp.float32))
    a = jnp.exp(log_a)
    b = jnp.sqrt(-jnp.expm1(2.0 * log_a)) * (in_gate * uf)

    def combine(left, right):
        a1, b1 = left
        a2, b2 = right
        return a1 * a2, a2 * b1 + b2

    _, h = lax.associative_scan(combine, (a, b), axis=1)
    return h

def rglru_block(x, w_in, conv_w, conv_b, gate_w, gate_b, lam, w_out):
    y_br, u_br = jnp.split(x @ w_in, 2, axis=-1)
    y = jax.nn.gelu(y_br)
    u = causal_depthwise_conv(u_br, conv_w, conv_b)
    h = rg_lru(u, gate_w, gate_b, lam)
    return (y * h.astype(y.dtype)) @ w_out

def alibi_slopes(n):
    return jnp.exp2(-8.0 * (jnp.arange(n, dtype=jnp.float32) + 1.0) / n)

def dilated_group(q, k, v, slopes, window, dilation):
    bsz, s, h, dh = q.shape
    reach = window // dilation
    blk = reach
    unit = dilation * blk
    s_pad = -(-s // unit) * unit
    length = s_pad // dilation
    nb = length // blk

    def to_blocks(t):
        t = jnp.pad(t, ((0, 0), (0, s_pad - s), (0, 0), (0, 0)))
        t = t.reshape(bsz, length, dilation, h, dh).transpose(0, 2, 1, 3, 4)
        return t.reshape(bsz, dilation, nb, blk, h, dh)

    def with_prev(t):
        prev = jnp.pad(t, ((0, 0), (0, 0), (1, 0), (0, 0), (0, 0), (0, 0)))[:, :, :-1]
        return jnp.concatenate([prev, t], axis=3)

    qb = to_blocks(q)
    kw = with_prev(to_blocks(k))
    vw = with_prev(to_blocks(v))

    scores = jnp.einsum("bpnqhd,bpnkhd->bpnhqk", qb, kw) * (1.0 / math.sqrt(dh))
    q_idx = jnp.arange(blk)[:, None] + blk
    k_idx = jnp.arange(2 * blk)[None, :]
    dist = q_idx - k_idx
    key_abs = jnp.arange(nb)[:, None] * blk - blk + k_idx
    valid = ((dist >= 0) & (dist <= reach))[None] & (key_abs >= 0)[:, None, :]
    bias = -slopes[:, None, None] * (dist * dilation).astype(jnp.float32)[None]
    scores = jnp.where(valid[:, None], scores + bias, NEG_INF)

    m = jnp.max(scores, axis=-1, keepdims=True)
    p = jnp.exp(scores - m)
    denom = jnp.sum(p, axis=-1, keepdims=True)
    lse = (m + jnp.log(denom))[..., 0]
    out = jnp.einsum("bpnhqk,bpnkhd->bpnqhd", p / denom, vw)

    out = out.reshape(bsz, dilation, length, h, dh).transpose(0, 2, 1, 3, 4).reshape(bsz, s_pad, h, dh)[:, :s]
    lse = lse.transpose(0, 1, 2, 4, 3).reshape(bsz, dilation, length, h).transpose(0, 2, 1, 3).reshape(bsz, s_pad, h)[:, :s]
    return out, lse

def dilated_attention(x, k, v, w_q, w_o):
    bsz, s, _ = x.shape
    q = (x @ w_q).reshape(bsz, s, N_GROUPS, N_HEADS, HEAD_DIM).astype(jnp.float32)
    slopes = alibi_slopes(N_HEADS)
    outs, lses = [], []
    for g, (window, dilation) in enumerate(DILATION_PAIRS):
        o, l = dilated_group(q[:, :, g], k, v, slopes, window, dilation)
        outs.append(o)
        lses.append(l)
    wts = jax.nn.softmax(jnp.stack(lses, axis=0), axis=0)
    out = jnp.sum(wts[..., None] * jnp.stack(outs, axis=0), axis=0)
    return out.reshape(bsz, s, N_HEADS * HEAD_DIM).astype(x.dtype) @ w_o

def first_inputs(seed: int = 0) -> dict:
    key = jax.random.key(seed)
    ks = jax.random.split(key, 20)
    f32 = jnp.float32
    nrm = lambda k, shape, scale: jax.random.normal(k, shape, f32) * scale

    x = jax.random.normal(ks[0], (BATCH, SEQ, D_MODEL), f32)
    ln_g = 1.0 + nrm(ks[1], (DEPTH, 3, D_MODEL), 0.02)
    ln_b = nrm(ks[2], (DEPTH, 3, D_MODEL), 0.02)
    ffn_w_in = nrm(ks[3], (DEPTH, 2, D_MODEL, 2 * D_FF), D_MODEL ** -0.5)
    ffn_w_out = nrm(ks[4], (DEPTH, 2, D_FF, D_MODEL), D_FF ** -0.5 * DEEPNORM_BETA)

    rg_w_in = nrm(ks[5], (N_A, D_MODEL, 2 * D_RNN), D_MODEL ** -0.5)
    rg_conv_w = nrm(ks[6], (N_A, CONV_WIDTH, D_RNN), CONV_WIDTH ** -0.5)
    rg_conv_b = nrm(ks[7], (N_A, D_RNN), 0.02)
    rg_gate_w = nrm(ks[8], (N_A, 2, N_GATE_BLOCKS, GATE_BW, GATE_BW), GATE_BW ** -0.5)
    rg_gate_b = nrm(ks[9], (N_A, 2, D_RNN), 0.02)
    a0 = jax.random.uniform(ks[10], (N_A, D_RNN), f32, 0.9, 0.999)
    rg_lam = jnp.log(a0) - jnp.log1p(-a0)
    rg_w_out = nrm(ks[11], (N_A, D_RNN, D_MODEL), D_RNN ** -0.5 * DEEPNORM_BETA)

    kv_w = nrm(ks[12], (D_MODEL, 2 * N_HEADS * HEAD_DIM), D_MODEL ** -0.5)
    attn_w_q = nrm(ks[13], (N_B, D_MODEL, N_GROUPS * N_HEADS * HEAD_DIM), D_MODEL ** -0.5)
    attn_w_o = nrm(ks[14], (N_B, N_HEADS * HEAD_DIM, D_MODEL), (N_HEADS * HEAD_DIM) ** -0.5 * DEEPNORM_BETA)
    return {
        "x": x, "ln_g": ln_g, "ln_b": ln_b, "ffn_w_in": ffn_w_in, "ffn_w_out": ffn_w_out,
        "rg_w_in": rg_w_in, "rg_conv_w": rg_conv_w, "rg_conv_b": rg_conv_b,
        "rg_gate_w": rg_gate_w, "rg_gate_b": rg_gate_b, "rg_lam": rg_lam, "rg_w_out": rg_w_out,
        "kv_w": kv_w, "attn_w_q": attn_w_q, "attn_w_o": attn_w_o,
    }

def first_block(x, ln_g, ln_b, ffn_w_in, ffn_w_out, rg_w_in, rg_conv_w, rg_conv_b,
              rg_gate_w, rg_gate_b, rg_lam, rg_w_out, kv_w, attn_w_q, attn_w_o):
    bsz, s, _ = x.shape
    k_shared = None
    v_shared = None
    for layer in range(DEPTH):
        x = layer_norm(DEEPNORM_ALPHA * x + 0.5 * swiglu(x, ffn_w_in[layer, 0], ffn_w_out[layer, 0]),
                       ln_g[layer, 0], ln_b[layer, 0])
        if layer < N_A:
            j = layer
            mix = rglru_block(x, rg_w_in[j], rg_conv_w[j], rg_conv_b[j], rg_gate_w[j],
                              rg_gate_b[j], rg_lam[j], rg_w_out[j])
        else:
            j = layer - N_A
            mix = dilated_attention(x, k_shared, v_shared, attn_w_q[j], attn_w_o[j])
        x = layer_norm(DEEPNORM_ALPHA * x + mix, ln_g[layer, 1], ln_b[layer, 1])
        x = layer_norm(DEEPNORM_ALPHA * x + 0.5 * swiglu(x, ffn_w_in[layer, 1], ffn_w_out[layer, 1]),
                       ln_g[layer, 2], ln_b[layer, 2])
        if layer == N_A - 1:
            kv = (x @ kv_w).reshape(bsz, s, 2, N_HEADS, HEAD_DIM).astype(jnp.float32)
            k_shared = kv[:, :, 0]
            v_shared = kv[:, :, 1]
    return x


N_META = 16
CHUNK = 128
PAD = (-N_META) % CHUNK
RET_HEADS = 4
RET_DK = 48
RET_DV = 96
RET_QK = RET_HEADS * RET_DK
RET_W = RET_HEADS * RET_DV
POOL_WINDOWS = (2, 4, 8, 16)
POOL_GROUP = 64
POOL_W = len(POOL_WINDOWS) * POOL_GROUP
FOX_HEADS = 6
FOX_DH = 64
FOX_W = FOX_HEADS * FOX_DH
D_MIX = RET_W + POOL_W + FOX_W
IN_SPLITS = (RET_QK, RET_QK, RET_W, RET_W, POOL_W, FOX_W, FOX_W, FOX_W, FOX_HEADS)
D_IN = sum(IN_SPLITS)
D_FF_2 = -(-8 * D_MODEL // (3 * 256)) * 256
ROPE_BASE = 10000.0
NEG_INF_2 = -1e30
ALPHA = (2.0 * DEPTH) ** 0.25
BETA = (8.0 * DEPTH) ** -0.25


def layer_norm_2(x, g, b):
    xf = x.astype(jnp.float32)
    mu = jnp.mean(xf, axis=-1, keepdims=True)
    var = jnp.mean(jnp.square(xf - mu), axis=-1, keepdims=True)
    y = (xf - mu) * lax.rsqrt(var + LN_EPS)
    return (y * g + b).astype(x.dtype)

def pad_front(a):
    widths = [(0, 0), (PAD, 0)] + [(0, 0)] * (a.ndim - 2)
    return jnp.pad(a, widths)

def rotary(x, cos, sin):
    half = x.shape[-1] // 2
    x1, x2 = x[..., :half], x[..., half:]
    return jnp.concatenate([x1 * cos - x2 * sin, x1 * sin + x2 * cos], axis=-1)

def retention_chunkwise(q, k, v):
    Bsz, Lp, H, dk = q.shape
    dv = v.shape[-1]
    n = Lp // CHUNK
    gamma = 1.0 - 2.0 ** (-5.0 - jnp.arange(H, dtype=jnp.float32))
    lg = jnp.log(gamma)
    i = jnp.arange(CHUNK, dtype=jnp.float32)
    diff = i[:, None] - i[None, :]
    dmask = jnp.where(diff >= 0, jnp.exp(lg[:, None, None] * jnp.maximum(diff, 0.0)), 0.0)
    xi = jnp.exp(lg[:, None] * (i + 1.0))
    zeta = jnp.exp(lg[:, None] * (CHUNK - 1.0 - i))
    chunk_decay = jnp.exp(lg * CHUNK)
    qc = q.astype(jnp.float32).reshape(Bsz, n, CHUNK, H, dk)
    kc = k.astype(jnp.float32).reshape(Bsz, n, CHUNK, H, dk) * (dk ** -0.5)
    vc = v.astype(jnp.float32).reshape(Bsz, n, CHUNK, H, dv)
    scores = jnp.einsum('bnihd,bnjhd->bnhij', qc, kc) * dmask
    inner = jnp.einsum('bnhij,bnjhe->bnihe', scores, vc)
    kv = jnp.einsum('bnjhd,hj,bnjhe->nbhde', kc, zeta, vc)

    def step(state, kv_n):
        return state * chunk_decay[None, :, None, None] + kv_n, state

    _, prev = lax.scan(step, jnp.zeros_like(kv[0]), kv)
    cross = jnp.einsum('bnihd,nbhde,hi->bnihe', qc, prev, xi)
    return (inner + cross).reshape(Bsz, Lp, H, dv)

def multiscale_pool(u, pool_w, pool_scale):
    Bsz, L, _ = u.shape
    G = len(POOL_WINDOWS)
    uf = u.astype(jnp.float32).reshape(Bsz, L, G, POOL_GROUP)
    cs = jnp.concatenate([jnp.zeros((Bsz, 1, G, POOL_GROUP), jnp.float32),
                          jnp.cumsum(uf, axis=1)], axis=1)
    t = jnp.arange(L)
    outs = []
    for g, w in enumerate(POOL_WINDOWS):
        lo = jnp.maximum(t + 1 - w, 0)
        cnt = (t + 1 - lo).astype(jnp.float32)
        window_sum = cs[:, t + 1, g] - cs[:, lo, g]
        outs.append(window_sum / cnt[None, :, None] - uf[:, :, g])
    pooled = jnp.stack(outs, axis=2)
    y = jnp.einsum('blgc,gcd->blgd', pooled, pool_w.astype(jnp.float32)).reshape(Bsz, L, POOL_W)
    return y * pool_scale

def forgetting_attention(q, k, v, logf):
    Bsz, Lp, H, d = q.shape
    c = jnp.cumsum(logf.astype(jnp.float32), axis=1).transpose(0, 2, 1)
    qf = q.astype(jnp.float32) * (d ** -0.5)
    kf = k.astype(jnp.float32)
    vf = v.astype(jnp.float32)
    kpos = jnp.arange(Lp)
    key_ok = kpos >= PAD
    nb = Lp // CHUNK

    def block(ib):
        start = ib * CHUNK
        qb = lax.dynamic_slice_in_dim(qf, start, CHUNK, axis=1)
        cb = lax.dynamic_slice_in_dim(c, start, CHUNK, axis=2)
        qpos = start + jnp.arange(CHUNK)
        s = jnp.einsum('bihd,bjhd->bhij', qb, kf)
        s = s + cb[..., :, None] - c[..., None, :]
        mask = (kpos[None, :] <= qpos[:, None]) & key_ok[None, :]
        s = jnp.where(mask, s, NEG_INF_2)
        p = jax.nn.softmax(s, axis=-1)
        return jnp.einsum('bhij,bjhd->bihd', p, vf)

    out = lax.map(block, jnp.arange(nb))
    return out.transpose(1, 0, 2, 3, 4).reshape(Bsz, Lp, H, d)

def head_group_norm(o, g):
    of = o.astype(jnp.float32)
    mu = jnp.mean(of, axis=-1, keepdims=True)
    var = jnp.mean(jnp.square(of - mu), axis=-1, keepdims=True)
    y = ((of - mu) * lax.rsqrt(var + LN_EPS)).reshape(o.shape[0], o.shape[1], -1)
    return y * g

def hybrid_layer(h, w_in, b_f, ret_gn_g, pool_w, pool_scale, w_out,
                 ln1_g, ln1_b, w1, w3, w2, ln2_g, ln2_b, cos, sin):
    Bsz, L, _ = h.shape
    proj = jnp.einsum('bld,de->ble', h, w_in)
    parts = []
    off = 0
    for sz in IN_SPLITS:
        parts.append(proj[..., off:off + sz])
        off += sz
    q_r, k_r, v_r, g_r, u_p, q_f, k_f, v_f, f_logit = parts

    qr = rotary(pad_front(q_r.reshape(Bsz, L, RET_HEADS, RET_DK)), cos, sin)
    kr = rotary(pad_front(k_r.reshape(Bsz, L, RET_HEADS, RET_DK)), cos, sin)
    vr = pad_front(v_r.reshape(Bsz, L, RET_HEADS, RET_DV))
    o_r = retention_chunkwise(qr, kr, vr)[:, PAD:]
    o_r = jax.nn.silu(g_r.astype(jnp.float32)) * head_group_norm(o_r, ret_gn_g)

    o_p = multiscale_pool(u_p, pool_w, pool_scale)

    logf = jax.nn.log_sigmoid(f_logit.astype(jnp.float32) + b_f)
    o_f = forgetting_attention(pad_front(q_f.reshape(Bsz, L, FOX_HEADS, FOX_DH)),
                               pad_front(k_f.reshape(Bsz, L, FOX_HEADS, FOX_DH)),
                               pad_front(v_f.reshape(Bsz, L, FOX_HEADS, FOX_DH)),
                               pad_front(logf))[:, PAD:].reshape(Bsz, L, FOX_W)

    mix = jnp.concatenate([o_r, o_p, o_f], axis=-1)
    mix = jnp.einsum('ble,ed->bld', mix, w_out)
    h = layer_norm_2(ALPHA * h + mix, ln1_g, ln1_b)

    a = jnp.einsum('bld,df->blf', h, w1)
    b = jnp.einsum('bld,df->blf', h, w3)
    y = jnp.einsum('blf,fd->bld', jax.nn.silu(a) * b, w2)
    return layer_norm_2(ALPHA * h + y, ln2_g, ln2_b)

def second_inputs(seed: int = 0) -> dict:
    key = jax.random.key(seed)
    ks = jax.random.split(key, 20)
    f32 = jnp.float32
    x = jax.random.normal(ks[0], (BATCH, SEQ, D_MODEL), f32)
    meta = jax.random.normal(ks[1], (N_META, D_MODEL), f32)
    ln_emb_g = 1.0 + 0.01 * jax.random.normal(ks[2], (D_MODEL,), f32)
    ln_emb_b = 0.01 * jax.random.normal(ks[3], (D_MODEL,), f32)
    w_in = jax.random.normal(ks[4], (DEPTH, D_MODEL, D_IN), f32) * D_MODEL ** -0.5
    b_f = jax.random.uniform(ks[5], (DEPTH, FOX_HEADS), f32, 1.0, 4.0)
    ret_gn_g = 1.0 + 0.01 * jax.random.normal(ks[6], (DEPTH, RET_W), f32)
    pool_w = jax.random.normal(ks[7], (DEPTH, len(POOL_WINDOWS), POOL_GROUP, POOL_GROUP), f32) * POOL_GROUP ** -0.5
    pool_scale = 1.0 + 0.1 * jax.random.normal(ks[8], (DEPTH, POOL_W), f32)
    w_out = jax.random.normal(ks[9], (DEPTH, D_MIX, D_MODEL), f32) * (D_MIX ** -0.5) * BETA
    ln1_g = 1.0 + 0.01 * jax.random.normal(ks[10], (DEPTH, D_MODEL), f32)
    ln1_b = 0.01 * jax.random.normal(ks[11], (DEPTH, D_MODEL), f32)
    w_ffn1 = jax.random.normal(ks[12], (DEPTH, D_MODEL, D_FF_2), f32) * D_MODEL ** -0.5
    w_ffn3 = jax.random.normal(ks[13], (DEPTH, D_MODEL, D_FF_2), f32) * D_MODEL ** -0.5
    w_ffn2 = jax.random.normal(ks[14], (DEPTH, D_FF_2, D_MODEL), f32) * (D_FF_2 ** -0.5) * BETA
    ln2_g = 1.0 + 0.01 * jax.random.normal(ks[15], (DEPTH, D_MODEL), f32)
    ln2_b = 0.01 * jax.random.normal(ks[16], (DEPTH, D_MODEL), f32)
    return {'x': x, 'meta': meta, 'ln_emb_g': ln_emb_g, 'ln_emb_b': ln_emb_b,
            'w_in': w_in, 'b_f': b_f, 'ret_gn_g': ret_gn_g, 'pool_w': pool_w,
            'pool_scale': pool_scale, 'w_out': w_out, 'ln1_g': ln1_g, 'ln1_b': ln1_b,
            'w_ffn1': w_ffn1, 'w_ffn3': w_ffn3, 'w_ffn2': w_ffn2,
            'ln2_g': ln2_g, 'ln2_b': ln2_b}

def second_block(x, meta, ln_emb_g, ln_emb_b, w_in, b_f, ret_gn_g, pool_w, pool_scale,
              w_out, ln1_g, ln1_b, w_ffn1, w_ffn3, w_ffn2, ln2_g, ln2_b):
    Bsz = x.shape[0]
    h = jnp.concatenate([jnp.broadcast_to(meta[None].astype(x.dtype), (Bsz, N_META, D_MODEL)), x], axis=1)
    h = layer_norm_2(h, ln_emb_g, ln_emb_b)
    L = h.shape[1]
    Lp = L + PAD
    pos = jnp.arange(Lp, dtype=jnp.float32) - PAD
    inv_freq = ROPE_BASE ** (-jnp.arange(RET_DK // 2, dtype=jnp.float32) / (RET_DK // 2))
    ang = pos[:, None] * inv_freq[None, :]
    cos = jnp.cos(ang)[:, None, :]
    sin = jnp.sin(ang)[:, None, :]
    for l in range(DEPTH):
        h = hybrid_layer(h, w_in[l], b_f[l], ret_gn_g[l], pool_w[l], pool_scale[l], w_out[l],
                         ln1_g[l], ln1_b[l], w_ffn1[l], w_ffn3[l], w_ffn2[l], ln2_g[l], ln2_b[l],
                         cos, sin)
    return h[:, N_META:]


def setup_inputs(seed=0):
    out = dict(first_inputs(seed))
    for name, value in second_inputs(seed + 1).items():
        if name != "x":
            out[name + "_2"] = value
    return out


def reference(
    x, ln_g, ln_b, ffn_w_in, ffn_w_out, rg_w_in, rg_conv_w, rg_conv_b, rg_gate_w, rg_gate_b,
    rg_lam, rg_w_out, kv_w, attn_w_q, attn_w_o, meta_2, ln_emb_g_2, ln_emb_b_2, w_in_2, b_f_2,
    ret_gn_g_2, pool_w_2, pool_scale_2, w_out_2, ln1_g_2, ln1_b_2, w_ffn1_2, w_ffn3_2, w_ffn2_2,
    ln2_g_2, ln2_b_2,
):
    x = first_block(
        x, ln_g, ln_b, ffn_w_in, ffn_w_out, rg_w_in, rg_conv_w, rg_conv_b, rg_gate_w, rg_gate_b,
        rg_lam, rg_w_out, kv_w, attn_w_q, attn_w_o,
    )
    return second_block(
        x, meta_2, ln_emb_g_2, ln_emb_b_2, w_in_2, b_f_2, ret_gn_g_2, pool_w_2, pool_scale_2,
        w_out_2, ln1_g_2, ln1_b_2, w_ffn1_2, w_ffn3_2, w_ffn2_2, ln2_g_2, ln2_b_2,
    )


_drawn_inputs = setup_inputs


def setup_inputs(seed=0):
    import zlib

    import numpy as np

    out = dict(_drawn_inputs(seed))
    spreads = {}
    factors = {'rg_conv_b': 5.294,
     'rg_gate_b': 8.0,
     'ln_emb_g_2': 5.212,
     'ln_emb_b_2': 5.05,
     'ret_gn_g_2': 8.0,
     'ln1_g_2': 3.87,
     'ln1_b_2': 3.765,
     'ln2_g_2': 4.111,
     'ln2_b_2': 3.903}
    for name, (base, spread) in spreads.items():
        noise = np.random.default_rng([zlib.crc32(name.encode()), seed]).standard_normal(out[name].shape)
        drawn = base * np.exp(spread * noise) if base else spread * noise
        out[name] = __import__('jax').numpy.asarray(drawn.astype(out[name].dtype))
    for name, factor in factors.items():
        out[name] = (out[name] * factor).astype(out[name].dtype)
    return out
```

```python
import numpy as np
import concourse.bass as bass
from concourse import mybir

P = 128
D = 1024
KD = D // P
SEQ = 256
META = 16
TOK = SEQ + META
FF = 2816
KF = FF // P
HALF_F = KF // 2
RNN = 1280
KR = RNN // P
GATE_BLOCKS = 5
CONV = 4
HEADS = 16
GROUPS = 3
PAIRS = HEADS // 2
HD = 64
DILATIONS = ((128, 1), (512, 4), (2048, 16))
SCORES = GROUPS * P + GROUPS * SEQ
RET_HEADS, RET_DK, RET_DV = 4, 48, 96
HALF_DK = RET_DK // 2
POOL_WINDOWS = (2, 4, 8, 16)
POOL_PAD = max(POOL_WINDOWS)
FOX_HEADS, FOX_W = 6, 384
LOGIT_ROW = RET_DV
LAYERS_2 = 2
ALPHA = float(4.0 ** 0.25)
LN_EPS = 1e-5
SLOTS = 4
AHEAD = 2
CHUNK = HALF_F * P
KEY_COLS = (TOK, TOK - P, TOK - 2 * P)
KEY_AT = (0, TOK, TOK + KEY_COLS[1])
KEYS_ALL = sum(KEY_COLS)
FOX_SCORES = P + 2 * P + TOK
MIX_K = RET_HEADS + 2 + 3
WIN_TILES = 23
FOX0, ROT0, VR0, GATE0, POOL0 = 1, 10, 14, 18, 21

N_LN = 11
C_G, C_B = 0, N_LN * KD
C_CW = 2 * N_LN * KD
C_CB = C_CW + CONV * KR
C_GB = C_CB + KR
C_LAM = C_GB + 2 * KR
C_GN = C_LAM + KR
C_PS = C_GN + LAYERS_2 * RET_HEADS
C_BF = C_PS + LAYERS_2 * 2
N_PAR = C_BF + LAYERS_2

B_EXP = 0
B_SEL = B_EXP + RET_HEADS * P
B_ONE = B_SEL + FOX_HEADS * P
B_COS = B_ONE + TOK
B_SIN = B_COS + TOK
B_DEC = B_SIN + TOK
B_MASK = B_DEC + RET_HEADS * KEYS_ALL
B_CNT = B_MASK + FOX_SCORES
B_HEAD = B_CNT + 2 * TOK
N_B = B_HEAD + RET_HEADS * RET_HEADS


class Stage:

    def __init__(self, name, chunks, tiles, units):
        self.name, self.chunks, self.tiles, self.units = name, chunks, tiles, units
        self.cols = tiles * P
        self.n0 = self.u0 = 0


def plan():
    ffn = lambda f: [Stage(f"in{f}", 2 * KF, KD, KF), Stage(f"out{f}", 2 * KD, HALF_F, KD)]
    s = ffn(0)
    s += [Stage("rg_u", KR, KD, KR), Stage("rg_gate", GATE_BLOCKS, 8, GATE_BLOCKS),
          Stage("rg_y", KR, KD, KR), Stage("rg_out", KD, KR, KD)]
    s += ffn(1) + [Stage("kv", 2 * KD, KD, 2 * KD)] + ffn(2)
    s += [Stage("q", GROUPS * PAIRS, KD, GROUPS * PAIRS), Stage("o", KD, KD, KD)] + ffn(3)
    for l in range(LAYERS_2):
        s += [Stage(f"mix{l}", WIN_TILES, KD, WIN_TILES), Stage(f"mixo{l}", KD, MIX_K, KD)] + ffn(4 + l)
    n, u = 0, SLOTS
    for st in s:
        st.n0, st.u0 = n, u
        n += st.chunks
        u += st.units
    for a, b in zip(s, s[1:]):
        a.next = b
    s[-1].next = None
    return s


def build(nc, x_in, meta_in, par_in, con_in, bias_in, con2_in, poolw_in, weights, out):
    fp32, fp32r = mybir.dt.float32, mybir.dt.float32r
    ALU, ACT = mybir.AluOpType, mybir.ActivationFunctionType
    AX = mybir.AxisListType
    stages = plan()
    by_name = {st.name: st for st in stages}

    first = -(-nc.sbuf_base // 32) * 32
    slab_bytes = nc.sbuf_usable_end - first - 64
    slab = nc.sbuf_tensor("slab", [P, slab_bytes // 4], fp32)
    slab.__enter__()
    cursor = [first]

    def place(name, free, dtype=fp32):
        t = nc.alloc_sbuf_tensor_at(name, [P, *free], dtype, offset=cursor[0])
        cursor[0] += -(-4 * int(np.prod(free)) // 32) * 32
        assert cursor[0] <= first + slab_bytes, name
        return t

    raw = [place(f"raw{i}", [CHUNK]) for i in range(SLOTS)]
    whi = [place(f"whi{i}", [CHUNK], fp32r) for i in range(SLOTS)]
    wlo = [place(f"wlo{i}", [CHUNK], fp32r) for i in range(SLOTS)]
    x_hi = place("x_hi", [KD, TOK], fp32r)
    x_lo = place("x_lo", [KD, TOK], fp32r)
    ax = place("ax", [KD, TOK])
    r_at = cursor[0]
    r = place("r", [KD, TOK])
    sq_at = cursor[0]
    sq = place("sq", [KD, TOK])
    hhi_at = cursor[0]
    h_hi = place("h_hi", [KF, TOK], fp32r)
    hlo_at = cursor[0]
    h_lo = place("h_lo", [KF, TOK], fp32r)
    con = place("con", [3 * P])
    ident, ones_d, ones_head = con[:, 0:P], con[:, P:2 * P], con[:, 2 * P:3 * P]
    par = place("par", [N_PAR])
    ab = place("ab", [N_LN * KD])
    eps = place("eps", [1])
    std = place("std", [TOK])
    rstd = place("rstd", [TOK])
    sgate = place("sgate", [2, TOK])
    prod = place("prod", [2, TOK])
    spc = place("spc", [KR])
    nspc = place("nspc", [KR])
    lser = place("lser", [5, KR])
    mix_at = cursor[0]

    uc = place("uc", [KR, SEQ])
    dec = place("dec", [KR, SEQ])
    tnh = place("tnh", [KR, SEQ])
    ybr = place("ybr", [KR, SEQ])
    a2 = place("a2", [2, SEQ])
    cursor[0] = mix_at
    kT = place("kT", [KD, SEQ])
    v_tok = place("v_tok", [2, D])
    qT = place("qT", [2, GROUPS, SEQ])
    dist = place("dist", [SCORES])
    s_at = place("s_at", [2, SCORES])
    nmax = place("nmax", [2, 2])
    den = place("den", [2, 2])
    rden = place("rden", [2, 2])
    dg = place("dg", [2, 2, P])
    pT = place("pT", [2, GROUPS * P])
    cursor[0] = mix_at
    con2 = place("con2", [N_B])
    poolw = place("poolw", [LAYERS_2, 2, P])
    gsb = place("gsb", [RET_HEADS, TOK])
    qf = place("qf", [3, TOK])
    kf = place("kf", [3, TOK])
    vf_tok = place("vf_tok", [3, FOX_W])
    vr_tok = place("vr_tok", [3, RET_HEADS * P])
    cursor[0] = sq_at
    upad = place("upad", [2, CONV - 1 + SEQ])
    cursor[0] = sq_at
    vf = place("vf", [3, TOK])
    vr = place("vr", [RET_HEADS, TOK])
    cursor[0] = sq_at
    osb = place("osb", [RET_HEADS, TOK])
    cursor[0] = r_at
    up = place("up", [2, POOL_PAD + TOK])
    w_a = place("w_a", [2, POOL_PAD + TOK])
    w_b = place("w_b", [2, POOL_PAD + TOK])
    std4 = place("std4", [TOK])
    cursor[0] = hhi_at + 10 * TOK * 4
    s_fox = place("s_fox", [2, FOX_SCORES])
    pT_fox = place("pT_fox", [2, KEYS_ALL])
    dg_fox = place("dg_fox", [2, 3, P])
    nmax_f = place("nmax_f", [2, 3])
    den_f = place("den_f", [2, 3])
    rden_f = place("rden_f", [2, 3])
    assert cursor[0] <= hlo_at
    cursor[0] = hlo_at + 10 * TOK * 4
    rot_in = place("rot_in", [4, TOK])
    rot = place("rot", [4, TOK])
    rtmp = place("rtmp", [2, TOK])
    sqh = place("sqh", [2, TOK])
    assert cursor[0] <= hlo_at + KF * TOK * 4

    psum = nc.psum_tensor("psum", [P, 8, 512], fp32)
    ps = psum.__enter__()

    sems = []

    def sem(name):
        s = nc.semaphore(name)
        sems.append(s)
        return s.__enter__()

    inputs_in = sem("inputs_in")
    bias_landed = sem("bias_landed")
    con2_landed = sem("con2_landed")
    raw_landed = [sem(f"raw_landed{i}") for i in range(SLOTS)]
    w_hi_done = sem("w_hi_done")
    w_lo_done = sem("w_lo_done")
    chunk_used = sem("chunk_used")
    acc_free = sem("acc_free")
    x_hi_done = sem("x_hi_done")
    x_ready = sem("x_ready")
    ax_done = sem("ax_done")
    gate_done = sem("gate_done")
    h_hi_done = sem("h_hi_done")
    h_ready = sem("h_ready")
    mean_done = sem("mean_done")
    xc_done = sem("xc_done")
    sq_done = sem("sq_done")
    var_done = sem("var_done")
    std_done = sem("std_done")
    xn_done = sem("xn_done")
    y_done = sem("y_done")
    out_landed = sem("out_landed")
    dve_step = sem("dve_step")
    act_step = sem("act_step")
    par_done = sem("par_done")
    ser_e = sem("ser_e")
    spc_done = sem("spc_done")
    u_raw = sem("u_raw")
    pad_zero = sem("pad_zero")
    conv_done = sem("conv_done")
    u_hi_done = sem("u_hi_done")
    u_ready = sem("u_ready")
    in_gate = sem("in_gate")
    tanh_done = sem("tanh_done")
    iu_done = sem("iu_done")
    dec_done = sem("dec_done")
    v_arg = sem("v_arg")
    v_root = sem("v_root")
    gelu_done = sem("gelu_done")
    vT_done = sem("vT_done")
    v_copied = sem("v_copied")
    scored = sem("scored")
    biased = sem("biased")
    nmax_done = sem("nmax_done")
    probs = sem("probs")
    dg_done = sem("dg_done")
    pT_done = sem("pT_done")
    pT_copied = sem("pT_copied")
    pv_done = sem("pv_done")
    at_hi = sem("at_hi")
    at_ready = sem("at_ready")
    fx_done = sem("fx_done")
    fe_done = sem("fe_done")
    c_done = sem("c_done")
    vt2_done = sem("vt2_done")
    vt2_copied = sem("vt2_copied")
    rot_done = sem("rot_done")
    up_zero = sem("up_zero")
    pool_done = sem("pool_done")
    pool_mm = sem("pool_mm")
    pool_hi = sem("pool_hi")
    pool_ready = sem("pool_ready")
    ret_s = sem("ret_s")
    ret_d = sem("ret_d")
    ret_o = sem("ret_o")
    ret_osb = sem("ret_osb")
    ret_mean = sem("ret_mean")
    ret_xc = sem("ret_xc")
    ret_sq = sem("ret_sq")
    ret_var = sem("ret_var")
    ret_std = sem("ret_std")
    ret_rstd = sem("ret_rstd")
    ret_bc = sem("ret_bc")
    silu2 = sem("silu2")
    ret_hi = sem("ret_hi")
    ret_ready = sem("ret_ready")

    block_guard = nc.Block()
    block = block_guard.__enter__()

    def steps(eng, count, body, start=0):
        full = (count - AHEAD) // SLOTS
        for s in range(SLOTS * start):
            body(s // SLOTS, s % SLOTS)
        if full - start > 1:
            with eng.Fori(start, full) as i:
                for j in range(SLOTS):
                    body(i, j)
        else:
            full = start
        for s in range(SLOTS * full, count):
            body(s // SLOTS, s % SLOTS)

    def at(st, i, j):
        return SLOTS * i + (st.n0 + j), (st.n0 + j) % SLOTS, i + (st.n0 + j) // SLOTS

    def ahead(st, i, j):
        cols = st.cols
        if isinstance(i, int) and SLOTS * i + j + AHEAD >= st.chunks:
            if st.next is None:
                return None
            cols = st.next.cols
        return *at(st, i, j + AHEAD), cols

    norms = [("out0", SEQ, "x"), ("rg_out", SEQ, "x"), ("out1", SEQ, "x"), ("out2", SEQ, "x"),
             ("o", SEQ, "x"), ("out3", SEQ, "y"), ("emb", TOK, "x"), ("mixo0", TOK, "x"),
             ("out4", TOK, "x"), ("mixo1", TOK, "x"), ("out5", TOK, "y")]
    norm_no = {name: n for n, (name, _, _) in enumerate(norms)}
    version, versions = {"start": 0}, 1
    for name, _, kind in norms:
        if kind == "x":
            version[name] = versions
            versions += 1
    tok0 = lambda T: TOK - T
    x_of = {}
    now = "start"
    for st in stages:
        x_of[st.name] = version[now]
        if st.name in norm_no:
            now = st.name if st.name in version else "emb"
    tokens = {st.name: SEQ if st.n0 < by_name["mix0"].n0 else TOK for st in stages}
    acc = lambda bank, T: ps[:, bank, 0:T]
    h_base = [0, KF + KR, 2 * KF + KR, 3 * KF + KR, 4 * KF + KR, 5 * KF + KR]

    @block.sync
    def _(sp):
        sp.dma_start(r[:, :, META:TOK], x_in).then_inc(inputs_in, 16)
        sp.dma_start(par[:, :], par_in).then_inc(inputs_in, 16)
        sp.dma_start(con[:, :], con_in).then_inc(inputs_in, 16)

        def load(st, i, j, first=False):
            n, slot, _ = at(st, i, j)
            if not first:
                sp.wait_ge(w_lo_done, n - SLOTS + 1)
            sp.dma_start(raw[slot][:, 0:st.cols], weights[st.name][SLOTS * i + j]).then_inc(raw_landed[slot], 16)

        for st in stages:
            start = 0
            if st.n0 == 0:
                for j in range(SLOTS):
                    load(st, 0, j, first=True)
                sp.dma_start(r[:, :, 0:META], meta_in).then_inc(inputs_in, 16)
                start = 1
            if st.name == "in1":
                sp.wait_ge(h_ready, KF + KR)
                sp.dma_start(dist[:, :], bias_in).then_inc(bias_landed, 16)
            if st.name == "out3":
                sp.wait_ge(at_ready, PAIRS)
                sp.dma_start(con2[:, :], con2_in).then_inc(con2_landed, 16)
                sp.dma_start(poolw[:, :, :, ], poolw_in).then_inc(con2_landed, 16)
            full = st.chunks // SLOTS
            if full - start > 1:
                with sp.Fori(start, full) as i:
                    for j in range(SLOTS):
                        load(st, i, j)
            else:
                full = start
            for s in range(SLOTS * full, st.chunks):
                load(st, s // SLOTS, s % SLOTS)
        for k in range(KD):
            sp.wait_ge(y_done, KD + k + 1)
            sp.dma_start(out[:, k, :], r[:, k, META:TOK]).then_inc(out_landed, 16)
        sp.wait_ge(out_landed, 16 * KD)

    @block.tensor
    def _(pe):
        def products(slot, tile, hi, lo, bank, T, start, stop):
            w = slice(tile * P, (tile + 1) * P)
            nc.tensor.matmul(acc(bank, T), whi[slot][:, w], hi, start=start, stop=False)
            nc.tensor.matmul(acc(bank, T), whi[slot][:, w], lo, start=False, stop=False)
            return nc.tensor.matmul(acc(bank, T), wlo[slot][:, w], hi, start=False, stop=stop)

        def x_tile(k, T):
            return x_hi[:, k, tok0(T):TOK], x_lo[:, k, tok0(T):TOK]

        def from_x(st, i, j, bank, behind):
            T = tokens[st.name]
            n, slot, _ = at(st, i, j)
            pe.wait_ge(acc_free, behind)
            pe.wait_ge(w_lo_done, n + 1)
            for k in range(KD):
                if j == 0:
                    pe.wait_ge(x_ready, KD * x_of[st.name] + k + 1)
                last = products(slot, k, *x_tile(k, T), bank, T, k == 0, k == KD - 1)
            last.then_inc(chunk_used, 1)

        def from_h(st, i, j, tiles, tile0=0, ready=None):
            T = tokens[st.name]
            n, slot, _ = at(st, i, j)
            pe.wait_ge(acc_free, SLOTS * i + (st.u0 + j - 3))
            pe.wait_ge(w_lo_done, n + 1)
            for k in range(tiles):
                if ready and j == 0 and isinstance(i, int) and i == 0:
                    ready(k)
                last = products(slot, k, h_hi[:, k, 0:T], h_lo[:, k, 0:T], j, T, k == 0, k == tiles - 1)
            last.then_inc(chunk_used, 1)

        def ffn(f):
            st = by_name[f"in{f}"]
            pe.wait_ge(acc_free, st.u0)
            steps(pe, st.chunks, lambda i, j: from_x(st, i, j, j, 2 * i + (st.u0 + j // 2 - 1)))
            so = by_name[f"out{f}"]
            T = tokens[so.name]
            pe.wait_ge(acc_free, so.u0)

            def half(i, j):
                n, slot, _ = at(so, i, j)
                if j % 2 == 0:
                    pe.wait_ge(acc_free, 2 * i + (so.u0 + j // 2 - 1))
                pe.wait_ge(w_lo_done, n + 1)
                for t in range(HALF_F):
                    k = (j % 2) * HALF_F + t
                    if t == 0 or k >= KF - 2:
                        pe.wait_ge(h_ready, h_base[f] + (HALF_F if k == 0 else KF - 2 if t == 0 else k + 1))
                    last = products(slot, t, h_hi[:, k, 0:T], h_lo[:, k, 0:T], j // 2, T, k == 0, k == KF - 1)
                last.then_inc(chunk_used, 1)

            steps(pe, so.chunks, half)

        def layer_norm(name):
            n = norm_no[name]
            T = norms[n][1]
            if name == "emb":
                pe.wait_ge(y_done, KD)
                pe.wait_ge(inputs_in, 64)
            else:
                pe.wait_ge(acc_free, by_name[name].u0 + by_name[name].units)
            for k in range(KD):
                last = nc.tensor.matmul(acc(4, T), ones_d, r[:, k, tok0(T):TOK], start=k == 0, stop=k == KD - 1)
            last.then_inc(mean_done, 1)
            for k in range(KD):
                if k % 4 == 0:
                    pe.wait_ge(sq_done, 2 * n + k // 4 + 1)
                last = nc.tensor.matmul(acc(5, T), ones_d, sq[:, k, tok0(T):TOK], start=k == 0, stop=k == KD - 1)
            last.then_inc(var_done, 1)

        def recurrent():
            st = by_name["rg_u"]
            pe.wait_ge(acc_free, st.u0)
            steps(pe, st.chunks, lambda i, j: from_x(st, i, j, j, SLOTS * i + (st.u0 + j - 3)))
            sg = by_name["rg_gate"]
            for b in range(GATE_BLOCKS):
                n, slot, _ = at(sg, b // SLOTS, b % SLOTS)
                pe.wait_ge(w_lo_done, n + 1)
                pe.wait_ge(acc_free, sg.u0 + b)
                pe.wait_ge(u_ready, 2 * b + 2)
                for m in range(4):
                    for k in range(2):
                        c = KR + 2 * b + k
                        last = products(slot, 2 * m + k, h_hi[:, c, 0:SEQ], h_lo[:, c, 0:SEQ], m, SEQ, k == 0, k == 1)
                last.then_inc(chunk_used, 1)
            sy = by_name["rg_y"]
            pe.wait_ge(acc_free, sy.u0)
            steps(pe, sy.chunks, lambda i, j: from_x(sy, i, j, j, SLOTS * i + (sy.u0 + j - 3)))
            so = by_name["rg_out"]
            pe.wait_ge(acc_free, so.u0)
            steps(pe, so.chunks, lambda i, j: from_h(so, i, j, KR, ready=lambda k: pe.wait_ge(h_ready, KF + k + 1)))

        def keys_values():
            st = by_name["kv"]
            pe.wait_ge(acc_free, st.u0)
            steps(pe, st.chunks, lambda i, j: from_x(st, i, j, j, SLOTS * i + (st.u0 + j - 3)))
            pe.wait_ge(acc_free, st.u0 + st.units)
            for t in range(2):
                for m in range(KD):
                    last = nc.tensor.transpose(ps[:, 4 + 2 * t + m // 4, (m % 4) * P:(m % 4 + 1) * P],
                                               sq[:, m, t * P:(t + 1) * P], ident)
            last.then_inc(vT_done, 1)

        def attention():
            st = by_name["q"]
            pe.wait_ge(acc_free, st.u0)
            pe.wait_ge(v_copied, 4)

            def query(s):
                from_x(st, s // SLOTS, s % SLOTS, s % 2, st.u0 + s - 1)

            def scores(a):
                hp, rows = a // 2, slice(HD * (a % 2), HD * (a % 2 + 1))
                pe.wait_ge(acc_free, st.u0 + GROUPS * (hp + 1))
                if a:
                    pe.wait_ge(biased, a)
                for g in range(GROUPS):
                    nc.tensor.matmul(ps[:, 2, g * P:(g + 1) * P], qT[rows, hp % 2, g, 0:P], kT[rows, hp, 0:P],
                                     start=True, stop=True)
                for g in range(GROUPS):
                    last = nc.tensor.matmul(ps[:, 3 + g // 2, (g % 2) * SEQ:(g % 2 + 1) * SEQ],
                                            qT[rows, hp % 2, g, P:SEQ], kT[rows, hp, :], start=True, stop=True)
                last.then_inc(scored, 1)

            def transposed(a):
                pe.wait_ge(dg_done, a + 1)
                if a:
                    pe.wait_ge(pT_copied, a)
                for n, (q, k) in enumerate(((0, 0), (1, 0), (1, 1))):
                    for g in range(GROUPS):
                        c = g * P if q == 0 else GROUPS * P + g * SEQ + k * P
                        last = nc.tensor.matmul(ps[:, 5, n * P:(n + 1) * P], s_at[:, a % 2, c:c + P],
                                                dg[:, a % 2, q, :], start=g == 0, stop=g == GROUPS - 1)
                last.then_inc(pT_done, 1)

            def values(a):
                hp, e = a // 2, a % 2
                o = ps[HD * e:HD * (e + 1), 6 + hp % 2, :]
                pe.wait_ge(pT_copied, a + 1)
                if hp >= 2:
                    pe.wait_ge(at_ready, hp - 1)
                col = slice(HD * a, HD * (a + 1))
                nc.tensor.matmul(o[:, 0:SEQ], v_tok[:, 0, col], pT[:, a % 2, 0:SEQ], start=True, stop=False)
                nc.tensor.matmul(o[:, P:SEQ], v_tok[:, 1, col], pT[:, a % 2, SEQ:SEQ + P],
                                 start=False, stop=True).then_inc(pv_done, 1)

            for hp in range(PAIRS + 2):
                a, b, behind = 2 * hp - 2, 2 * hp - 1, 2 * hp - 3
                if 1 <= hp <= PAIRS:
                    scores(a)
                if hp < PAIRS:
                    query(3 * hp)
                if hp >= 2:
                    values(behind)
                if hp < PAIRS:
                    query(3 * hp + 1)
                if 1 <= hp <= PAIRS:
                    transposed(a)
                    scores(b)
                if hp < PAIRS:
                    query(3 * hp + 2)
                if 1 <= hp <= PAIRS:
                    values(a)
                    transposed(b)
            so = by_name["o"]
            steps(pe, so.chunks, lambda i, j: from_h(so, i, j, KD, ready=lambda k: pe.wait_ge(at_ready, k + 1)))

        def hybrid(l):
            st = by_name[f"mix{l}"]
            pe.wait_ge(acc_free, st.u0)
            pe.wait_ge(con2_landed, 32)
            f0 = FOX_HEADS * l

            def tile(s):
                from_x(st, s // SLOTS, s % SLOTS, s % 2, st.u0 + s - 1)

            def token_tiles(t):
                return slice(t * P, min((t + 1) * P, TOK))

            def fox_scores(h):
                rows = slice(HD * (h % 2), HD * (h % 2 + 1))
                if h == 0:
                    pe.wait_ge(c_done, l + 1)
                    pe.wait_ge(acc_free, st.u0 + FOX0 + 6)
                if f0 + h:
                    pe.wait_ge(biased, HEADS + f0 + h)
                for q, (bank, c, n) in enumerate(((2, 0, P), (2, P, 2 * P), (3, 0, TOK))):
                    o = ps[0:P if q < 2 else META, bank, c:c + n]
                    nc.tensor.matmul(o, qf[rows, h // 2, token_tiles(q)], kf[rows, h // 2, 0:n], start=True, stop=False)
                    sel = con2[LOGIT_ROW:LOGIT_ROW + FOX_HEADS, B_SEL + h * P:B_SEL + h * P + (P if q < 2 else META)]
                    last = nc.tensor.matmul(o, sel, rstd[LOGIT_ROW:LOGIT_ROW + FOX_HEADS, 0:n], start=False, stop=True)
                last.then_inc(scored, 1)

            def fox_transposed(h):
                pe.wait_ge(dg_done, HEADS + f0 + h + 1)
                pe.wait_ge(pT_copied, HEADS + f0 + h)
                b = h % 2
                for k in range(3):
                    for q in range(k, 3):
                        m = P if q < 2 else META
                        kn = P if k < 2 else META
                        c = (0, P, 3 * P)[q] + k * P
                        o = ps[0:kn, 4, KEY_AT[k] + (q - k) * P:KEY_AT[k] + (q - k) * P + m]
                        last = nc.tensor.matmul(o, s_fox[0:m, b, c:c + kn], dg_fox[0:m, b, q, 0:m], start=True, stop=True)
                last.then_inc(pT_done, 1)

            def by_values(o, v, col, weights_t):
                for k in range(3):
                    kn = P if k < 2 else META
                    last = nc.tensor.matmul(o[:, k * P:TOK], v[0:kn, k, col],
                                            weights_t[0:kn, KEY_AT[k]:KEY_AT[k] + KEY_COLS[k]], start=k == 0, stop=k == 2)
                return last

            def fox_values(h):
                o = ps[HD * (h % 2):HD * (h % 2 + 1), 5, :]
                pe.wait_ge(pT_copied, HEADS + f0 + h + 1)
                if h == 0:
                    pe.wait_ge(vt2_copied, 4 * l + 2)
                pe.wait_ge(at_ready, PAIRS + 3 * l + h // 2)
                by_values(o, vf_tok, slice(HD * h, HD * (h + 1)), pT_fox[:, h % 2, :]).then_inc(pv_done, 1)

            def transposes(src, tiles, dst_bank):
                for t in range(3):
                    for m in range(tiles):
                        last = nc.tensor.transpose(ps[0:P if t < 2 else META, dst_bank[t][0], dst_bank[t][1] + m * P:dst_bank[t][1] + (m + 1) * P],
                                                   src[:, m, token_tiles(t)], ident)
                return last

            for s in range(FOX0 + 9):
                tile(s)
            pe.wait_ge(acc_free, st.u0 + ROT0)
            transposes(vf, 3, ((5, 0), (6, 0), (7, 0))).then_inc(vt2_done, 1)
            for h in range(FOX_HEADS):
                fox_scores(h)
                tile(ROT0 + 2 * h)
                if h:
                    fox_values(h - 1)
                tile(ROT0 + 2 * h + 1)
                fox_transposed(h)
            tile(WIN_TILES - 1)
            fox_values(FOX_HEADS - 1)
            pe.wait_ge(vt2_copied, 4 * l + 2)
            pe.wait_ge(biased, HEADS + f0 + FOX_HEADS)
            transposes(vr, RET_HEADS, ((6, 0), (7, 0), (2, 0))).then_inc(vt2_done, 1)
            pe.wait_ge(rot_done, 4 * (l + 1))
            pe.wait_ge(acc_free, st.u0 + st.units)
            pe.wait_ge(at_ready, PAIRS + 3 * l + 3)
            out_bank = (0, 1, 6, 7)

            def ret_scores(h):
                n = RET_HEADS * l + h
                rows = slice(32 * h, 32 * h + 32)
                if h >= 2:
                    pe.wait_ge(ret_d, n - 1)
                for k in range(3):
                    kn = P if k < 2 else META
                    o = ps[0:kn, 3 + h % 2, KEY_AT[k]:KEY_AT[k] + KEY_COLS[k]]
                    for half in range(2):
                        last = nc.tensor.matmul(o, rot[rows, 2 + half, token_tiles(k)], rot[rows, half, k * P:TOK],
                                                start=half == 0, stop=half == 1)
                last.then_inc(ret_s, 1)

            def ret_values(h):
                n = RET_HEADS * l + h
                pe.wait_ge(ret_d, n + 1)
                if h == 0:
                    pe.wait_ge(vt2_copied, 4 * l + 4)
                by_values(acc(out_bank[h], 512), vr_tok, slice(P * h, P * (h + 1)), s_fox[:, h % 2, 0:KEYS_ALL]).then_inc(ret_o, 1)

            ret_scores(0)
            ret_scores(1)
            for h in range(RET_HEADS):
                ret_values(h)
                if h + 2 < RET_HEADS:
                    ret_scores(h + 2)
            pe.wait_ge(pool_done, l + 1)
            pe.wait_ge(vt2_copied, 4 * l + 4)
            for m in range(2):
                last = nc.tensor.matmul(acc((2, 5)[m], TOK), poolw[:, l, m, :], w_b[:, m, POOL_PAD:], start=True, stop=True)
            last.then_inc(pool_mm, 1)
            for h in range(RET_HEADS):
                n = RET_HEADS * l + h
                pe.wait_ge(ret_osb, n + 1)
                nc.tensor.matmul(acc(out_bank[h], TOK), ones_head, osb[:, h, :], start=True, stop=True).then_inc(ret_mean, 1)
            for h in range(RET_HEADS):
                n = RET_HEADS * l + h
                pe.wait_ge(ret_sq, n + 1)
                last = nc.tensor.matmul(ps[0:RET_HEADS, 3, 0:TOK], con2[:, B_HEAD + RET_HEADS * h:B_HEAD + RET_HEADS * (h + 1)],
                                        sqh[:, h % 2, :], start=h == 0, stop=h == RET_HEADS - 1)
                last.then_inc(ret_var, 1)
            pe.wait_ge(ret_rstd, l + 1)
            for h in range(RET_HEADS):
                nc.tensor.matmul(acc(out_bank[h], TOK), con2[0:RET_HEADS, B_EXP + h * P:B_EXP + (h + 1) * P],
                                 std4[0:RET_HEADS, :], start=True, stop=True).then_inc(ret_bc, 1)
            so = by_name[f"mixo{l}"]

            def mixed(k):
                if k < RET_HEADS:
                    pe.wait_ge(ret_ready, RET_HEADS * l + k + 1)
                elif k == RET_HEADS:
                    pe.wait_ge(pool_ready, 2 * l + 2)

            steps(pe, so.chunks, lambda i, j: from_h(so, i, j, MIX_K, ready=mixed))

        pe.wait_ge(inputs_in, 64)
        ffn(0)
        layer_norm("out0")
        recurrent()
        layer_norm("rg_out")
        ffn(1)
        layer_norm("out1")
        keys_values()
        ffn(2)
        layer_norm("out2")
        attention()
        layer_norm("o")
        ffn(3)
        layer_norm("out3")
        layer_norm("emb")
        for l in range(LAYERS_2):
            hybrid(l)
            layer_norm(f"mixo{l}")
            ffn(4 + l)
            layer_norm(f"out{4 + l}")


    @block.scalar
    def _(act):
        own = [0]

        def link(ins):
            own[0] += 1
            ins.then_inc(act_step, 1)
            act.wait_ge(act_step, own[0])

        def round_chunk(n, slot, rnd, cols):
            act.wait_ge(raw_landed[slot], 16 * rnd + 16)
            if not isinstance(n, int) or n >= SLOTS:
                act.wait_ge(chunk_used, n - SLOTS + 1)
            nc.scalar.activation(whi[slot][:, 0:cols], raw[slot][:, 0:cols], ACT.Copy).then_inc(w_hi_done, 1)

        def round_ahead(st, i, j):
            a = ahead(st, i, j)
            if a:
                round_chunk(*a)

        def start():
            act.wait_ge(inputs_in, 64)
            for n in range(AHEAD):
                round_chunk(n, n, 0, stages[0].cols)
            for k in range(KD):
                nc.scalar.activation(x_hi[:, k, META:TOK], r[:, k, META:TOK], ACT.Copy).then_inc(x_hi_done, 1)
            for k in range(KD):
                nc.scalar.activation(ax[:, k, META:TOK], r[:, k, META:TOK], ACT.Copy, scale=ALPHA).then_inc(ax_done, 1)
            nc.scalar.activation(ab[:, :], par[:, C_B:C_B + N_LN * KD], ACT.Copy, scale=ALPHA).then_inc(par_done, 1)
            link(nc.scalar.activation(lser[:, 0, :], par[:, C_LAM:C_LAM + KR], ACT.Abs))
            nc.scalar.activation(lser[:, 1, :], lser[:, 0, :], ACT.Exp, scale=-1.0).then_inc(ser_e, 1)

        def ffn(f):
            st = by_name[f"in{f}"]
            T = tokens[st.name]

            def step(i, j):
                round_ahead(st, i, j)
                if j % 2 == 0:
                    p = 2 * i + j // 2
                    act.wait_ge(chunk_used, SLOTS * i + (st.n0 + j + 1))
                    act.wait_ge(acc_free, 2 * i + (st.u0 + j // 2 - 1))
                    nc.scalar.activation(sgate[:, j // 2, 0:T], acc(j, T), ACT.Silu).then_inc(gate_done, 1)

            steps(act, st.chunks, step, start=int(st.n0 == 0))
            so = by_name[f"out{f}"]
            steps(act, so.chunks, lambda i, j: round_ahead(so, i, j))

        def layer_norm(name):
            n = norm_no[name]
            _, T, kind = norms[n]
            t = slice(tok0(T), TOK)
            for half in range(2):
                act.wait_ge(xc_done, 2 * n + half + 1)
                ks = slice(4 * half, 4 * half + 4)
                nc.scalar.activation(sq[:, ks, t], r[:, ks, t], ACT.Square).then_inc(sq_done, 1)
            act.wait_ge(var_done, n + 1)
            nc.scalar.activation(std[:, 0:T], acc(5, T), ACT.Sqrt, bias=eps[:, 0:1]).then_inc(std_done, 1)
            b = lambda k: par[:, C_B + KD * n + k:C_B + KD * n + k + 1]
            for k in range(KD):
                act.wait_ge(xn_done, KD * n + k + 1)
                if kind == "x":
                    nc.scalar.activation(x_hi[:, k, t], r[:, k, t], ACT.Identity, bias=b(k)).then_inc(x_hi_done, 1)
                else:
                    nc.scalar.activation(r[:, k, t], r[:, k, t], ACT.Identity, bias=b(k)).then_inc(y_done, 1)
            if kind == "x":
                for k in range(KD):
                    nc.scalar.activation(ax[:, k, t], r[:, k, t], ACT.Identity, scale=ALPHA,
                                         bias=ab[:, KD * n + k:KD * n + k + 1]).then_inc(ax_done, 1)

        def recurrent():
            st = by_name["rg_u"]
            col = lambda c, k: par[:, c + k:c + k + 1]
            for s in range(KR):
                round_ahead(st, s // SLOTS, s % SLOTS)
                act.wait_ge(chunk_used, st.n0 + s + 1)
                if s == 0:
                    act.wait_ge(pad_zero, 1)
                if s >= 2:
                    act.wait_ge(conv_done, s - 1)
                bank = acc(s % SLOTS, SEQ)
                nc.scalar.activation(upad[:, s % 2, CONV - 1:], bank, ACT.Copy).then_inc(u_raw, 1)
                nc.scalar.activation(uc[:, s, :], bank, ACT.Identity, scale=col(C_CW, (CONV - 1) * KR + s),
                                     bias=col(C_CB, s)).then_inc(acc_free, 1)
            sg = by_name["rg_gate"]
            act.wait_ge(spc_done, 1)
            for b in range(GATE_BLOCKS):
                round_ahead(sg, b // SLOTS, b % SLOTS)
                act.wait_ge(chunk_used, sg.n0 + b + 1)
                for d in range(2):
                    c = 2 * b + d
                    nc.scalar.activation(dec[:, c, :], acc(d, SEQ), ACT.Sigmoid, bias=col(C_GB, c)).then_inc(act_step, 1)
                    own[0] += 1
                for d in range(2):
                    c = 2 * b + d
                    last = nc.scalar.activation(ybr[:, c, :], acc(2 + d, SEQ), ACT.Sigmoid, bias=col(C_GB, KR + c))
                    last.then_inc(acc_free if d else in_gate, 1)
                act.wait_ge(act_step, own[0])
                for d in range(2):
                    c = 2 * b + d
                    nc.scalar.activation(tnh[:, c, :], dec[:, c, :], ACT.Tanh, scale=spc[:, c:c + 1]).then_inc(tanh_done, 1)
            sy = by_name["rg_y"]
            for s in range(KR):
                round_ahead(sy, s // SLOTS, s % SLOTS)
                act.wait_ge(tanh_done, s + 1)
                nc.scalar.activation(dec[:, s, :], dec[:, s, :], ACT.Exp, scale=nspc[:, s:s + 1]).then_inc(dec_done, 1)
                act.wait_ge(chunk_used, sy.n0 + s + 1)
                if s % 2 == 0:
                    act.wait_ge(iu_done, s // 2 + 1)
                nc.scalar.activation(ybr[:, s, :], acc(s % SLOTS, SEQ), ACT.Copy).then_inc(acc_free, 1)
            for half in range(2):
                c = slice(5 * half, 5 * half + 5)
                act.wait_ge(v_arg, 5 * half + 5)
                nc.scalar.activation(tnh[:, c, :], tnh[:, c, :], ACT.Sqrt).then_inc(v_root, 1)
            act.wait_ge(acc_free, sy.u0 + KR)
            for half in range(2):
                c = slice(5 * half, 5 * half + 5)
                nc.scalar.activation(ybr[:, c, :], ybr[:, c, :], ACT.Gelu_apprx_tanh).then_inc(gelu_done, 1)
            so = by_name["rg_out"]
            steps(act, so.chunks, lambda i, j: round_ahead(so, i, j))

        def keys_values():
            st = by_name["kv"]
            for s in range(2 * KD):
                round_ahead(st, s // SLOTS, s % SLOTS)
                act.wait_ge(chunk_used, st.n0 + s + 1)
                dst = kT[:, s, :] if s < KD else sq[:, s - KD, 0:SEQ]
                nc.scalar.activation(dst, acc(s % SLOTS, SEQ), ACT.Copy).then_inc(acc_free, 1)
            act.wait_ge(vT_done, 1)
            for t in range(2):
                for half in range(2):
                    nc.scalar.activation(v_tok[:, t, 512 * half:512 * half + 512], ps[:, 4 + 2 * t + half, :],
                                         ACT.Copy).then_inc(v_copied, 1)

        def attention():
            st = by_name["q"]

            def query(s):
                round_ahead(st, s // SLOTS, s % SLOTS)
                act.wait_ge(chunk_used, st.n0 + s + 1)
                hp = s // GROUPS
                if hp >= 2:
                    act.wait_ge(scored, 2 * hp - 2)
                nc.scalar.activation(qT[:, hp % 2, s % GROUPS, :], acc(s % 2, SEQ), ACT.Copy,
                                     scale=float(HD) ** -0.5).then_inc(acc_free, 1)

            def exps(a):
                act.wait_ge(nmax_done, a + 1)
                b = a % 2
                nc.scalar.activation(s_at[:, b, 0:GROUPS * P], s_at[:, b, 0:GROUPS * P], ACT.Exp,
                                     bias=nmax[:, b, 0:1], accum_out=den[:, b, 0:1])
                nc.scalar.activation(s_at[:, b, GROUPS * P:], s_at[:, b, GROUPS * P:], ACT.Exp,
                                     bias=nmax[:, b, 1:2], accum_out=den[:, b, 1:2]).then_inc(probs, 1)

            def copy_transposed(a):
                act.wait_ge(pT_done, a + 1)
                if a >= 2:
                    act.wait_ge(pv_done, a - 1)
                nc.scalar.activation(pT[:, a % 2, :], ps[:, 5, 0:GROUPS * P], ACT.Copy).then_inc(pT_copied, 1)

            def round_output(hp):
                act.wait_ge(pv_done, 2 * hp + 2)
                nc.scalar.activation(h_hi[:, hp, 0:SEQ], acc(6 + hp % 2, SEQ), ACT.Copy).then_inc(at_hi, 1)

            for hp in range(PAIRS + 2):
                a, b, behind = 2 * hp - 2, 2 * hp - 1, 2 * hp - 3
                if hp >= 2:
                    copy_transposed(behind)
                if hp < PAIRS:
                    query(3 * hp)
                if 1 <= hp <= PAIRS:
                    exps(a)
                if hp < PAIRS:
                    query(3 * hp + 1)
                if hp >= 2:
                    round_output(hp - 2)
                if 1 <= hp <= PAIRS:
                    copy_transposed(a)
                if hp < PAIRS:
                    query(3 * hp + 2)
                if 1 <= hp <= PAIRS:
                    exps(b)
            so = by_name["o"]
            steps(act, so.chunks, lambda i, j: round_ahead(so, i, j))

        def hybrid(l):
            st = by_name[f"mix{l}"]
            f0 = FOX_HEADS * l
            lr = slice(LOGIT_ROW, LOGIT_ROW + FOX_HEADS)

            def tile(s):
                round_ahead(st, s // SLOTS, s % SLOTS)
                act.wait_ge(chunk_used, st.n0 + s + 1)
                src = acc(s % 2, TOK)
                if s == 0:
                    bf = par[lr, C_BF + l:C_BF + l + 1]
                    nc.scalar.activation(sgate[lr, 0, :], ps[lr, 0, 0:TOK], ACT.Identity, bias=bf).then_inc(fx_done, 1)
                    link(nc.scalar.activation(sgate[lr, 1, :], ps[lr, 0, 0:TOK], ACT.Abs, bias=bf))
                    nc.scalar.activation(sgate[lr, 1, :], sgate[lr, 1, :], ACT.Exp, scale=-1.0).then_inc(fe_done, 1)
                    dst, scale = gsb[:, 0, :], 1.0
                elif s < FOX0 + 3:
                    dst, scale = qf[:, s - FOX0, :], float(HD) ** -0.5
                elif s < FOX0 + 6:
                    dst, scale = kf[:, s - FOX0 - 3, :], 1.0
                elif s < ROT0:
                    dst, scale = vf[:, s - FOX0 - 6, :], 1.0
                elif s < VR0:
                    dst, scale = rot_in[:, s - ROT0, :], 1.0
                elif s < GATE0:
                    dst, scale = vr[:, s - VR0, :], 1.0
                elif s < POOL0:
                    dst, scale = gsb[:, 1 + s - GATE0, :], 1.0
                else:
                    if s == POOL0:
                        act.wait_ge(up_zero, l + 1)
                    dst, scale = up[:, s - POOL0, POOL_PAD:], 1.0
                nc.scalar.activation(dst, src, ACT.Copy, scale=scale).then_inc(acc_free, 1)

            def exps(h):
                act.wait_ge(nmax_done, HEADS + f0 + h + 1)
                b = h % 2
                for q, (c, n) in enumerate(((0, P), (P, 2 * P), (3 * P, TOK))):
                    m = P if q < 2 else META
                    last = nc.scalar.activation(s_fox[0:m, b, c:c + n], s_fox[0:m, b, c:c + n], ACT.Exp,
                                                bias=nmax_f[0:m, b, q:q + 1], accum_out=den_f[0:m, b, q:q + 1])
                last.then_inc(probs, 1)

            def copy_transposed(h):
                act.wait_ge(pT_done, HEADS + f0 + h + 1)
                if h >= 2:
                    act.wait_ge(pv_done, HEADS + f0 + h - 1)
                nc.scalar.activation(pT_fox[:, h % 2, 0:KEY_AT[2]], ps[:, 4, 0:KEY_AT[2]], ACT.Copy).then_inc(act_step, 1)
                own[0] += 1
                nc.scalar.activation(pT_fox[0:META, h % 2, KEY_AT[2]:], ps[0:META, 4, KEY_AT[2]:KEYS_ALL], ACT.Copy).then_inc(pT_copied, 1)

            def round_output(hp):
                act.wait_ge(pv_done, HEADS + f0 + 2 * hp + 2)
                nc.scalar.activation(h_hi[:, RET_HEADS + 2 + hp, :], acc(5, TOK), ACT.Copy).then_inc(at_hi, 1)

            def copy_values(n, dst, banks, cols):
                act.wait_ge(vt2_done, 2 * l + n + 1)
                for t in range(2):
                    ins = nc.scalar.activation(dst[:, t, 0:cols], ps[:, banks[t], 0:cols], ACT.Copy)
                    if t:
                        ins.then_inc(vt2_copied, 1)
                nc.scalar.activation(dst[0:META, 2, 0:cols], ps[0:META, banks[2], 0:cols], ACT.Copy).then_inc(vt2_copied, 1)

            for s in range(ROT0):
                tile(s)
            copy_values(0, vf_tok, (5, 6, 7), FOX_W)
            for h in range(FOX_HEADS):
                tile(ROT0 + 2 * h)
                exps(h)
                if h >= 2 and h % 2 == 0:
                    round_output(h // 2 - 1)
                tile(ROT0 + 2 * h + 1)
                copy_transposed(h)
            tile(WIN_TILES - 1)
            round_output(2)
            copy_values(1, vr_tok, (6, 7, 2), RET_HEADS * P)
            act.wait_ge(acc_free, st.u0 + st.units)
            nc.scalar.activation(gsb[:, :, :], gsb[:, :, :], ACT.Silu).then_inc(silu2, 1)
            out_bank = (0, 1, 6, 7)
            for h in range(RET_HEADS):
                act.wait_ge(ret_o, RET_HEADS * l + h + 1)
                nc.scalar.activation(osb[:, h, :], acc(out_bank[h], TOK), ACT.Copy).then_inc(ret_osb, 1)
            act.wait_ge(pool_mm, l + 1)
            for m in range(2):
                nc.scalar.activation(h_hi[:, RET_HEADS + m, :], acc((2, 5)[m], TOK), ACT.Copy,
                                     scale=par[:, C_PS + 2 * l + m:C_PS + 2 * l + m + 1]).then_inc(pool_hi, 1)
            for h in range(RET_HEADS):
                n = RET_HEADS * l + h
                act.wait_ge(ret_xc, n + 1)
                if h >= 2:
                    act.wait_ge(ret_var, n - 1)
                nc.scalar.activation(sqh[:, h % 2, :], osb[:, h, :], ACT.Square).then_inc(ret_sq, 1)
            act.wait_ge(ret_var, RET_HEADS * (l + 1))
            nc.scalar.activation(std4[0:RET_HEADS, :], ps[0:RET_HEADS, 3, 0:TOK], ACT.Sqrt,
                                 bias=eps[0:RET_HEADS, 0:1]).then_inc(ret_std, 1)
            so = by_name[f"mixo{l}"]
            steps(act, so.chunks, lambda i, j: round_ahead(so, i, j))

        start()
        act.wait_ge(par_done, 2)
        ffn(0)
        layer_norm("out0")
        recurrent()
        layer_norm("rg_out")
        ffn(1)
        layer_norm("out1")
        keys_values()
        ffn(2)
        layer_norm("out2")
        attention()
        layer_norm("o")
        ffn(3)
        layer_norm("out3")
        layer_norm("emb")
        for l in range(LAYERS_2):
            hybrid(l)
            layer_norm(f"mixo{l}")
            ffn(4 + l)
            layer_norm(f"out{4 + l}")

    @block.vector
    def _(dve):
        own = [0]

        def link(ins):
            own[0] += 1
            ins.then_inc(dve_step, 1)
            dve.wait_ge(dve_step, own[0])

        V = nc.vector
        f = lambda ap: ap.bitcast(fp32)

        def rest_of_chunk(n, slot, rnd, cols):
            dve.wait_ge(w_hi_done, n + 1)
            V.tensor_tensor(wlo[slot][:, 0:cols], raw[slot][:, 0:cols], f(whi[slot][:, 0:cols]),
                            ALU.subtract).then_inc(w_lo_done, 1)

        def rest_ahead(st, i, j):
            a = ahead(st, i, j)
            if a:
                rest_of_chunk(*a)

        def log1p(e, s, s2, p):
            link(V.tensor_scalar(s, e, 2.0, None, ALU.add))
            link(V.reciprocal(s, s))
            link(V.tensor_tensor(s, s, e, ALU.mult))
            link(V.tensor_tensor(s2, s, s, ALU.mult))
            link(V.tensor_scalar(p, s2, 1.0 / 17, None, ALU.mult))
            for odd in (15, 13, 11, 9, 7, 5, 3):
                link(V.scalar_tensor_tensor(p, p, 1.0 / odd, s2, ALU.add, ALU.mult))

        def start():
            link(V.memset(eps[:, :], LN_EPS))
            dve.sem_inc(acc_free, SLOTS)
            for n in range(AHEAD):
                rest_of_chunk(n, n, 0, stages[0].cols)
            for k in range(KD):
                dve.wait_ge(x_hi_done, k + 1)
                V.tensor_tensor(x_lo[:, k, META:TOK], r[:, k, META:TOK], f(x_hi[:, k, META:TOK]),
                                ALU.subtract).then_inc(x_ready, 1)
            dve.wait_ge(ser_e, 1)
            s, s2, p = lser[:, 2, :], lser[:, 3, :], lser[:, 4, :]
            log1p(lser[:, 1, :], s, s2, p)
            link(V.scalar_tensor_tensor(s, p, 1.0, s, ALU.add, ALU.mult))
            link(V.tensor_scalar(s2, par[:, C_LAM:C_LAM + KR], -1.0, 0.0, ALU.mult, ALU.max))
            link(V.scalar_tensor_tensor(s, s, 2.0, s2, ALU.mult, ALU.add))
            link(V.tensor_scalar(nspc[:, :], s, -8.0, None, ALU.mult))
            V.tensor_scalar(spc[:, :], s, 8.0, None, ALU.mult).then_inc(spc_done, 1)
            dve.sem_inc(par_done, 1)

        def ffn(fn):
            st = by_name[f"in{fn}"]
            T = tokens[st.name]
            h0 = h_base[fn]

            def step(i, j):
                rest_ahead(st, i, j)
                if j % 2:
                    b = j // 2
                    p = 2 * i + b
                    dve.wait_ge(chunk_used, SLOTS * i + (st.n0 + j + 1))
                    dve.wait_ge(gate_done, 2 * i + (KF * fn + b + 1))
                    V.tensor_tensor(prod[:, b, 0:T], sgate[:, b, 0:T], acc(j, T), ALU.mult).then_inc(acc_free, 1)
                    dve.wait_ge(acc_free, 2 * i + (st.u0 + b + 1))
                    V.tensor_copy(h_hi[:, p, 0:T], prod[:, b, 0:T]).then_inc(h_hi_done, 1)
                    dve.wait_ge(h_hi_done, 2 * i + (h0 + b + 1))
                    V.tensor_tensor(h_lo[:, p, 0:T], prod[:, b, 0:T], f(h_hi[:, p, 0:T]),
                                    ALU.subtract).then_inc(h_ready, 1)

            steps(dve, st.chunks, step)
            so = by_name[f"out{fn}"]
            t = slice(tok0(T), TOK)
            dve.wait_ge(ax_done, KD * (x_of[so.name] + 1))

            def out_step(i, j):
                rest_ahead(so, i, j)
                if j % 2:
                    dve.wait_ge(chunk_used, SLOTS * i + (so.n0 + j + 1))
                    m = 2 * i + j // 2
                    V.scalar_tensor_tensor(r[:, m, t], acc(j // 2, T), 0.5 if fn < 4 else 1.0, ax[:, m, t],
                                           ALU.mult, ALU.add).then_inc(acc_free, 1)

            steps(dve, so.chunks, out_step)

        def add_to_ax(st):
            T = tokens[st.name]
            t = slice(tok0(T), TOK)
            dve.wait_ge(ax_done, KD * (x_of[st.name] + 1))

            def step(i, j):
                rest_ahead(st, i, j)
                dve.wait_ge(chunk_used, SLOTS * i + (st.n0 + j + 1))
                m = SLOTS * i + j
                V.tensor_tensor(r[:, m, t], acc(j, T), ax[:, m, t], ALU.add).then_inc(acc_free, 1)

            steps(dve, st.chunks, step)

        def layer_norm(name):
            n = norm_no[name]
            _, T, kind = norms[n]
            t = slice(tok0(T), TOK)
            dve.wait_ge(mean_done, n + 1)
            for half in range(2):
                ks = slice(4 * half, 4 * half + 4)
                mean = acc(4, T).unsqueeze(1).broadcast_to([P, 4, T])
                V.tensor_tensor(r[:, ks, t], r[:, ks, t], mean, ALU.subtract).then_inc(xc_done, 1)
            dve.wait_ge(std_done, n + 1)
            link(V.reciprocal(rstd[:, 0:T], std[:, 0:T]))
            v = version.get(name, 0)
            for k in range(KD + 1):
                if k < KD:
                    V.scalar_tensor_tensor(r[:, k, t], r[:, k, t], par[:, C_G + KD * n + k:C_G + KD * n + k + 1],
                                           rstd[:, 0:T], ALU.mult, ALU.mult).then_inc(xn_done, 1)
                if k and kind == "x":
                    c = C_B + KD * n + k - 1
                    dve.wait_ge(x_hi_done, KD * v + k)
                    V.scalar_tensor_tensor(x_lo[:, k - 1, t], r[:, k - 1, t], par[:, c:c + 1], f(x_hi[:, k - 1, t]),
                                           ALU.add, ALU.subtract).then_inc(x_ready, 1)

        def recurrent():
            st = by_name["rg_u"]
            V.memset(upad[:, :, 0:CONV - 1], 0.0).then_inc(pad_zero, 1)
            for s in range(KR):
                rest_ahead(st, s // SLOTS, s % SLOTS)
                dve.wait_ge(u_raw, s + 1)
                dve.wait_ge(acc_free, st.u0 + s + 1)
                for j in range(CONV - 1):
                    ins = V.scalar_tensor_tensor(uc[:, s, :], upad[:, s % 2, j:j + SEQ],
                                                 par[:, C_CW + j * KR + s:C_CW + j * KR + s + 1], uc[:, s, :], ALU.mult, ALU.add)
                    if j < CONV - 2:
                        link(ins)
                ins.then_inc(conv_done, 1)
                dve.wait_ge(conv_done, s + 1)
                V.tensor_copy(h_hi[:, KR + s, 0:SEQ], uc[:, s, :]).then_inc(u_hi_done, 1)
                dve.wait_ge(u_hi_done, s + 1)
                V.tensor_tensor(h_lo[:, KR + s, 0:SEQ], uc[:, s, :], f(h_hi[:, KR + s, 0:SEQ]),
                                ALU.subtract).then_inc(u_ready, 1)
            sg = by_name["rg_gate"]
            for b in range(GATE_BLOCKS):
                rest_ahead(sg, b // SLOTS, b % SLOTS)
                dve.wait_ge(acc_free, sg.u0 + b + 1)
                c = slice(2 * b, 2 * b + 2)
                V.tensor_tensor(uc[:, c, :], uc[:, c, :], ybr[:, c, :], ALU.mult).then_inc(iu_done, 1)
            sy = by_name["rg_y"]
            for s in range(KR):
                rest_ahead(sy, s // SLOTS, s % SLOTS)
                dve.wait_ge(dec_done, s + 1)
                link(V.tensor_tensor(a2[:, s % 2, :], dec[:, s, :], dec[:, s, :], ALU.mult))
                V.scalar_tensor_tensor(tnh[:, s, :], a2[:, s % 2, :], 1.0, tnh[:, s, :], ALU.add, ALU.mult).then_inc(v_arg, 1)
            for half in range(2):
                c = slice(5 * half, 5 * half + 5)
                dve.wait_ge(v_root, half + 1)
                link(V.tensor_tensor(uc[:, c, :], uc[:, c, :], tnh[:, c, :], ALU.mult))
                for s in range(5 * half, 5 * half + 5):
                    V.tensor_tensor_scan(tnh[:, s, :], dec[:, s, :], uc[:, s, :], 0.0, ALU.mult, ALU.add).then_inc(dve_step, 1)
                    own[0] += 1
                dve.wait_ge(dve_step, own[0])
                dve.wait_ge(gelu_done, half + 1)
                link(V.tensor_tensor(dec[:, c, :], tnh[:, c, :], ybr[:, c, :], ALU.mult))
                for s in range(5 * half, 5 * half + 5):
                    V.tensor_copy(h_hi[:, s, 0:SEQ], dec[:, s, :]).then_inc(h_hi_done, 1)
                for s in range(5 * half, 5 * half + 5):
                    dve.wait_ge(h_hi_done, KF + s + 1)
                    V.tensor_tensor(h_lo[:, s, 0:SEQ], dec[:, s, :], f(h_hi[:, s, 0:SEQ]), ALU.subtract).then_inc(h_ready, 1)
            add_to_ax(by_name["rg_out"])

        def keys_values():
            st = by_name["kv"]
            steps(dve, st.chunks, lambda i, j: rest_ahead(st, i, j))

        def attention():
            st = by_name["q"]

            def rest(s):
                rest_ahead(st, s // SLOTS, s % SLOTS)

            def bias_max(a):
                slope = float(2.0 ** (-8.0 * (a + 1) / HEADS))
                b = a % 2
                dve.wait_ge(scored, a + 1)
                if a >= 2:
                    dve.wait_ge(pT_done, a - 1)
                for bank, c, n in ((2, 0, GROUPS * P), (3, GROUPS * P, 2 * SEQ), (4, GROUPS * P + 2 * SEQ, SEQ)):
                    ins = V.scalar_tensor_tensor(s_at[:, b, c:c + n], dist[:, c:c + n], slope, ps[:, bank, 0:n],
                                                 ALU.mult, ALU.add)
                ins.then_inc(biased, 1)
                dve.wait_ge(biased, a + 1)
                V.tensor_reduce(nmax[:, b, 0:1], s_at[:, b, 0:GROUPS * P], AX.X, ALU.max, negate=True)
                V.tensor_reduce(nmax[:, b, 1:2], s_at[:, b, GROUPS * P:], AX.X, ALU.max, negate=True).then_inc(nmax_done, 1)

            def diagonals(a):
                b = a % 2
                dve.wait_ge(probs, a + 1)
                link(V.reciprocal(rden[:, b, :], den[:, b, :]))
                for q in range(2):
                    ins = V.tensor_scalar(dg[:, b, q, :], ident, rden[:, b, q:q + 1], None, ALU.mult)
                ins.then_inc(dg_done, 1)

            def rest_of_output(hp):
                dve.wait_ge(at_hi, hp + 1)
                V.tensor_tensor(h_lo[:, hp, 0:SEQ], acc(6 + hp % 2, SEQ), f(h_hi[:, hp, 0:SEQ]), ALU.subtract).then_inc(at_ready, 1)

            dve.wait_ge(bias_landed, 16)
            for hp in range(PAIRS + 2):
                a, b = 2 * hp - 2, 2 * hp - 1
                if 1 <= hp <= PAIRS:
                    bias_max(a)
                if hp < PAIRS:
                    rest(3 * hp)
                if 1 <= hp <= PAIRS:
                    diagonals(a)
                if hp < PAIRS:
                    rest(3 * hp + 1)
                if hp >= 2:
                    rest_of_output(hp - 2)
                if 1 <= hp <= PAIRS:
                    bias_max(b)
                if hp < PAIRS:
                    rest(3 * hp + 2)
                if 1 <= hp <= PAIRS:
                    diagonals(b)
            add_to_ax(by_name["o"])

        def hybrid(l):
            st = by_name[f"mix{l}"]
            f0 = FOX_HEADS * l
            lr = slice(LOGIT_ROW, LOGIT_ROW + FOX_HEADS)
            k2 = lambda c, n: con2[:, c:c + n]

            def rest(s):
                rest_ahead(st, s // SLOTS, s % SLOTS)

            def cumulative_logits():
                e, s, s2, p = sgate[lr, 1, :], prod[lr, 0, :], prod[lr, 1, :], std[lr, :]
                dve.wait_ge(fe_done, l + 1)
                log1p(e, s, s2, p)
                link(V.scalar_tensor_tensor(s, p, 1.0, s, ALU.add, ALU.mult))
                link(V.tensor_scalar(s2, sgate[lr, 0, :], 0.0, None, ALU.min))
                link(V.scalar_tensor_tensor(s, s, -2.0, s2, ALU.mult, ALU.add))
                V.tensor_tensor_scan(rstd[lr, :], con2[lr, B_ONE:B_ONE + TOK], s, 0.0, ALU.mult, ALU.add).then_inc(c_done, 1)

            def mask_max(h):
                b = h % 2
                n = HEADS + f0 + h
                dve.wait_ge(scored, n + 1)
                if h >= 2:
                    dve.wait_ge(pT_done, n - 1)
                V.tensor_tensor(s_fox[:, b, 0:3 * P], ps[:, 2, 0:3 * P], k2(B_MASK, 3 * P), ALU.add)
                V.tensor_tensor(s_fox[0:META, b, 3 * P:], ps[0:META, 3, 0:TOK],
                                con2[0:META, B_MASK + 3 * P:B_MASK + FOX_SCORES], ALU.add).then_inc(biased, 1)
                dve.wait_ge(biased, n + 1)
                V.tensor_reduce(nmax_f[:, b, 0:1], s_fox[:, b, 0:P], AX.X, ALU.max, negate=True)
                V.tensor_reduce(nmax_f[:, b, 1:2], s_fox[:, b, P:3 * P], AX.X, ALU.max, negate=True)
                V.tensor_reduce(nmax_f[0:META, b, 2:3], s_fox[0:META, b, 3 * P:], AX.X, ALU.max, negate=True).then_inc(nmax_done, 1)

            def diagonals(h):
                b = h % 2
                dve.wait_ge(probs, HEADS + f0 + h + 1)
                V.reciprocal(rden_f[:, b, 0:2], den_f[:, b, 0:2])
                link(V.reciprocal(rden_f[0:META, b, 2:3], den_f[0:META, b, 2:3]))
                for q in range(3):
                    m = P if q < 2 else META
                    ins = V.tensor_scalar(dg_fox[0:m, b, q, 0:m], con[0:m, 0:m], rden_f[0:m, b, q:q + 1], None, ALU.mult)
                ins.then_inc(dg_done, 1)

            def rest_of_output(hp):
                dve.wait_ge(at_hi, PAIRS + 3 * l + hp + 1)
                k = RET_HEADS + 2 + hp
                V.tensor_tensor(h_lo[:, k, :], acc(5, TOK), f(h_hi[:, k, :]), ALU.subtract).then_inc(at_ready, 1)

            def rotate(which):
                x1, x2 = rot_in[:, 2 * which, :], rot_in[:, 2 * which + 1, :]
                cos, sin = k2(B_COS, TOK), k2(B_SIN, TOK)
                dve.wait_ge(acc_free, st.u0 + ROT0 + 2 * which + 2)
                for half, (p, q, op) in enumerate(((cos, sin, ALU.subtract), (sin, cos, ALU.add))):
                    V.tensor_tensor(rtmp[:, 0, :], x1, p, ALU.mult)
                    link(V.tensor_tensor(rtmp[:, 1, :], x2, q, ALU.mult))
                    ins = V.tensor_tensor(rot[:, 2 * which + half, :], rtmp[:, 0, :], rtmp[:, 1, :], op)
                    ins.then_inc(rot_done, 1)
                    dve.wait_ge(rot_done, 4 * l + 2 * which + half + 1)

            def pool():
                dve.wait_ge(acc_free, st.u0 + st.units)
                end = POOL_PAD + TOK
                back = lambda a, w, m, d: a[:, m, w - 1 - d:end - d]
                both = slice(0, 2)
                link(V.tensor_tensor(w_a[:, both, 1:end], up[:, both, 1:end], up[:, both, 0:end - 1], ALU.add))
                link(V.tensor_tensor(w_b[:, both, 3:end], w_a[:, both, 3:end], w_a[:, both, 1:end - 2], ALU.add))
                link(V.tensor_tensor(w_a[:, 1, 7:end], w_b[:, 1, 7:end], w_b[:, 1, 3:end - 4], ALU.add))
                link(V.tensor_tensor(w_b[:, 1, 15:end], w_a[:, 1, 15:end], w_a[:, 1, 7:end - 8], ALU.add))
                tok = slice(POOL_PAD, end)
                half = P // 2
                for m in range(2):
                    V.tensor_copy(w_b[0:half, m, tok], w_a[0:half, m, tok]).then_inc(dve_step, 1)
                    own[0] += 1
                dve.wait_ge(dve_step, own[0])
                cnt = con2[:, B_CNT:B_CNT + 2 * TOK].rearrange("p (m t) -> p m t", m=2)
                link(V.tensor_tensor(w_b[:, :, tok], w_b[:, :, tok], cnt, ALU.mult))
                V.tensor_tensor(w_b[:, :, tok], w_b[:, :, tok], up[:, :, tok], ALU.subtract).then_inc(pool_done, 1)

            rest(0)
            cumulative_logits()
            for s in range(1, ROT0):
                rest(s)
            V.memset(up[:, :, 0:POOL_PAD], 0.0).then_inc(up_zero, 1)
            for h in range(FOX_HEADS):
                mask_max(h)
                rest(ROT0 + 2 * h)
                diagonals(h)
                if h >= 2 and h % 2 == 0:
                    rest_of_output(h // 2 - 1)
                rest(ROT0 + 2 * h + 1)
                if h in (2, 3):
                    rotate(h - 2)
            rest(WIN_TILES - 1)
            rest_of_output(2)

            def decay(h):
                n = RET_HEADS * l + h
                dve.wait_ge(ret_s, n + 1)
                if h >= 2:
                    dve.wait_ge(ret_o, n - 1)
                c = B_DEC + h * KEYS_ALL
                V.tensor_tensor(s_fox[:, h % 2, 0:KEY_AT[2]], ps[:, 3 + h % 2, 0:KEY_AT[2]], k2(c, KEY_AT[2]), ALU.mult)
                V.tensor_tensor(s_fox[0:META, h % 2, KEY_AT[2]:KEYS_ALL], ps[0:META, 3 + h % 2, KEY_AT[2]:KEYS_ALL],
                                con2[0:META, c + KEY_AT[2]:c + KEYS_ALL], ALU.mult).then_inc(ret_d, 1)

            for h in range(RET_HEADS):
                decay(h)
            pool()
            out_bank = (0, 1, 6, 7)
            for h in range(RET_HEADS):
                dve.wait_ge(ret_mean, RET_HEADS * l + h + 1)
                V.tensor_tensor(osb[:, h, :], osb[:, h, :], acc(out_bank[h], TOK), ALU.subtract).then_inc(ret_xc, 1)
            for m in range(2):
                dve.wait_ge(pool_hi, 2 * l + m + 1)
                V.scalar_tensor_tensor(h_lo[:, RET_HEADS + m, :], acc((2, 5)[m], TOK),
                                       par[:, C_PS + 2 * l + m:C_PS + 2 * l + m + 1], f(h_hi[:, RET_HEADS + m, :]),
                                       ALU.mult, ALU.subtract).then_inc(pool_ready, 1)
            dve.wait_ge(ret_std, l + 1)
            V.reciprocal(std4[0:RET_HEADS, :], std4[0:RET_HEADS, :]).then_inc(ret_rstd, 1)
            dve.wait_ge(silu2, l + 1)
            for h in range(RET_HEADS):
                n = RET_HEADS * l + h
                dve.wait_ge(ret_bc, n + 1)
                c = C_GN + n
                link(V.scalar_tensor_tensor(osb[:, h, :], osb[:, h, :], par[:, c:c + 1], acc(out_bank[h], TOK), ALU.mult, ALU.mult))
                link(V.tensor_tensor(osb[:, h, :], osb[:, h, :], gsb[:, h, :], ALU.mult))
                V.tensor_copy(h_hi[:, h, :], osb[:, h, :]).then_inc(ret_hi, 1)
                dve.wait_ge(ret_hi, n + 1)
                V.tensor_tensor(h_lo[:, h, :], osb[:, h, :], f(h_hi[:, h, :]), ALU.subtract).then_inc(ret_ready, 1)
            add_to_ax(by_name[f"mixo{l}"])

        start()
        ffn(0)
        layer_norm("out0")
        recurrent()
        layer_norm("rg_out")
        ffn(1)
        layer_norm("out1")
        keys_values()
        ffn(2)
        layer_norm("out2")
        attention()
        layer_norm("o")
        ffn(3)
        layer_norm("out3")
        layer_norm("emb")
        for l in range(LAYERS_2):
            hybrid(l)
            layer_norm(f"mixo{l}")
            ffn(4 + l)
            layer_norm(f"out{4 + l}")

    block_guard.__exit__(None, None, None)
    for s in reversed(sems):
        s.__exit__(None, None, None)
    psum.__exit__(None, None, None)
    slab.__exit__(None, None, None)


def constants():
    con = np.zeros((P, 3, P), np.float32)
    con[:, 0] = np.eye(P)
    con[:, 1] = 1.0 / D
    con[:RET_DV, 2] = 1.0 / RET_DV

    far = -1e33
    t = np.arange(SEQ)
    dist = t[:, None] - t[None, :]
    bias = np.full((P, SCORES), far, np.float32)
    for g, (window, dilation) in enumerate(DILATIONS):
        seen = (dist >= 0) & (dist <= window) & (dist % dilation == 0)
        b = np.where(seen, -dist, far)
        bias[:, g * P:(g + 1) * P] = b[:P, :P]
        bias[:, GROUPS * P + g * SEQ:GROUPS * P + (g + 1) * SEQ] = b[P:]

    c2 = np.zeros((P, N_B), np.float32)
    for h in range(RET_HEADS):
        c2[h, B_EXP + h * P:B_EXP + (h + 1) * P] = 1.0
        c2[:RET_DV, B_HEAD + RET_HEADS * h + h] = 1.0 / RET_DV
    for h in range(FOX_HEADS):
        c2[LOGIT_ROW + h, B_SEL + h * P:B_SEL + (h + 1) * P] = -1.0
    c2[:, B_ONE:B_ONE + TOK] = 1.0
    pos = np.arange(TOK, dtype=np.float32)
    freq = np.float32(10000.0) ** (-np.arange(HALF_DK, dtype=np.float32) / np.float32(HALF_DK))
    ang = (freq[:, None] * pos[None, :]).astype(np.float32)
    for h in range(RET_HEADS):
        c2[32 * h:32 * h + HALF_DK, B_COS:B_COS + TOK] = np.cos(ang)
        c2[32 * h:32 * h + HALF_DK, B_SIN:B_SIN + TOK] = np.sin(ang)
        log_gamma = np.log(1.0 - 2.0 ** (-5.0 - h))
        for k in range(3):
            keys = np.arange(k * P, min((k + 1) * P, TOK))
            away = np.arange(k * P, TOK)[None, :] - keys[:, None]
            decay = np.where(away >= 0, np.exp(log_gamma * np.maximum(away, 0)), 0.0) * RET_DK ** -0.5
            at = B_DEC + h * KEYS_ALL + KEY_AT[k]
            c2[:len(keys), at:at + KEY_COLS[k]] = decay
    below = np.where(np.arange(P)[:, None] >= np.arange(P)[None, :], 0.0, -1e30)
    c2[:, B_MASK:B_MASK + P] = below
    c2[:, B_MASK + 2 * P:B_MASK + 3 * P] = below
    c2[:META, B_MASK + 5 * P:B_MASK + 5 * P + META] = below[:META, :META]
    for n, w in enumerate(POOL_WINDOWS):
        rows = slice(64 * (n % 2), 64 * (n % 2) + 64)
        c2[rows, B_CNT + (n // 2) * TOK:B_CNT + (n // 2 + 1) * TOK] = 1.0 / np.minimum(np.arange(TOK) + 1, w)
    return con.reshape(P, 3 * P), bias, c2


def chunks(w, halves=1):
    K, M = w.shape
    w = w.reshape(halves, K // halves // P, P, M // P, P).transpose(3, 0, 2, 1, 4)
    return np.ascontiguousarray(w.reshape(M // P * halves, P, K // halves))


def paired(gate, up):
    K = gate.shape[0]
    return np.stack([gate.reshape(K, KF, P), up.reshape(K, KF, P)], 2).reshape(K, 2 * FF)


def hybrid_columns(w):
    parts = np.split(w, np.cumsum([192, 192, 384, 384, 256, 384, 384, 384]), axis=1)
    q, k, v, g, u, qf, kf, vf, logits = parts

    def halves(a):
        a = a.reshape(D, RET_HEADS, 2, HALF_DK)
        t = np.zeros((D, 2, RET_HEADS, 32), w.dtype)
        t[..., :HALF_DK] = a.transpose(0, 2, 1, 3)
        return t.reshape(D, 2 * P)

    def padded(a):
        t = np.zeros((D, RET_HEADS, P), w.dtype)
        t[..., :RET_DV] = a.reshape(D, RET_HEADS, RET_DV)
        return t

    g = padded(g)
    g[:, 0, LOGIT_ROW:LOGIT_ROW + FOX_HEADS] = logits
    g = g.reshape(D, RET_HEADS * P)
    return np.concatenate([g[:, :P], qf, kf, vf, halves(q), halves(k), padded(v).reshape(D, -1), g[:, P:], u], axis=1)


def hybrid_rows(w):
    t = np.zeros((RET_HEADS, P, D), w.dtype)
    t[:, :RET_DV] = w[:RET_HEADS * RET_DV].reshape(RET_HEADS, RET_DV, D)
    return np.concatenate([t.reshape(-1, D), w[RET_HEADS * RET_DV:]], axis=0)


def tiles(v):
    return v.reshape(-1, P).T


def kernel(**inputs):
    import concourse.bacc as bacc
    from concourse.bass_utils import run_bass_kernel_spmd

    a = {k: np.asarray(v) for k, v in inputs.items()}
    f32 = np.float32
    ffn_in = [paired(*np.split(a["ffn_w_in"][l, i], 2, axis=1)) for l in range(2) for i in range(2)]
    ffn_in += [paired(a["w_ffn1_2"][l], a["w_ffn3_2"][l]) for l in range(LAYERS_2)]
    ffn_out = [a["ffn_w_out"][l, i] for l in range(2) for i in range(2)] + [a["w_ffn2_2"][l] for l in range(LAYERS_2)]
    weights = {}
    for f in range(6):
        weights[f"in{f}"] = chunks(ffn_in[f])
        weights[f"out{f}"] = chunks(ffn_out[f], 2)
    y_cols, u_cols = np.split(a["rg_w_in"][0], 2, axis=1)
    weights["rg_u"], weights["rg_y"] = chunks(u_cols), chunks(y_cols)
    gate = a["rg_gate_w"][0].reshape(2, GATE_BLOCKS, 2, P, 2, P)
    weights["rg_gate"] = np.ascontiguousarray(gate.transpose(1, 3, 0, 4, 2, 5).reshape(GATE_BLOCKS, P, 8 * P))
    weights["rg_out"] = chunks(a["rg_w_out"][0])
    weights["kv"] = chunks(a["kv_w"])
    q = a["attn_w_q"][0].reshape(D, GROUPS, PAIRS, P).transpose(0, 2, 1, 3)
    weights["q"] = chunks(q.reshape(D, GROUPS * PAIRS * P))
    weights["o"] = chunks(a["attn_w_o"][0])
    for l in range(LAYERS_2):
        weights[f"mix{l}"] = chunks(hybrid_columns(a["w_in_2"][l]))
        weights[f"mixo{l}"] = chunks(hybrid_rows(a["w_out_2"][l]))

    gains = [a["ln_g"].reshape(-1), a["ln_emb_g_2"]]
    shifts = [a["ln_b"].reshape(-1), a["ln_emb_b_2"]]
    for l in range(LAYERS_2):
        gains += [a["ln1_g_2"][l], a["ln2_g_2"][l]]
        shifts += [a["ln1_b_2"][l], a["ln2_b_2"][l]]
    par = np.zeros((P, N_PAR), f32)
    par[:, C_G:C_B] = tiles(np.concatenate(gains))
    par[:, C_B:C_CW] = tiles(np.concatenate(shifts))
    par[:, C_CW:C_CB] = tiles(a["rg_conv_w"][0].reshape(-1))
    par[:, C_CB:C_GB] = tiles(a["rg_conv_b"][0])
    par[:, C_GB:C_LAM] = tiles(a["rg_gate_b"][0].reshape(-1))
    par[:, C_LAM:C_GN] = tiles(a["rg_lam"][0])
    par[:RET_DV, C_GN:C_PS] = a["ret_gn_g_2"].reshape(-1, RET_DV).T
    par[:, C_PS:C_BF] = tiles(a["pool_scale_2"].reshape(-1))
    par[LOGIT_ROW:LOGIT_ROW + FOX_HEADS, C_BF:] = a["b_f_2"].T
    poolw = np.zeros((P, LAYERS_2, 2, P), f32)
    for l in range(LAYERS_2):
        for n in range(len(POOL_WINDOWS)):
            s = slice(64 * (n % 2), 64 * (n % 2) + 64)
            poolw[s, l, n // 2, s] = a["pool_w_2"][l, n]
    con, bias, con2 = constants()
    feature_major = lambda v: np.ascontiguousarray(v.reshape(-1, KD, P).transpose(2, 1, 0))
    arrays = {"x": feature_major(a["x"][0]), "meta": feature_major(a["meta_2"]), "par": par, "con": con,
              "bias": bias, "con2": con2, "poolw": poolw}
    arrays.update({f"w_{n}": w for n, w in weights.items()})

    nc = bacc.Bacc("TRN2", target_bir_lowering=False, num_devices=1)
    d = {n: nc.dram_tensor(n, v.shape, mybir.dt.float32, kind="ExternalInput").ap() for n, v in arrays.items()}
    out = nc.dram_tensor("out", (P, KD, SEQ), mybir.dt.float32, kind="ExternalOutput").ap()
    build(nc, d["x"], d["meta"], d["par"], d["con"], d["bias"], d["con2"], d["poolw"],
          {n: d[f"w_{n}"] for n in weights}, out)
    got = run_bass_kernel_spmd(nc, [arrays], core_ids=[0]).results[0]["out"]
    return np.ascontiguousarray(got.transpose(2, 1, 0).reshape(1, SEQ, D))
```

```python
import numpy as np
import concourse.bass as bass
from concourse import mybir

P = 128
D = 1024
KD = D // P
SEQ = 256
META = 16
TOK = SEQ + META
FF = 2816
KF = FF // P
HALF_F = KF // 2
RNN = 1280
KR = RNN // P
GATE_BLOCKS = 5
CONV = 4
HEADS = 16
GROUPS = 3
PAIRS = HEADS // 2
HD = 64
DILATIONS = ((128, 1), (512, 4), (2048, 16))
SCORES = P + SEQ
RET_HEADS, RET_DK, RET_DV = 4, 48, 96
HALF_DK = RET_DK // 2
POOL_WINDOWS = (2, 4, 8, 16)
POOL_PAD = max(POOL_WINDOWS)
FOX_HEADS, FOX_W = 6, 384
LOGIT_ROW = RET_DV
LAYERS_2 = 2
ALPHA = float(4.0 ** 0.25)
LN_EPS = 1e-5
SLOTS = 4
AHEAD = 2
CHUNK = HALF_F * P
KEY_COLS = (TOK, TOK - P, TOK - 2 * P)
KEY_AT = (0, TOK, TOK + KEY_COLS[1])
KEYS_ALL = sum(KEY_COLS)
FOX_SCORES = P + 2 * P + TOK
MIX_K = RET_HEADS + 2 + 3
WIN_TILES = 23
FOX0, ROT0, VR0, GATE0, POOL0 = 1, 10, 14, 18, 21

N_LN = 11
C_G, C_B = 0, N_LN * KD
C_CW = 2 * N_LN * KD
C_CB = C_CW + CONV * KR
C_GB = C_CB + KR
C_LAM = C_GB + 2 * KR
C_GN = C_LAM + KR
C_PS = C_GN + LAYERS_2 * RET_HEADS
C_BF = C_PS + LAYERS_2 * 2
N_PAR = C_BF + LAYERS_2

B_EXP = 0
B_SEL = B_EXP + RET_HEADS * P
B_ONE = B_SEL + FOX_HEADS * P
B_COS = B_ONE + TOK
B_SIN = B_COS + TOK
B_DEC = B_SIN + TOK
B_MASK = B_DEC + RET_HEADS * KEYS_ALL
B_CNT = B_MASK + FOX_SCORES
B_HEAD = B_CNT + 2 * TOK
N_B = B_HEAD + RET_HEADS * RET_HEADS


class Stage:

    def __init__(self, name, chunks, tiles, units):
        self.name, self.chunks, self.tiles, self.units = name, chunks, tiles, units
        self.cols = tiles * P
        self.n0 = self.u0 = 0


def plan():
    ffn = lambda f: [Stage(f"in{f}", 2 * KF, KD, KF), Stage(f"out{f}", 2 * KD, HALF_F, KD)]
    s = ffn(0)
    s += [Stage("rg_u", KR, KD, KR), Stage("rg_gate", GATE_BLOCKS, 8, GATE_BLOCKS),
          Stage("rg_y", KR, KD, KR), Stage("rg_out", KD, KR, KD)]
    s += ffn(1) + [Stage("kv", 2 * KD, KD, 2 * KD)] + ffn(2)
    s += [Stage("q", GROUPS * PAIRS, KD, GROUPS * PAIRS), Stage("o", KD, KD, KD)] + ffn(3)
    for l in range(LAYERS_2):
        s += [Stage(f"mix{l}", WIN_TILES, KD, WIN_TILES), Stage(f"mixo{l}", KD, MIX_K, KD)] + ffn(4 + l)
    n, u = 0, SLOTS
    for st in s:
        st.n0, st.u0 = n, u
        n += st.chunks
        u += st.units
    for a, b in zip(s, s[1:]):
        a.next = b
    s[-1].next = None
    return s


def build(nc, x_in, meta_in, par_in, con_in, bias_in, con2_in, poolw_in, weights, out):
    fp32, fp32r = mybir.dt.float32, mybir.dt.float32r
    ALU, ACT = mybir.AluOpType, mybir.ActivationFunctionType
    AX = mybir.AxisListType
    stages = plan()
    by_name = {st.name: st for st in stages}

    first = -(-nc.sbuf_base // 32) * 32
    slab_bytes = nc.sbuf_usable_end - first - 64
    slab = nc.sbuf_tensor("slab", [P, slab_bytes // 4], fp32)
    slab.__enter__()
    cursor = [first]

    def place(name, free, dtype=fp32):
        t = nc.alloc_sbuf_tensor_at(name, [P, *free], dtype, offset=cursor[0])
        cursor[0] += -(-4 * int(np.prod(free)) // 32) * 32
        assert cursor[0] <= first + slab_bytes, name
        return t

    raw = [place(f"raw{i}", [CHUNK]) for i in range(SLOTS)]
    whi = [place(f"whi{i}", [CHUNK], fp32r) for i in range(SLOTS)]
    wlo = [place(f"wlo{i}", [CHUNK], fp32r) for i in range(SLOTS)]
    x_hi = place("x_hi", [KD, TOK], fp32r)
    x_lo = place("x_lo", [KD, TOK], fp32r)
    ax = place("ax", [KD, TOK])
    r_at = cursor[0]
    r = place("r", [KD, TOK])
    sq_at = cursor[0]
    sq = place("sq", [KD, TOK])
    hhi_at = cursor[0]
    h_hi = place("h_hi", [KF, TOK], fp32r)
    hlo_at = cursor[0]
    h_lo = place("h_lo", [KF, TOK], fp32r)
    con = place("con", [3 * P])
    ident, ones_d, ones_head = con[:, 0:P], con[:, P:2 * P], con[:, 2 * P:3 * P]
    par = place("par", [N_PAR])
    ab = place("ab", [N_LN * KD])
    eps = place("eps", [1])
    sums = place("sums", [2, TOK])
    msq = place("msq", [3])
    var_t = place("var_t", [3])
    std_t = place("std_t", [3])
    rstd_t = place("rstd_t", [3])
    spare = place("spare", [1])
    frow = place("frow", [2, TOK])
    sgate = place("sgate", [2, TOK])
    prod = place("prod", [2, TOK])
    spc = place("spc", [KR])
    nspc = place("nspc", [KR])
    lser = place("lser", [5, KR])
    mix_at = cursor[0]

    uc = place("uc", [KR, SEQ])
    dec = place("dec", [KR, SEQ])
    tnh = place("tnh", [KR, SEQ])
    ybr = place("ybr", [KR, SEQ])
    cursor[0] = mix_at
    kT = place("kT", [KD, SEQ])
    v_tok = place("v_tok", [2, D])
    qT = place("qT", [2, GROUPS, SEQ])
    dist = place("dist", [GROUPS, SCORES])
    s_at = place("s_at", [2, GROUPS, SCORES])
    nmax = place("nmax", [2, 2])
    den = place("den", [2, 2])
    rden = place("rden", [2, 2])
    pT = place("pT", [2, SCORES])
    cursor[0] = mix_at
    con2 = place("con2", [N_B])
    poolw = place("poolw", [LAYERS_2, 2, P])
    gsb = place("gsb", [RET_HEADS, TOK])
    qf_at = cursor[0]
    qf = place("qf", [3, TOK])
    kf = place("kf", [3, TOK])
    vf_tok = place("vf_tok", [3, FOX_W])
    cursor[0] = qf_at
    vr_tok = place("vr_tok", [3, RET_HEADS * P])
    cursor[0] = sq_at
    upad = place("upad", [2, CONV - 1 + SEQ])
    a2 = place("a2", [2, SEQ])
    cursor[0] = sq_at
    vf = place("vf", [3, TOK])
    vr = place("vr", [RET_HEADS, TOK])
    cursor[0] = sq_at
    osb = place("osb", [RET_HEADS, TOK])
    cursor[0] = r_at
    up = place("up", [2, POOL_PAD + TOK])
    w_a = place("w_a", [2, POOL_PAD + TOK])
    w_b = place("w_b", [2, POOL_PAD + TOK])
    std4 = place("std4", [TOK])
    cursor[0] = hhi_at + 10 * TOK * 4
    s_fox = place("s_fox", [2, FOX_SCORES])
    pT_fox = place("pT_fox", [2, KEYS_ALL])
    nmax_f = place("nmax_f", [2, 3])
    den_f = place("den_f", [2, 3])
    rden_f = place("rden_f", [2, 3])
    assert cursor[0] <= hlo_at
    cursor[0] = hlo_at + 10 * TOK * 4
    rot_in = place("rot_in", [4, TOK])
    rot = place("rot", [4, TOK])
    rtmp = place("rtmp", [2, TOK])
    sqh = place("sqh", [2, TOK])
    assert cursor[0] <= hlo_at + KF * TOK * 4

    psum = nc.psum_tensor("psum", [P, 8, 512], fp32)
    ps = psum.__enter__()

    sems = []

    def sem(name):
        s = nc.semaphore(name)
        sems.append(s)
        return s.__enter__()

    x_landed = [sem(f"x_landed{i}") for i in range(2)]
    inputs_in = sem("inputs_in")
    bias_landed = sem("bias_landed")
    con2_landed = sem("con2_landed")
    raw_landed = [sem(f"raw_landed{i}") for i in range(SLOTS)]
    w_hi_done = sem("w_hi_done")
    w_lo_done = sem("w_lo_done")
    chunk_used = sem("chunk_used")
    acc_free = sem("acc_free")
    x_hi_done = sem("x_hi_done")
    x_ready = sem("x_ready")
    ax_done = sem("ax_done")
    gate_done = sem("gate_done")
    h_hi_done = sem("h_hi_done")
    h_ready = sem("h_ready")
    mean_done = sem("mean_done")
    shift_done = sem("shift_done")
    shifted = sem("shifted")
    ax_shifted = sem("ax_shifted")
    xc_done = sem("xc_done")
    sums_done = sem("sums_done")
    stat_done = sem("stat_done")
    msq_done = sem("msq_done")
    sq_done = sem("sq_done")
    var_ready = sem("var_ready")
    std_done = sem("std_done")
    rstd_done = sem("rstd_done")
    spread = sem("spread")
    xn_done = sem("xn_done")
    y_done = sem("y_done")
    out_landed = sem("out_landed")
    dve_step = sem("dve_step")
    act_step = sem("act_step")
    par_done = sem("par_done")
    ser_e = sem("ser_e")
    spc_done = sem("spc_done")
    u_raw = sem("u_raw")
    pad_zero = sem("pad_zero")
    conv_done = sem("conv_done")
    u_hi_done = sem("u_hi_done")
    u_ready = sem("u_ready")
    in_gate = sem("in_gate")
    tanh_done = sem("tanh_done")
    iu_done = sem("iu_done")
    dec_done = sem("dec_done")
    v_arg = sem("v_arg")
    v_root = sem("v_root")
    gelu_done = sem("gelu_done")
    vT_done = sem("vT_done")
    v_copied = sem("v_copied")
    scored = sem("scored")
    biased = sem("biased")
    nmax_done = sem("nmax_done")
    probs = sem("probs")
    probs_ready = sem("probs_ready")
    pT_done = sem("pT_done")
    pT_copied = sem("pT_copied")
    pv_done = sem("pv_done")
    at_hi = sem("at_hi")
    at_ready = sem("at_ready")
    fx_done = sem("fx_done")
    fe_done = sem("fe_done")
    c_done = sem("c_done")
    vt2_done = sem("vt2_done")
    vt2_copied = sem("vt2_copied")
    rot_done = sem("rot_done")
    up_zero = sem("up_zero")
    pool_done = sem("pool_done")
    pool_mm = sem("pool_mm")
    pool_hi = sem("pool_hi")
    pool_ready = sem("pool_ready")
    ret_s = sem("ret_s")
    ret_d = sem("ret_d")
    ret_o = sem("ret_o")
    ret_osb = sem("ret_osb")
    ret_mean = sem("ret_mean")
    ret_xc = sem("ret_xc")
    ret_sq = sem("ret_sq")
    ret_var = sem("ret_var")
    ret_std = sem("ret_std")
    ret_rstd = sem("ret_rstd")
    ret_bc = sem("ret_bc")
    silu2 = sem("silu2")
    ret_hi = sem("ret_hi")
    ret_ready = sem("ret_ready")

    block_guard = nc.Block()
    block = block_guard.__enter__()

    def steps(eng, count, body, start=0, done=0):
        full = (count - AHEAD) // SLOTS
        for s in range(SLOTS * done, SLOTS * start):
            body(s // SLOTS, s % SLOTS)
        if full - start > 1:
            with eng.Fori(start, full) as i:
                for j in range(SLOTS):
                    body(i, j)
        else:
            full = start
        for s in range(SLOTS * full, count):
            body(s // SLOTS, s % SLOTS)

    def at(st, i, j):
        return SLOTS * i + (st.n0 + j), (st.n0 + j) % SLOTS, i + (st.n0 + j) // SLOTS

    def ahead(st, i, j):
        cols = st.cols
        if isinstance(i, int) and SLOTS * i + j + AHEAD >= st.chunks:
            if st.next is None:
                return None
            cols = st.next.cols
        return *at(st, i, j + AHEAD), cols

    norms = [("out0", SEQ, "x"), ("rg_out", SEQ, "x"), ("out1", SEQ, "x"), ("out2", SEQ, "x"),
             ("o", SEQ, "x"), ("out3", SEQ, "y"), ("emb", TOK, "x"), ("mixo0", TOK, "x"),
             ("out4", TOK, "x"), ("mixo1", SEQ, "x"), ("out5", SEQ, "y")]
    norm_no = {name: n for n, (name, _, _) in enumerate(norms)}
    version, versions = {"start": 0}, 1
    for name, _, kind in norms:
        if kind == "x":
            version[name] = versions
            versions += 1
    tok0 = lambda T: TOK - T
    x_of = {}
    now = "start"
    for st in stages:
        x_of[st.name] = version[now]
        if st.name in norm_no:
            now = st.name if st.name in version else "emb"
    tokens = {st.name: SEQ if st.n0 < by_name["mix0"].n0 or st.n0 > by_name["mix1"].n0 else TOK for st in stages}
    h_at = lambda st: META if st.name == "mixo1" else 0
    token_starts = lambda T: [tok0(T) + min(t * P, T - P) for t in range(-(-T // P))]
    n_sums = {name: n for n, name in enumerate(x[0] for x in norms if x[0] != "emb")}
    behind_norm = {a.next.name for a in stages if a.name in norm_no and a.next}
    shifts_before = lambda st: norm_no[st.name] + (KD - 1 if norm_no[st.name] > norm_no["emb"] else 0)
    acc = lambda bank, T: ps[:, bank, 0:T]
    h_base = [0, KF + KR, 2 * KF + KR, 3 * KF + KR, 4 * KF + KR, 5 * KF + KR]

    @block.sync
    def _(sp):
        def load(st, i, j, first=False):
            n, slot, _ = at(st, i, j)
            if not first:
                sp.wait_ge(w_lo_done, n - SLOTS + 1)
            sp.dma_start(raw[slot][:, 0:st.cols], weights[st.name][SLOTS * i + j]).then_inc(raw_landed[slot], 16)

        for st in stages:
            start = 0
            if st.n0 == 0:
                for j in range(SLOTS):
                    load(st, 0, j, first=True)
                    if j < 2:
                        half = slice(KD // 2 * j, KD // 2 * (j + 1))
                        sp.dma_start(r[:, half, META:TOK], x_in[:, half, :]).then_inc(x_landed[j], 16)
                sp.dma_start(par[:, :], par_in).then_inc(inputs_in, 16)
                sp.dma_start(con[:, :], con_in).then_inc(inputs_in, 16)
                sp.dma_start(r[:, :, 0:META], meta_in).then_inc(inputs_in, 16)
                start = 1
            if st.name == "in1":
                sp.wait_ge(h_ready, KF + KR)
                sp.dma_start(dist[:, :, :], bias_in).then_inc(bias_landed, 16)
            if st.name == "out3":
                sp.wait_ge(at_ready, PAIRS)
                sp.dma_start(con2[:, :], con2_in).then_inc(con2_landed, 16)
                sp.dma_start(poolw[:, :, :, ], poolw_in).then_inc(con2_landed, 16)
            full = st.chunks // SLOTS
            if full - start > 1:
                with sp.Fori(start, full) as i:
                    for j in range(SLOTS):
                        load(st, i, j)
            else:
                full = start
            for s in range(SLOTS * full, st.chunks):
                load(st, s // SLOTS, s % SLOTS)
        for k in range(KD):
            sp.wait_ge(y_done, KD + k + 1)
            sp.dma_start(out[:, k, :], r[:, k, META:TOK]).then_inc(out_landed, 16)
        sp.wait_ge(out_landed, 16 * KD)

    @block.tensor
    def _(pe):
        def products(slot, tile, hi, lo, bank, T, start, stop):
            w = slice(tile * P, (tile + 1) * P)
            nc.tensor.matmul(acc(bank, T), whi[slot][:, w], hi, start=start, stop=False)
            nc.tensor.matmul(acc(bank, T), whi[slot][:, w], lo, start=False, stop=False)
            return nc.tensor.matmul(acc(bank, T), wlo[slot][:, w], hi, start=False, stop=stop)

        def x_tile(k, T):
            return x_hi[:, k, tok0(T):TOK], x_lo[:, k, tok0(T):TOK]

        def from_x(st, i, j, bank, behind):
            T = tokens[st.name]
            n, slot, _ = at(st, i, j)
            pe.wait_ge(acc_free, behind)
            pe.wait_ge(w_lo_done, n + 1)
            for k in range(KD):
                last = products(slot, k, *x_tile(k, T), bank, T, k == 0, k == KD - 1)
            last.then_inc(chunk_used, 1)

        def first_two(st):
            T = tokens[st.name]
            for j in range(2):
                pe.wait_ge(w_lo_done, st.n0 + j + 1)
            for k in range(KD):
                pe.wait_ge(x_ready, KD * x_of[st.name] + k + 1)
                for j in range(2):
                    last = products((st.n0 + j) % SLOTS, k, *x_tile(k, T), j, T, k == 0, k == KD - 1)
                    if k == KD - 1:
                        last.then_inc(chunk_used, 1)

        def all_from_x(st, behind):
            pe.wait_ge(acc_free, st.u0)
            first_two(st)
            for j in range(2, SLOTS):
                from_x(st, 0, j, j, behind(0, j))
            steps(pe, st.chunks, lambda i, j: from_x(st, i, j, j, behind(i, j)), start=1, done=1)

        def from_h(st, i, j, tiles, ready=None):
            T = tokens[st.name]
            t = slice(h_at(st), h_at(st) + T)
            n, slot, _ = at(st, i, j)
            pe.wait_ge(acc_free, SLOTS * i + (st.u0 + j - 3))
            pe.wait_ge(w_lo_done, n + 1)
            for k in range(tiles):
                if ready and j == 0 and isinstance(i, int) and i == 0:
                    ready(k)
                last = products(slot, k, h_hi[:, k, t], h_lo[:, k, t], j, T, k == 0, k == tiles - 1)
            last.then_inc(chunk_used, 1)
            shift(st, i, j)

        def keep_warm(count):
            for _ in range(count):
                nc.tensor.matmul(acc(7, SEQ), h_hi[:, 0, 0:P], h_hi[:, 0, 0:SEQ], start=True, stop=True)

        def shift(st, i, j):
            if isinstance(i, int) and i == 0 and j == (2 if st.chunks == 2 * KD else 1):
                T = tokens[st.name]
                pe.wait_ge(inputs_in, 48)
                pe.wait_ge(acc_free, st.u0 + 1)
                nc.tensor.matmul(acc(7, T), ones_d, r[:, 0, tok0(T):TOK], start=True, stop=True).then_inc(shift_done, 1)

        def ffn(f):
            st = by_name[f"in{f}"]
            all_from_x(st, lambda i, j: 2 * i + (st.u0 + j // 2 - 1))
            so = by_name[f"out{f}"]
            T = tokens[so.name]
            pe.wait_ge(acc_free, so.u0)

            def half(i, j):
                n, slot, _ = at(so, i, j)
                if j % 2 == 0:
                    pe.wait_ge(acc_free, 2 * i + (so.u0 + j // 2 - 1))
                pe.wait_ge(w_lo_done, n + 1)
                for t in range(HALF_F):
                    k = (j % 2) * HALF_F + t
                    if t == 0 or k >= KF - 2:
                        pe.wait_ge(h_ready, h_base[f] + (HALF_F if k == 0 else KF - 2 if t == 0 else k + 1))
                    last = products(slot, t, h_hi[:, k, 0:T], h_lo[:, k, 0:T], j // 2, T, k == 0, k == KF - 1)
                last.then_inc(chunk_used, 1)
                shift(so, i, j)

            steps(pe, so.chunks, half, start=1)

        def layer_norm(name):
            n = norm_no[name]
            T = norms[n][1]
            t = slice(tok0(T), TOK)
            starts = token_starts(T)
            started = []

            def means(tile, first=False, last=False):
                return nc.tensor.matmul(acc(4, T), ones_d, tile[:, t], start=first, stop=last)

            def token_means(tile, col, last=False):
                for m, c in enumerate(starts):
                    ins = nc.tensor.matmul(ps[:, 5, col + m:col + m + 1], tile[:, c:c + P], ones_d[:, 0:1],
                                           start=not started, stop=last and m == len(starts) - 1, skip_group_check=True)
                    started.append(1)
                return ins

            if name == "emb":
                pe.wait_ge(y_done, 1)
                nc.tensor.matmul(acc(7, T), ones_d, r[:, 0, :], start=True, stop=True).then_inc(shift_done, 1)
                for k in range(KD):
                    pe.wait_ge(shifted, n + k + 1)
                    ins = means(r[:, k, :], k == 0, k == KD - 1)
                    token_means(r[:, k, :], 0)
                ins.then_inc(mean_done, 1)
                for k in range(KD):
                    pe.wait_ge(sq_done, KD * n + k + 1)
                    ins = token_means(sq[:, k, :], 4, k == KD - 1)
            else:
                pe.wait_ge(sums_done, n_sums[name] + 1)
                means(sums[:, 0, :], first=True)
                token_means(sums[:, 0, :], 0)
                token_means(sums[:, 1, :], 4)
                pe.wait_ge(acc_free, by_name[name].u0 + by_name[name].units)
                means(r[:, KD - 1, :], last=True).then_inc(mean_done, 1)
                token_means(r[:, KD - 1, :], 0)
                pe.wait_ge(sq_done, KD * (n + 1))
                ins = token_means(sq[:, KD - 1, :], 4, True)
            ins.then_inc(stat_done, 1)
            keep_warm(6)
            pe.wait_ge(rstd_done, n + 1)
            for m, c in enumerate(starts):
                ins = nc.tensor.matmul(ps[:, 6, c - starts[0]:c - starts[0] + P], rstd_t[:, m:m + 1].broadcast_to([P, P]),
                                       ident, start=True, stop=True)
            ins.then_inc(spread, 1)
            keep_warm(12)

        def recurrent():
            st = by_name["rg_u"]
            all_from_x(st, lambda i, j: SLOTS * i + (st.u0 + j - 3))
            sg = by_name["rg_gate"]
            for b in range(GATE_BLOCKS):
                n, slot, _ = at(sg, b // SLOTS, b % SLOTS)
                pe.wait_ge(w_lo_done, n + 1)
                pe.wait_ge(acc_free, sg.u0 + b)
                pe.wait_ge(u_ready, 2 * b + 2)
                for m in range(4):
                    for k in range(2):
                        c = KR + 2 * b + k
                        last = products(slot, 2 * m + k, h_hi[:, c, 0:SEQ], h_lo[:, c, 0:SEQ], m, SEQ, k == 0, k == 1)
                last.then_inc(chunk_used, 1)
            sy = by_name["rg_y"]
            pe.wait_ge(acc_free, sy.u0)
            steps(pe, sy.chunks, lambda i, j: from_x(sy, i, j, j, SLOTS * i + (sy.u0 + j - 3)))
            so = by_name["rg_out"]
            pe.wait_ge(acc_free, so.u0)
            steps(pe, so.chunks, lambda i, j: from_h(so, i, j, KR, ready=lambda k: pe.wait_ge(h_ready, KF + k + 1)))

        def keys_values():
            st = by_name["kv"]
            all_from_x(st, lambda i, j: SLOTS * i + (st.u0 + j - 3))
            pe.wait_ge(acc_free, st.u0 + st.units)
            for t in range(2):
                for m in range(KD):
                    last = nc.tensor.transpose(ps[:, 4 + 2 * t + m // 4, (m % 4) * P:(m % 4 + 1) * P],
                                               sq[:, m, t * P:(t + 1) * P], ident)
            last.then_inc(vT_done, 1)

        def attention():
            st = by_name["q"]
            pe.wait_ge(acc_free, st.u0)
            pe.wait_ge(v_copied, 4)

            def query(s):
                if s == 0:
                    first_two(st)
                if s >= 2:
                    from_x(st, s // SLOTS, s % SLOTS, s % 2, st.u0 + s - 1)

            def scores(a):
                hp, rows = a // 2, slice(HD * (a % 2), HD * (a % 2 + 1))
                pe.wait_ge(acc_free, st.u0 + GROUPS * (hp + 1))
                if a:
                    pe.wait_ge(biased, a)
                for g in range(GROUPS):
                    nc.tensor.matmul(ps[:, 2 + g, 0:P], qT[rows, hp % 2, g, 0:P], kT[rows, hp, 0:P], start=True, stop=True)
                    last = nc.tensor.matmul(ps[:, 2 + g, P:SCORES], qT[rows, hp % 2, g, P:SEQ], kT[rows, hp, :],
                                            start=True, stop=True)
                last.then_inc(scored, 1)

            def transposed(a):
                pe.wait_ge(probs_ready, a + 1)
                if a:
                    pe.wait_ge(pT_copied, a)
                for n in range(SCORES // P):
                    last = nc.tensor.transpose(ps[:, 5, n * P:(n + 1) * P], s_at[:, a % 2, 0, n * P:(n + 1) * P], ident)
                last.then_inc(pT_done, 1)

            def values(a):
                hp, e = a // 2, a % 2
                o = ps[HD * e:HD * (e + 1), 6 + hp % 2, :]
                pe.wait_ge(pT_copied, a + 1)
                if hp >= 2:
                    pe.wait_ge(at_ready, hp - 1)
                col = slice(HD * a, HD * (a + 1))
                nc.tensor.matmul(o[:, 0:SEQ], v_tok[:, 0, col], pT[:, a % 2, 0:SEQ], start=True, stop=False)
                nc.tensor.matmul(o[:, P:SEQ], v_tok[:, 1, col], pT[:, a % 2, SEQ:SEQ + P],
                                 start=False, stop=True).then_inc(pv_done, 1)

            for hp in range(PAIRS + 2):
                a, b, behind = 2 * hp - 2, 2 * hp - 1, 2 * hp - 3
                if 1 <= hp <= PAIRS:
                    scores(a)
                if hp >= 2:
                    transposed(behind)
                if hp < PAIRS:
                    query(3 * hp)
                if hp >= 2:
                    values(behind)
                if 1 <= hp <= PAIRS:
                    scores(b)
                if hp < PAIRS:
                    query(3 * hp + 1)
                if 1 <= hp <= PAIRS:
                    transposed(a)
                if hp < PAIRS:
                    query(3 * hp + 2)
                if 1 <= hp <= PAIRS:
                    values(a)
            so = by_name["o"]
            steps(pe, so.chunks, lambda i, j: from_h(so, i, j, KD, ready=lambda k: pe.wait_ge(at_ready, k + 1)))

        def hybrid(l):
            st = by_name[f"mix{l}"]
            pe.wait_ge(acc_free, st.u0)
            pe.wait_ge(con2_landed, 32)
            f0 = FOX_HEADS * l

            def tile(s):
                if s == 0:
                    first_two(st)
                if s >= 2:
                    from_x(st, s // SLOTS, s % SLOTS, s % 2, st.u0 + s - 1)

            def token_tiles(t):
                return slice(t * P, min((t + 1) * P, TOK))

            def fox_scores(h):
                rows = slice(HD * (h % 2), HD * (h % 2 + 1))
                if h == 0:
                    pe.wait_ge(c_done, l + 1)
                    pe.wait_ge(acc_free, st.u0 + FOX0 + 6)
                if f0 + h:
                    pe.wait_ge(biased, HEADS + f0 + h)
                for q, (bank, c, n) in enumerate(((2, 0, P), (2, P, 2 * P), (3, 0, TOK))):
                    o = ps[0:P if q < 2 else META, bank, c:c + n]
                    nc.tensor.matmul(o, qf[rows, h // 2, token_tiles(q)], kf[rows, h // 2, 0:n], start=True, stop=False)
                    sel = con2[LOGIT_ROW:LOGIT_ROW + FOX_HEADS, B_SEL + h * P:B_SEL + h * P + (P if q < 2 else META)]
                    last = nc.tensor.matmul(o, sel, frow[LOGIT_ROW:LOGIT_ROW + FOX_HEADS, 1, 0:n], start=False, stop=True)
                last.then_inc(scored, 1)

            def fox_transposed(h):
                pe.wait_ge(probs_ready, HEADS + f0 + h + 1)
                pe.wait_ge(pT_copied, HEADS + f0 + h)
                b = h % 2
                for k in range(3):
                    for q in range(k, 3):
                        m = P if q < 2 else META
                        kn = P if k < 2 else META
                        c = (0, P, 3 * P)[q] + k * P
                        o = ps[0:kn, 4, KEY_AT[k] + (q - k) * P:KEY_AT[k] + (q - k) * P + m]
                        last = nc.tensor.transpose(o, s_fox[0:m, b, c:c + kn], con[0:m, 0:m])
                last.then_inc(pT_done, 1)

            def by_values(o, v, col, weights_t):
                for k in range(3):
                    kn = P if k < 2 else META
                    last = nc.tensor.matmul(o[:, k * P:TOK], v[0:kn, k, col],
                                            weights_t[0:kn, KEY_AT[k]:KEY_AT[k] + KEY_COLS[k]], start=k == 0, stop=k == 2)
                return last

            def fox_values(h):
                o = ps[HD * (h % 2):HD * (h % 2 + 1), 5, :]
                pe.wait_ge(pT_copied, HEADS + f0 + h + 1)
                if h == 0:
                    pe.wait_ge(vt2_copied, 4 * l + 2)
                pe.wait_ge(at_ready, PAIRS + 3 * l + h // 2)
                by_values(o, vf_tok, slice(HD * h, HD * (h + 1)), pT_fox[:, h % 2, :]).then_inc(pv_done, 1)

            def transposes(src, tiles, dst_bank):
                for t in range(3):
                    for m in range(tiles):
                        last = nc.tensor.transpose(ps[0:P if t < 2 else META, dst_bank[t][0], dst_bank[t][1] + m * P:dst_bank[t][1] + (m + 1) * P],
                                                   src[:, m, token_tiles(t)], ident)
                return last

            for s in range(FOX0 + 9):
                tile(s)
            pe.wait_ge(acc_free, st.u0 + ROT0)
            transposes(vf, 3, ((5, 0), (6, 0), (7, 0))).then_inc(vt2_done, 1)
            for h in range(FOX_HEADS):
                fox_scores(h)
                tile(ROT0 + 2 * h)
                if h:
                    fox_values(h - 1)
                tile(ROT0 + 2 * h + 1)
                fox_transposed(h)
            tile(WIN_TILES - 1)
            fox_values(FOX_HEADS - 1)
            pe.wait_ge(vt2_copied, 4 * l + 2)
            pe.wait_ge(biased, HEADS + f0 + FOX_HEADS)
            transposes(vr, RET_HEADS, ((6, 0), (7, 0), (2, 0))).then_inc(vt2_done, 1)
            pe.wait_ge(rot_done, 4 * (l + 1))
            pe.wait_ge(acc_free, st.u0 + st.units)
            pe.wait_ge(at_ready, PAIRS + 3 * l + 3)
            out_bank = (0, 1, 6, 7)

            def ret_scores(h):
                n = RET_HEADS * l + h
                rows = slice(32 * h, 32 * h + 32)
                if h >= 2:
                    pe.wait_ge(ret_d, n - 1)
                for k in range(3):
                    kn = P if k < 2 else META
                    o = ps[0:kn, 3 + h % 2, KEY_AT[k]:KEY_AT[k] + KEY_COLS[k]]
                    for half in range(2):
                        last = nc.tensor.matmul(o, rot[rows, 2 + half, token_tiles(k)], rot[rows, half, k * P:TOK],
                                                start=half == 0, stop=half == 1)
                last.then_inc(ret_s, 1)

            def ret_values(h):
                n = RET_HEADS * l + h
                pe.wait_ge(ret_d, n + 1)
                if h == 0:
                    pe.wait_ge(vt2_copied, 4 * l + 4)
                by_values(acc(out_bank[h], 512), vr_tok, slice(P * h, P * (h + 1)), s_fox[:, h % 2, 0:KEYS_ALL]).then_inc(ret_o, 1)

            ret_scores(0)
            ret_scores(1)
            for h in range(RET_HEADS):
                ret_values(h)
                if h + 2 < RET_HEADS:
                    ret_scores(h + 2)
            pe.wait_ge(pool_done, l + 1)
            pe.wait_ge(vt2_copied, 4 * l + 4)
            for m in range(2):
                last = nc.tensor.matmul(acc((2, 5)[m], TOK), poolw[:, l, m, :], w_b[:, m, POOL_PAD:], start=True, stop=True)
            last.then_inc(pool_mm, 1)
            for h in range(RET_HEADS):
                n = RET_HEADS * l + h
                pe.wait_ge(ret_osb, n + 1)
                nc.tensor.matmul(acc(out_bank[h], TOK), ones_head, osb[:, h, :], start=True, stop=True).then_inc(ret_mean, 1)
            for h in range(RET_HEADS):
                n = RET_HEADS * l + h
                pe.wait_ge(ret_sq, n + 1)
                last = nc.tensor.matmul(ps[0:RET_HEADS, 3, 0:TOK], con2[:, B_HEAD + RET_HEADS * h:B_HEAD + RET_HEADS * (h + 1)],
                                        sqh[:, h % 2, :], start=h == 0, stop=h == RET_HEADS - 1)
                last.then_inc(ret_var, 1)
            pe.wait_ge(ret_rstd, l + 1)
            for h in range(RET_HEADS):
                nc.tensor.matmul(acc(out_bank[h], TOK), con2[0:RET_HEADS, B_EXP + h * P:B_EXP + (h + 1) * P],
                                 std4[0:RET_HEADS, :], start=True, stop=True).then_inc(ret_bc, 1)
            so = by_name[f"mixo{l}"]

            def mixed(k):
                if k < RET_HEADS:
                    pe.wait_ge(ret_ready, RET_HEADS * l + k + 1)
                elif k == RET_HEADS:
                    pe.wait_ge(pool_ready, 2 * l + 2)

            steps(pe, so.chunks, lambda i, j: from_h(so, i, j, MIX_K, ready=mixed))

        ffn(0)
        layer_norm("out0")
        recurrent()
        layer_norm("rg_out")
        ffn(1)
        layer_norm("out1")
        keys_values()
        ffn(2)
        layer_norm("out2")
        attention()
        layer_norm("o")
        ffn(3)
        layer_norm("out3")
        layer_norm("emb")
        for l in range(LAYERS_2):
            hybrid(l)
            layer_norm(f"mixo{l}")
            ffn(4 + l)
            layer_norm(f"out{4 + l}")


    @block.scalar
    def _(act):
        own = [0]

        def link(ins):
            own[0] += 1
            ins.then_inc(act_step, 1)
            act.wait_ge(act_step, own[0])

        def round_chunk(n, slot, rnd, cols):
            act.wait_ge(raw_landed[slot], 16 * rnd + 16)
            if not isinstance(n, int) or n >= SLOTS:
                act.wait_ge(chunk_used, n - SLOTS + 1)
            nc.scalar.activation(whi[slot][:, 0:cols], raw[slot][:, 0:cols], ACT.Copy).then_inc(w_hi_done, 1)

        def next_chunk(st, i, j):
            a = ahead(st, i, j)
            if a:
                round_chunk(*a)

        def round_ahead(st, i, j):
            if st.name in behind_norm and isinstance(i, int) and i == 0:
                if j >= 2:
                    next_chunk(st, i, j)
                n, t = last_norm
                for k in range((0, 0, 3, 6)[j], (0, 3, 6, KD)[j]):
                    nc.scalar.activation(ax[:, k, t], r[:, k, t], ACT.Identity, scale=ALPHA,
                                         bias=ab[:, KD * n + k:KD * n + k + 1]).then_inc(ax_done, 1)
            else:
                next_chunk(st, i, j)

        last_norm = []

        def before_norm(st):
            nc.scalar.activation(spare[:, :], eps[:, :], ACT.Sqrt)
            if st.next:
                round_chunk(*ahead(st.next, 0, 0))

        def start():
            round_chunk(0, 0, 0, stages[0].cols)
            for k in range(KD):
                act.wait_ge(x_landed[k // (KD // 2)], 16)
                nc.scalar.activation(x_hi[:, k, META:TOK], r[:, k, META:TOK], ACT.Copy).then_inc(x_hi_done, 1)
                if k == 1:
                    round_chunk(1, 1, 0, stages[0].cols)

        def parameters():
            for k in range(KD):
                nc.scalar.activation(ax[:, k, META:TOK], r[:, k, META:TOK], ACT.Copy, scale=ALPHA).then_inc(ax_done, 1)
            act.wait_ge(inputs_in, 48)
            nc.scalar.activation(ab[:, :], par[:, C_B:C_B + N_LN * KD], ACT.Copy, scale=ALPHA).then_inc(par_done, 1)
            link(nc.scalar.activation(lser[:, 0, :], par[:, C_LAM:C_LAM + KR], ACT.Abs))
            nc.scalar.activation(lser[:, 1, :], lser[:, 0, :], ACT.Exp, scale=-1.0).then_inc(ser_e, 1)
            act.wait_ge(par_done, 2)

        def ffn(f):
            st = by_name[f"in{f}"]
            T = tokens[st.name]

            def step(i, j):
                round_ahead(st, i, j)
                if j % 2 == 0:
                    p = 2 * i + j // 2
                    act.wait_ge(chunk_used, SLOTS * i + (st.n0 + j + 1))
                    act.wait_ge(acc_free, 2 * i + (st.u0 + j // 2 - 1))
                    nc.scalar.activation(sgate[:, j // 2, 0:T], acc(j, T), ACT.Silu).then_inc(gate_done, 1)

            steps(act, st.chunks, step, start=1)
            if f == 0:
                parameters()
            so = by_name[f"out{f}"]

            def out_step(i, j):
                round_ahead(so, i, j)
                if j % 2:
                    if isinstance(i, int) and SLOTS * i + j == so.chunks - 1:
                        before_norm(so)
                    square(so, 2 * i, j // 2)

            steps(act, so.chunks, out_step, start=1)

        def square(st, i, j):
            T = tokens[st.name]
            t = slice(tok0(T), TOK)
            if isinstance(i, int) and i + j == 0:
                return
            if isinstance(i, int) and i + j == 1:
                act.wait_ge(shifted, shifts_before(st) + 1)
                nc.scalar.activation(sq[:, 0, t], r[:, 0, t], ACT.Square).then_inc(sq_done, 1)
            act.wait_ge(acc_free, i + (st.u0 + j + 1))
            nc.scalar.activation(sq[:, i + j, t], r[:, i + j, t], ACT.Square).then_inc(sq_done, 1)

        def squares(st):
            def step(i, j):
                round_ahead(st, i, j)
                if SLOTS * i + j == st.chunks - 1:
                    before_norm(st)
                square(st, SLOTS * i, j)

            steps(act, st.chunks, step)

        def layer_norm(name):
            n = norm_no[name]
            _, T, kind = norms[n]
            t = slice(tok0(T), TOK)
            nt = len(token_starts(T))
            act.wait_ge(stat_done, n + 1)
            nc.scalar.activation(msq[:, 0:nt], ps[:, 5, 0:nt], ACT.Square).then_inc(msq_done, 1)
            act.wait_ge(var_ready, n + 1)
            nc.scalar.activation(std_t[:, 0:nt], var_t[:, 0:nt], ACT.Sqrt, bias=eps[:, 0:1]).then_inc(std_done, 1)
            nxt = None if name == "out3" else by_name["out3" if name == "emb" else name].next
            if nxt:
                round_chunk(*ahead(nxt, 0, 1))
            b = lambda k: par[:, C_B + KD * n + k:C_B + KD * n + k + 1]
            for k in range(KD):
                act.wait_ge(xn_done, KD * n + k + 1)
                if kind == "x":
                    nc.scalar.activation(x_hi[:, k, t], r[:, k, t], ACT.Identity, bias=b(k)).then_inc(x_hi_done, 1)
                else:
                    nc.scalar.activation(r[:, k, t], r[:, k, t], ACT.Identity, bias=b(k)).then_inc(y_done, 1)
            if name == "out3":
                for k in range(KD):
                    act.wait_ge(shifted, n + 1 + k + 1)
                    nc.scalar.activation(sq[:, k, :], r[:, k, :], ACT.Square).then_inc(sq_done, 1)
            last_norm[:] = n, t

        def recurrent():
            st = by_name["rg_u"]
            col = lambda c, k: par[:, c + k:c + k + 1]
            for s in range(KR):
                round_ahead(st, s // SLOTS, s % SLOTS)
                act.wait_ge(chunk_used, st.n0 + s + 1)
                if s == 0:
                    act.wait_ge(pad_zero, 1)
                if s >= 2:
                    act.wait_ge(conv_done, s - 1)
                bank = acc(s % SLOTS, SEQ)
                nc.scalar.activation(upad[:, s % 2, CONV - 1:], bank, ACT.Copy).then_inc(u_raw, 1)
                nc.scalar.activation(uc[:, s, :], bank, ACT.Identity, scale=col(C_CW, (CONV - 1) * KR + s),
                                     bias=col(C_CB, s)).then_inc(acc_free, 1)
            sg = by_name["rg_gate"]
            act.wait_ge(spc_done, 1)
            for b in range(GATE_BLOCKS):
                round_ahead(sg, b // SLOTS, b % SLOTS)
                act.wait_ge(chunk_used, sg.n0 + b + 1)
                for d in range(2):
                    c = 2 * b + d
                    nc.scalar.activation(dec[:, c, :], acc(d, SEQ), ACT.Sigmoid, bias=col(C_GB, c)).then_inc(act_step, 1)
                    own[0] += 1
                for d in range(2):
                    c = 2 * b + d
                    last = nc.scalar.activation(ybr[:, c, :], acc(2 + d, SEQ), ACT.Sigmoid, bias=col(C_GB, KR + c))
                    last.then_inc(acc_free if d else in_gate, 1)
                act.wait_ge(act_step, own[0])
                for d in range(2):
                    c = 2 * b + d
                    nc.scalar.activation(tnh[:, c, :], dec[:, c, :], ACT.Tanh, scale=spc[:, c:c + 1]).then_inc(tanh_done, 1)
            sy = by_name["rg_y"]
            for s in range(KR):
                round_ahead(sy, s // SLOTS, s % SLOTS)
                act.wait_ge(tanh_done, s + 1)
                nc.scalar.activation(dec[:, s, :], dec[:, s, :], ACT.Exp, scale=nspc[:, s:s + 1]).then_inc(dec_done, 1)
                act.wait_ge(chunk_used, sy.n0 + s + 1)
                if s % 2 == 0:
                    act.wait_ge(iu_done, s // 2 + 1)
                nc.scalar.activation(ybr[:, s, :], acc(s % SLOTS, SEQ), ACT.Copy).then_inc(acc_free, 1)
            for half in range(2):
                c = slice(5 * half, 5 * half + 5)
                act.wait_ge(v_arg, 5 * half + 5)
                nc.scalar.activation(tnh[:, c, :], tnh[:, c, :], ACT.Sqrt).then_inc(v_root, 1)
            act.wait_ge(acc_free, sy.u0 + KR)
            for half in range(2):
                c = slice(5 * half, 5 * half + 5)
                nc.scalar.activation(ybr[:, c, :], ybr[:, c, :], ACT.Gelu_apprx_tanh).then_inc(gelu_done, 1)
            squares(by_name["rg_out"])

        def keys_values():
            st = by_name["kv"]
            for s in range(2 * KD):
                round_ahead(st, s // SLOTS, s % SLOTS)
                act.wait_ge(chunk_used, st.n0 + s + 1)
                dst = kT[:, s, :] if s < KD else sq[:, s - KD, 0:SEQ]
                nc.scalar.activation(dst, acc(s % SLOTS, SEQ), ACT.Copy).then_inc(acc_free, 1)
            act.wait_ge(vT_done, 1)
            for t in range(2):
                for half in range(2):
                    nc.scalar.activation(v_tok[:, t, 512 * half:512 * half + 512], ps[:, 4 + 2 * t + half, :],
                                         ACT.Copy).then_inc(v_copied, 1)

        def attention():
            st = by_name["q"]

            def query(s):
                round_ahead(st, s // SLOTS, s % SLOTS)
                act.wait_ge(chunk_used, st.n0 + s + 1)
                hp = s // GROUPS
                if hp >= 2:
                    act.wait_ge(scored, 2 * hp - 2)
                nc.scalar.activation(qT[:, hp % 2, s % GROUPS, :], acc(s % 2, SEQ), ACT.Copy,
                                     scale=float(HD) ** -0.5).then_inc(acc_free, 1)

            def exps(a):
                act.wait_ge(nmax_done, a + 1)
                b = a % 2
                nc.scalar.activation(s_at[:, b, :, 0:P], s_at[:, b, :, 0:P], ACT.Exp,
                                     bias=nmax[:, b, 0:1], accum_out=den[:, b, 0:1])
                nc.scalar.activation(s_at[:, b, :, P:], s_at[:, b, :, P:], ACT.Exp,
                                     bias=nmax[:, b, 1:2], accum_out=den[:, b, 1:2]).then_inc(probs, 1)

            def copy_transposed(a):
                act.wait_ge(pT_done, a + 1)
                if a >= 2:
                    act.wait_ge(pv_done, a - 1)
                nc.scalar.activation(pT[:, a % 2, :], ps[:, 5, 0:SCORES], ACT.Copy).then_inc(pT_copied, 1)

            def round_output(hp):
                act.wait_ge(pv_done, 2 * hp + 2)
                nc.scalar.activation(h_hi[:, hp, 0:SEQ], acc(6 + hp % 2, SEQ), ACT.Copy).then_inc(at_hi, 1)

            for hp in range(PAIRS + 2):
                a, b, behind = 2 * hp - 2, 2 * hp - 1, 2 * hp - 3
                if hp >= 2:
                    copy_transposed(behind)
                if 1 <= hp <= PAIRS:
                    exps(a)
                if hp < PAIRS:
                    query(3 * hp)
                if hp >= 2:
                    round_output(hp - 2)
                if hp < PAIRS:
                    query(3 * hp + 1)
                if 1 <= hp <= PAIRS:
                    copy_transposed(a)
                    exps(b)
                if hp < PAIRS:
                    query(3 * hp + 2)
            squares(by_name["o"])

        def hybrid(l):
            st = by_name[f"mix{l}"]
            f0 = FOX_HEADS * l
            lr = slice(LOGIT_ROW, LOGIT_ROW + FOX_HEADS)

            def tile(s):
                round_ahead(st, s // SLOTS, s % SLOTS)
                act.wait_ge(chunk_used, st.n0 + s + 1)
                src = acc(s % 2, TOK)
                if s == 0:
                    bf = par[lr, C_BF + l:C_BF + l + 1]
                    nc.scalar.activation(sgate[lr, 0, :], ps[lr, 0, 0:TOK], ACT.Identity, bias=bf).then_inc(fx_done, 1)
                    link(nc.scalar.activation(sgate[lr, 1, :], ps[lr, 0, 0:TOK], ACT.Abs, bias=bf))
                    nc.scalar.activation(sgate[lr, 1, :], sgate[lr, 1, :], ACT.Exp, scale=-1.0).then_inc(fe_done, 1)
                    dst, scale = gsb[:, 0, :], 1.0
                elif s < FOX0 + 3:
                    dst, scale = qf[:, s - FOX0, :], float(HD) ** -0.5
                elif s < FOX0 + 6:
                    dst, scale = kf[:, s - FOX0 - 3, :], 1.0
                elif s < ROT0:
                    dst, scale = vf[:, s - FOX0 - 6, :], 1.0
                elif s < VR0:
                    dst, scale = rot_in[:, s - ROT0, :], 1.0
                elif s < GATE0:
                    dst, scale = vr[:, s - VR0, :], 1.0
                elif s < POOL0:
                    dst, scale = gsb[:, 1 + s - GATE0, :], 1.0
                else:
                    if s == POOL0:
                        act.wait_ge(up_zero, l + 1)
                    dst, scale = up[:, s - POOL0, POOL_PAD:], 1.0
                nc.scalar.activation(dst, src, ACT.Copy, scale=scale).then_inc(acc_free, 1)

            def exps(h):
                act.wait_ge(nmax_done, HEADS + f0 + h + 1)
                b = h % 2
                for q, (c, n) in enumerate(((0, P), (P, 2 * P), (3 * P, TOK))):
                    m = P if q < 2 else META
                    last = nc.scalar.activation(s_fox[0:m, b, c:c + n], s_fox[0:m, b, c:c + n], ACT.Exp,
                                                bias=nmax_f[0:m, b, q:q + 1], accum_out=den_f[0:m, b, q:q + 1])
                last.then_inc(probs, 1)

            def copy_transposed(h):
                act.wait_ge(pT_done, HEADS + f0 + h + 1)
                if h >= 2:
                    act.wait_ge(pv_done, HEADS + f0 + h - 1)
                nc.scalar.activation(pT_fox[:, h % 2, 0:KEY_AT[2]], ps[:, 4, 0:KEY_AT[2]], ACT.Copy).then_inc(act_step, 1)
                own[0] += 1
                nc.scalar.activation(pT_fox[0:META, h % 2, KEY_AT[2]:], ps[0:META, 4, KEY_AT[2]:KEYS_ALL], ACT.Copy).then_inc(pT_copied, 1)

            def round_output(hp):
                act.wait_ge(pv_done, HEADS + f0 + 2 * hp + 2)
                nc.scalar.activation(h_hi[:, RET_HEADS + 2 + hp, :], acc(5, TOK), ACT.Copy).then_inc(at_hi, 1)

            def copy_values(n, dst, banks, cols):
                act.wait_ge(vt2_done, 2 * l + n + 1)
                for t in range(2):
                    ins = nc.scalar.activation(dst[:, t, 0:cols], ps[:, banks[t], 0:cols], ACT.Copy)
                    if t:
                        ins.then_inc(vt2_copied, 1)
                nc.scalar.activation(dst[0:META, 2, 0:cols], ps[0:META, banks[2], 0:cols], ACT.Copy).then_inc(vt2_copied, 1)

            for s in range(ROT0):
                tile(s)
            copy_values(0, vf_tok, (5, 6, 7), FOX_W)
            for h in range(FOX_HEADS):
                tile(ROT0 + 2 * h)
                exps(h)
                if h >= 2 and h % 2 == 0:
                    round_output(h // 2 - 1)
                tile(ROT0 + 2 * h + 1)
                copy_transposed(h)
            tile(WIN_TILES - 1)
            round_output(2)
            copy_values(1, vr_tok, (6, 7, 2), RET_HEADS * P)
            act.wait_ge(acc_free, st.u0 + st.units)
            nc.scalar.activation(gsb[:, :, :], gsb[:, :, :], ACT.Silu).then_inc(silu2, 1)
            out_bank = (0, 1, 6, 7)
            for h in range(RET_HEADS):
                act.wait_ge(ret_o, RET_HEADS * l + h + 1)
                nc.scalar.activation(osb[:, h, :], acc(out_bank[h], TOK), ACT.Copy).then_inc(ret_osb, 1)
            act.wait_ge(pool_mm, l + 1)
            for m in range(2):
                nc.scalar.activation(h_hi[:, RET_HEADS + m, :], acc((2, 5)[m], TOK), ACT.Copy,
                                     scale=par[:, C_PS + 2 * l + m:C_PS + 2 * l + m + 1]).then_inc(pool_hi, 1)
            for h in range(RET_HEADS):
                n = RET_HEADS * l + h
                act.wait_ge(ret_xc, n + 1)
                if h >= 2:
                    act.wait_ge(ret_var, n - 1)
                nc.scalar.activation(sqh[:, h % 2, :], osb[:, h, :], ACT.Square).then_inc(ret_sq, 1)
            act.wait_ge(ret_var, RET_HEADS * (l + 1))
            nc.scalar.activation(std4[0:RET_HEADS, :], ps[0:RET_HEADS, 3, 0:TOK], ACT.Sqrt,
                                 bias=eps[0:RET_HEADS, 0:1]).then_inc(ret_std, 1)
            squares(by_name[f"mixo{l}"])

        start()
        ffn(0)
        layer_norm("out0")
        recurrent()
        layer_norm("rg_out")
        ffn(1)
        layer_norm("out1")
        keys_values()
        ffn(2)
        layer_norm("out2")
        attention()
        layer_norm("o")
        ffn(3)
        layer_norm("out3")
        layer_norm("emb")
        for l in range(LAYERS_2):
            hybrid(l)
            layer_norm(f"mixo{l}")
            ffn(4 + l)
            layer_norm(f"out{4 + l}")

    @block.vector
    def _(dve):
        own = [0]

        def link(ins):
            own[0] += 1
            ins.then_inc(dve_step, 1)
            dve.wait_ge(dve_step, own[0])

        V = nc.vector
        f = lambda ap: ap.bitcast(fp32)

        def rest_of_chunk(n, slot, rnd, cols):
            dve.wait_ge(w_hi_done, n + 1)
            V.tensor_tensor(wlo[slot][:, 0:cols], raw[slot][:, 0:cols], f(whi[slot][:, 0:cols]),
                            ALU.subtract).then_inc(w_lo_done, 1)

        def rest_ahead(st, i, j):
            if st.name in behind_norm and isinstance(i, int) and i + j == 0:
                return
            a = ahead(st, i, j)
            if a:
                rest_of_chunk(*a)

        def log1p(e, s, s2, p):
            link(V.tensor_scalar(s, e, 2.0, None, ALU.add))
            link(V.reciprocal(s, s))
            link(V.tensor_tensor(s, s, e, ALU.mult))
            link(V.tensor_tensor(s2, s, s, ALU.mult))
            link(V.tensor_scalar(p, s2, 1.0 / 17, None, ALU.mult))
            for odd in (15, 13, 11, 9, 7, 5, 3):
                link(V.scalar_tensor_tensor(p, p, 1.0 / odd, s2, ALU.add, ALU.mult))

        def start():
            link(V.memset(eps[:, :], LN_EPS))
            dve.sem_inc(acc_free, SLOTS)
            rest_of_chunk(0, 0, 0, stages[0].cols)
            for k in range(KD):
                dve.wait_ge(x_hi_done, k + 1)
                V.tensor_tensor(x_lo[:, k, META:TOK], r[:, k, META:TOK], f(x_hi[:, k, META:TOK]),
                                ALU.subtract).then_inc(x_ready, 1)
                if k == 1:
                    rest_of_chunk(1, 1, 0, stages[0].cols)

        def parameters():
            dve.wait_ge(ser_e, 1)
            s, s2, p = lser[:, 2, :], lser[:, 3, :], lser[:, 4, :]
            log1p(lser[:, 1, :], s, s2, p)
            link(V.scalar_tensor_tensor(s, p, 1.0, s, ALU.add, ALU.mult))
            link(V.tensor_scalar(s2, par[:, C_LAM:C_LAM + KR], -1.0, 0.0, ALU.mult, ALU.max))
            link(V.scalar_tensor_tensor(s, s, 2.0, s2, ALU.mult, ALU.add))
            link(V.tensor_scalar(nspc[:, :], s, -8.0, None, ALU.mult))
            V.tensor_scalar(spc[:, :], s, 8.0, None, ALU.mult).then_inc(spc_done, 1)
            dve.sem_inc(par_done, 1)

        def ffn(fn):
            st = by_name[f"in{fn}"]
            T = tokens[st.name]
            h0 = h_base[fn]

            def step(i, j):
                rest_ahead(st, i, j)
                if j % 2:
                    b = j // 2
                    p = 2 * i + b
                    dve.wait_ge(chunk_used, SLOTS * i + (st.n0 + j + 1))
                    dve.wait_ge(gate_done, 2 * i + (KF * fn + b + 1))
                    V.tensor_tensor(prod[:, b, 0:T], sgate[:, b, 0:T], acc(j, T), ALU.mult).then_inc(acc_free, 1)
                    dve.wait_ge(acc_free, 2 * i + (st.u0 + b + 1))
                    V.tensor_copy(h_hi[:, p, 0:T], prod[:, b, 0:T]).then_inc(h_hi_done, 1)
                    dve.wait_ge(h_hi_done, 2 * i + (h0 + b + 1))
                    V.tensor_tensor(h_lo[:, p, 0:T], prod[:, b, 0:T], f(h_hi[:, p, 0:T]),
                                    ALU.subtract).then_inc(h_ready, 1)

            steps(dve, st.chunks, step, start=1)
            if fn == 0:
                parameters()
            so = by_name[f"out{fn}"]
            new_sums(so)

            def out_step(i, j):
                rest_ahead(so, i, j)
                if j % 2:
                    add_tile(so, 2 * i, j // 2, j // 2, SLOTS * i + (so.n0 + j + 1), 0.5 if fn < 4 else 1.0)

            steps(dve, so.chunks, out_step, start=1)

        def new_sums(st):
            dve.wait_ge(ax_done, KD * (x_of[st.name] + 1))
            link(V.memset(sums[:, :, :], 0.0))

        def add_tile(st, i, j, bank, chunks_used, scale):
            T = tokens[st.name]
            t = slice(tok0(T), TOK)
            m = i + j
            first = isinstance(i, int) and m == 0
            last = isinstance(i, int) and m == KD - 1

            def less_shift(tile, signal):
                return V.scalar_tensor_tensor(tile, acc(7, T), float(-KD), tile, ALU.mult, ALU.add).then_inc(signal, 1)

            def add_square(late):
                dve.wait_ge(sq_done, i + (KD * norm_no[st.name] + j - late + 1))
                return V.tensor_tensor(sums[:, 1, t], sums[:, 1, t], sq[:, i + (j - late), t], ALU.add)

            if isinstance(i, int) and m == 1:
                dve.wait_ge(shift_done, norm_no[st.name] + 1)
                less_shift(r[:, 0, t], shifted)
                dve.wait_ge(shifted, shifts_before(st) + 1)
                V.tensor_tensor(sums[:, 0, t], sums[:, 0, t], r[:, 0, t], ALU.add)
            if not first:
                less_shift(ax[:, m, t], ax_shifted)
                dve.wait_ge(ax_shifted, i + ((KD - 1) * n_sums[st.name] + j))
            if last:
                link(add_square(2))
                add_square(1).then_inc(sums_done, 1)
            elif not first and not (isinstance(i, int) and m == 1):
                add_square(2)
            if last and st.next:
                rest_of_chunk(*ahead(st.next, 0, 0))
            dve.wait_ge(chunk_used, chunks_used)
            V.scalar_tensor_tensor(r[:, m, t], acc(bank, T), scale, ax[:, m, t], ALU.mult, ALU.add).then_inc(acc_free, 1)
            if not first and not last:
                dve.wait_ge(acc_free, i + (st.u0 + j + 1))
                V.tensor_tensor(sums[:, 0, t], sums[:, 0, t], r[:, m, t], ALU.add)

        def add_to_ax(st):
            new_sums(st)

            def step(i, j):
                rest_ahead(st, i, j)
                add_tile(st, SLOTS * i, j, j, SLOTS * i + (st.n0 + j + 1), 1.0)

            steps(dve, st.chunks, step)

        def layer_norm(name):
            n = norm_no[name]
            _, T, kind = norms[n]
            t = slice(tok0(T), TOK)
            nt = len(token_starts(T))

            def centre(k):
                if name == "emb":
                    dve.wait_ge(sq_done, KD * n + k + 2)
                mean = acc(4, T).unsqueeze(1).broadcast_to([P, 2, T])
                V.tensor_tensor(r[:, k:k + 2, t], r[:, k:k + 2, t], mean, ALU.subtract).then_inc(xc_done, 1)

            if name == "emb":
                dve.wait_ge(shift_done, n + 1)
                for k in range(KD):
                    dve.wait_ge(y_done, k + 1)
                    V.scalar_tensor_tensor(r[:, k, :], acc(7, T), float(-KD), r[:, k, :], ALU.mult, ALU.add).then_inc(shifted, 1)
            dve.wait_ge(mean_done, n + 1)
            centre(0)
            dve.wait_ge(msq_done, n + 1)
            V.tensor_tensor(var_t[:, 0:nt], ps[:, 5, 4:4 + nt], msq[:, 0:nt], ALU.subtract).then_inc(var_ready, 1)
            dve.wait_ge(std_done, n + 1)
            V.reciprocal(rstd_t[:, 0:nt], std_t[:, 0:nt]).then_inc(rstd_done, 1)
            centre(2)
            centre(4)
            dve.wait_ge(spread, n + 1)
            dve.wait_ge(xc_done, 4 * n + 3)
            v = version.get(name, 0)
            for k in range(KD + 1):
                if k == 2:
                    centre(6)
                if k == 6:
                    dve.wait_ge(xc_done, 4 * n + 4)
                if k < KD:
                    V.scalar_tensor_tensor(r[:, k, t], r[:, k, t], par[:, C_G + KD * n + k:C_G + KD * n + k + 1],
                                           acc(6, T), ALU.mult, ALU.mult).then_inc(xn_done, 1)
                if k and kind == "x":
                    c = C_B + KD * n + k - 1
                    dve.wait_ge(x_hi_done, KD * v + k)
                    V.scalar_tensor_tensor(x_lo[:, k - 1, t], r[:, k - 1, t], par[:, c:c + 1], f(x_hi[:, k - 1, t]),
                                           ALU.add, ALU.subtract).then_inc(x_ready, 1)

        def recurrent():
            st = by_name["rg_u"]
            V.memset(upad[:, :, 0:CONV - 1], 0.0).then_inc(pad_zero, 1)
            for s in range(KR):
                rest_ahead(st, s // SLOTS, s % SLOTS)
                dve.wait_ge(u_raw, s + 1)
                dve.wait_ge(acc_free, st.u0 + s + 1)
                for j in range(CONV - 1):
                    ins = V.scalar_tensor_tensor(uc[:, s, :], upad[:, s % 2, j:j + SEQ],
                                                 par[:, C_CW + j * KR + s:C_CW + j * KR + s + 1], uc[:, s, :], ALU.mult, ALU.add)
                    if j < CONV - 2:
                        link(ins)
                ins.then_inc(conv_done, 1)
                dve.wait_ge(conv_done, s + 1)
                V.tensor_copy(h_hi[:, KR + s, 0:SEQ], uc[:, s, :]).then_inc(u_hi_done, 1)
                dve.wait_ge(u_hi_done, s + 1)
                V.tensor_tensor(h_lo[:, KR + s, 0:SEQ], uc[:, s, :], f(h_hi[:, KR + s, 0:SEQ]),
                                ALU.subtract).then_inc(u_ready, 1)
            sg = by_name["rg_gate"]
            for b in range(GATE_BLOCKS):
                rest_ahead(sg, b // SLOTS, b % SLOTS)
                dve.wait_ge(acc_free, sg.u0 + b + 1)
                c = slice(2 * b, 2 * b + 2)
                V.tensor_tensor(uc[:, c, :], uc[:, c, :], ybr[:, c, :], ALU.mult).then_inc(iu_done, 1)
            sy = by_name["rg_y"]
            for s in range(KR):
                rest_ahead(sy, s // SLOTS, s % SLOTS)
                dve.wait_ge(dec_done, s + 1)
                link(V.tensor_tensor(a2[:, s % 2, :], dec[:, s, :], dec[:, s, :], ALU.mult))
                V.scalar_tensor_tensor(tnh[:, s, :], a2[:, s % 2, :], 1.0, tnh[:, s, :], ALU.add, ALU.mult).then_inc(v_arg, 1)
            for half in range(2):
                c = slice(5 * half, 5 * half + 5)
                dve.wait_ge(v_root, half + 1)
                link(V.tensor_tensor(uc[:, c, :], uc[:, c, :], tnh[:, c, :], ALU.mult))
                for s in range(5 * half, 5 * half + 5):
                    V.tensor_tensor_scan(tnh[:, s, :], dec[:, s, :], uc[:, s, :], 0.0, ALU.mult, ALU.add).then_inc(dve_step, 1)
                    own[0] += 1
                dve.wait_ge(dve_step, own[0])
                dve.wait_ge(gelu_done, half + 1)
                link(V.tensor_tensor(dec[:, c, :], tnh[:, c, :], ybr[:, c, :], ALU.mult))
                for s in range(5 * half, 5 * half + 5):
                    V.tensor_copy(h_hi[:, s, 0:SEQ], dec[:, s, :]).then_inc(h_hi_done, 1)
                for s in range(5 * half, 5 * half + 5):
                    dve.wait_ge(h_hi_done, KF + s + 1)
                    V.tensor_tensor(h_lo[:, s, 0:SEQ], dec[:, s, :], f(h_hi[:, s, 0:SEQ]), ALU.subtract).then_inc(h_ready, 1)
            add_to_ax(by_name["rg_out"])

        def keys_values():
            st = by_name["kv"]
            steps(dve, st.chunks, lambda i, j: rest_ahead(st, i, j), start=1)

        def attention():
            st = by_name["q"]

            def rest(s):
                rest_ahead(st, s // SLOTS, s % SLOTS)

            def bias_max(a):
                slope = float(2.0 ** (-8.0 * (a + 1) / HEADS))
                b = a % 2
                dve.wait_ge(scored, a + 1)
                if a >= 2:
                    dve.wait_ge(pT_done, a - 1)
                V.scalar_tensor_tensor(s_at[:, b, :, :], dist[:, :, :], slope, ps[:, 2:2 + GROUPS, 0:SCORES],
                                       ALU.mult, ALU.add).then_inc(biased, 1)
                dve.wait_ge(biased, a + 1)
                V.tensor_reduce(nmax[:, b, 0:1], s_at[:, b, :, 0:P], AX.XY, ALU.max, negate=True)
                V.tensor_reduce(nmax[:, b, 1:2], s_at[:, b, :, P:], AX.XY, ALU.max, negate=True).then_inc(nmax_done, 1)

            def sum_groups(a):
                b = a % 2
                dve.wait_ge(probs, a + 1)
                V.reciprocal(rden[:, b, :], den[:, b, :])
                s = s_at[:, b, 0, :]
                link(V.tensor_tensor(s, s, s_at[:, b, 1, :], ALU.add))
                link(V.tensor_tensor(s, s, s_at[:, b, 2, :], ALU.add))
                V.tensor_scalar(s_at[:, b, 0, 0:P], s_at[:, b, 0, 0:P], rden[:, b, 0:1], None, ALU.mult)
                V.tensor_scalar(s_at[:, b, 0, P:], s_at[:, b, 0, P:], rden[:, b, 1:2], None, ALU.mult).then_inc(probs_ready, 1)

            def rest_of_output(hp):
                dve.wait_ge(at_hi, hp + 1)
                V.tensor_tensor(h_lo[:, hp, 0:SEQ], acc(6 + hp % 2, SEQ), f(h_hi[:, hp, 0:SEQ]), ALU.subtract).then_inc(at_ready, 1)

            dve.wait_ge(bias_landed, 16)
            for hp in range(PAIRS + 2):
                a, b = 2 * hp - 2, 2 * hp - 1
                if 1 <= hp <= PAIRS:
                    bias_max(a)
                    rest(3 * hp - 1)
                    sum_groups(a)
                if hp < PAIRS:
                    rest(3 * hp)
                if 1 <= hp <= PAIRS:
                    bias_max(b)
                if hp >= 2:
                    rest_of_output(hp - 2)
                if hp < PAIRS:
                    rest(3 * hp + 1)
                if 1 <= hp <= PAIRS:
                    sum_groups(b)
            add_to_ax(by_name["o"])

        def hybrid(l):
            st = by_name[f"mix{l}"]
            f0 = FOX_HEADS * l
            lr = slice(LOGIT_ROW, LOGIT_ROW + FOX_HEADS)
            k2 = lambda c, n: con2[:, c:c + n]

            def rest(s):
                rest_ahead(st, s // SLOTS, s % SLOTS)

            def cumulative_logits():
                e, s, s2, p = sgate[lr, 1, :], prod[lr, 0, :], prod[lr, 1, :], frow[lr, 0, :]
                dve.wait_ge(fe_done, l + 1)
                log1p(e, s, s2, p)
                link(V.scalar_tensor_tensor(s, p, 1.0, s, ALU.add, ALU.mult))
                link(V.tensor_scalar(s2, sgate[lr, 0, :], 0.0, None, ALU.min))
                link(V.scalar_tensor_tensor(s, s, -2.0, s2, ALU.mult, ALU.add))
                V.tensor_tensor_scan(frow[lr, 1, :], con2[lr, B_ONE:B_ONE + TOK], s, 0.0, ALU.mult, ALU.add).then_inc(c_done, 1)

            def mask_max(h):
                b = h % 2
                n = HEADS + f0 + h
                dve.wait_ge(scored, n + 1)
                if h >= 2:
                    dve.wait_ge(pT_done, n - 1)
                V.tensor_tensor(s_fox[:, b, 0:3 * P], ps[:, 2, 0:3 * P], k2(B_MASK, 3 * P), ALU.add)
                V.tensor_tensor(s_fox[0:META, b, 3 * P:], ps[0:META, 3, 0:TOK],
                                con2[0:META, B_MASK + 3 * P:B_MASK + FOX_SCORES], ALU.add).then_inc(biased, 1)
                dve.wait_ge(biased, n + 1)
                V.tensor_reduce(nmax_f[:, b, 0:1], s_fox[:, b, 0:P], AX.X, ALU.max, negate=True)
                V.tensor_reduce(nmax_f[:, b, 1:2], s_fox[:, b, P:3 * P], AX.X, ALU.max, negate=True)
                V.tensor_reduce(nmax_f[0:META, b, 2:3], s_fox[0:META, b, 3 * P:], AX.X, ALU.max, negate=True).then_inc(nmax_done, 1)

            def normalise(h):
                b = h % 2
                dve.wait_ge(probs, HEADS + f0 + h + 1)
                V.reciprocal(rden_f[:, b, 0:2], den_f[:, b, 0:2])
                link(V.reciprocal(rden_f[0:META, b, 2:3], den_f[0:META, b, 2:3]))
                for q, (c, n) in enumerate(((0, P), (P, 2 * P), (3 * P, TOK))):
                    m = P if q < 2 else META
                    s = s_fox[0:m, b, c:c + n]
                    ins = V.tensor_scalar(s, s, rden_f[0:m, b, q:q + 1], None, ALU.mult)
                ins.then_inc(probs_ready, 1)

            def rest_of_output(hp):
                dve.wait_ge(at_hi, PAIRS + 3 * l + hp + 1)
                k = RET_HEADS + 2 + hp
                V.tensor_tensor(h_lo[:, k, :], acc(5, TOK), f(h_hi[:, k, :]), ALU.subtract).then_inc(at_ready, 1)

            def rotate(which):
                x1, x2 = rot_in[:, 2 * which, :], rot_in[:, 2 * which + 1, :]
                cos, sin = k2(B_COS, TOK), k2(B_SIN, TOK)
                dve.wait_ge(acc_free, st.u0 + ROT0 + 2 * which + 2)
                for half, (p, q, op) in enumerate(((cos, sin, ALU.subtract), (sin, cos, ALU.add))):
                    V.tensor_tensor(rtmp[:, 0, :], x1, p, ALU.mult)
                    link(V.tensor_tensor(rtmp[:, 1, :], x2, q, ALU.mult))
                    ins = V.tensor_tensor(rot[:, 2 * which + half, :], rtmp[:, 0, :], rtmp[:, 1, :], op)
                    ins.then_inc(rot_done, 1)
                    dve.wait_ge(rot_done, 4 * l + 2 * which + half + 1)

            def pool():
                dve.wait_ge(acc_free, st.u0 + st.units)
                end = POOL_PAD + TOK
                back = lambda a, w, m, d: a[:, m, w - 1 - d:end - d]
                both = slice(0, 2)
                link(V.tensor_tensor(w_a[:, both, 1:end], up[:, both, 1:end], up[:, both, 0:end - 1], ALU.add))
                link(V.tensor_tensor(w_b[:, both, 3:end], w_a[:, both, 3:end], w_a[:, both, 1:end - 2], ALU.add))
                link(V.tensor_tensor(w_a[:, 1, 7:end], w_b[:, 1, 7:end], w_b[:, 1, 3:end - 4], ALU.add))
                link(V.tensor_tensor(w_b[:, 1, 15:end], w_a[:, 1, 15:end], w_a[:, 1, 7:end - 8], ALU.add))
                tok = slice(POOL_PAD, end)
                half = P // 2
                for m in range(2):
                    V.tensor_copy(w_b[0:half, m, tok], w_a[0:half, m, tok]).then_inc(dve_step, 1)
                    own[0] += 1
                dve.wait_ge(dve_step, own[0])
                cnt = con2[:, B_CNT:B_CNT + 2 * TOK].rearrange("p (m t) -> p m t", m=2)
                link(V.tensor_tensor(w_b[:, :, tok], w_b[:, :, tok], cnt, ALU.mult))
                V.tensor_tensor(w_b[:, :, tok], w_b[:, :, tok], up[:, :, tok], ALU.subtract).then_inc(pool_done, 1)

            rest(0)
            cumulative_logits()
            for s in range(1, ROT0):
                rest(s)
            V.memset(up[:, :, 0:POOL_PAD], 0.0).then_inc(up_zero, 1)
            for h in range(FOX_HEADS):
                mask_max(h)
                rest(ROT0 + 2 * h)
                normalise(h)
                if h >= 2 and h % 2 == 0:
                    rest_of_output(h // 2 - 1)
                rest(ROT0 + 2 * h + 1)
                if h in (2, 3):
                    rotate(h - 2)
            rest(WIN_TILES - 1)
            rest_of_output(2)

            def decay(h):
                n = RET_HEADS * l + h
                dve.wait_ge(ret_s, n + 1)
                if h >= 2:
                    dve.wait_ge(ret_o, n - 1)
                c = B_DEC + h * KEYS_ALL
                V.tensor_tensor(s_fox[:, h % 2, 0:KEY_AT[2]], ps[:, 3 + h % 2, 0:KEY_AT[2]], k2(c, KEY_AT[2]), ALU.mult)
                V.tensor_tensor(s_fox[0:META, h % 2, KEY_AT[2]:KEYS_ALL], ps[0:META, 3 + h % 2, KEY_AT[2]:KEYS_ALL],
                                con2[0:META, c + KEY_AT[2]:c + KEYS_ALL], ALU.mult).then_inc(ret_d, 1)

            for h in range(RET_HEADS):
                decay(h)
            pool()
            out_bank = (0, 1, 6, 7)
            for h in range(RET_HEADS):
                dve.wait_ge(ret_mean, RET_HEADS * l + h + 1)
                V.tensor_tensor(osb[:, h, :], osb[:, h, :], acc(out_bank[h], TOK), ALU.subtract).then_inc(ret_xc, 1)
            for m in range(2):
                dve.wait_ge(pool_hi, 2 * l + m + 1)
                V.scalar_tensor_tensor(h_lo[:, RET_HEADS + m, :], acc((2, 5)[m], TOK),
                                       par[:, C_PS + 2 * l + m:C_PS + 2 * l + m + 1], f(h_hi[:, RET_HEADS + m, :]),
                                       ALU.mult, ALU.subtract).then_inc(pool_ready, 1)
            dve.wait_ge(ret_std, l + 1)
            V.reciprocal(std4[0:RET_HEADS, :], std4[0:RET_HEADS, :]).then_inc(ret_rstd, 1)
            dve.wait_ge(silu2, l + 1)
            for h in range(RET_HEADS):
                n = RET_HEADS * l + h
                dve.wait_ge(ret_bc, n + 1)
                c = C_GN + n
                link(V.scalar_tensor_tensor(osb[:, h, :], osb[:, h, :], par[:, c:c + 1], acc(out_bank[h], TOK), ALU.mult, ALU.mult))
                link(V.tensor_tensor(osb[:, h, :], osb[:, h, :], gsb[:, h, :], ALU.mult))
                V.tensor_copy(h_hi[:, h, :], osb[:, h, :]).then_inc(ret_hi, 1)
                dve.wait_ge(ret_hi, n + 1)
                V.tensor_tensor(h_lo[:, h, :], osb[:, h, :], f(h_hi[:, h, :]), ALU.subtract).then_inc(ret_ready, 1)
            add_to_ax(by_name[f"mixo{l}"])

        start()
        ffn(0)
        layer_norm("out0")
        recurrent()
        layer_norm("rg_out")
        ffn(1)
        layer_norm("out1")
        keys_values()
        ffn(2)
        layer_norm("out2")
        attention()
        layer_norm("o")
        ffn(3)
        layer_norm("out3")
        layer_norm("emb")
        for l in range(LAYERS_2):
            hybrid(l)
            layer_norm(f"mixo{l}")
            ffn(4 + l)
            layer_norm(f"out{4 + l}")

    block_guard.__exit__(None, None, None)
    for s in reversed(sems):
        s.__exit__(None, None, None)
    psum.__exit__(None, None, None)
    slab.__exit__(None, None, None)


def constants():
    con = np.zeros((P, 3, P), np.float32)
    con[:, 0] = np.eye(P)
    con[:, 1] = 1.0 / D
    con[:RET_DV, 2] = 1.0 / RET_DV

    far = -1e33
    t = np.arange(SEQ)
    dist = t[:, None] - t[None, :]
    bias = np.full((P, GROUPS, SCORES), far, np.float32)
    for g, (window, dilation) in enumerate(DILATIONS):
        seen = (dist >= 0) & (dist <= window) & (dist % dilation == 0)
        b = np.where(seen, -dist, far)
        bias[:, g, :P] = b[:P, :P]
        bias[:, g, P:] = b[P:]

    c2 = np.zeros((P, N_B), np.float32)
    for h in range(RET_HEADS):
        c2[h, B_EXP + h * P:B_EXP + (h + 1) * P] = 1.0
        c2[:RET_DV, B_HEAD + RET_HEADS * h + h] = 1.0 / RET_DV
    for h in range(FOX_HEADS):
        c2[LOGIT_ROW + h, B_SEL + h * P:B_SEL + (h + 1) * P] = -1.0
    c2[:, B_ONE:B_ONE + TOK] = 1.0
    pos = np.arange(TOK, dtype=np.float32)
    freq = np.float32(10000.0) ** (-np.arange(HALF_DK, dtype=np.float32) / np.float32(HALF_DK))
    ang = (freq[:, None] * pos[None, :]).astype(np.float32)
    for h in range(RET_HEADS):
        c2[32 * h:32 * h + HALF_DK, B_COS:B_COS + TOK] = np.cos(ang)
        c2[32 * h:32 * h + HALF_DK, B_SIN:B_SIN + TOK] = np.sin(ang)
        log_gamma = np.log(1.0 - 2.0 ** (-5.0 - h))
        for k in range(3):
            keys = np.arange(k * P, min((k + 1) * P, TOK))
            away = np.arange(k * P, TOK)[None, :] - keys[:, None]
            decay = np.where(away >= 0, np.exp(log_gamma * np.maximum(away, 0)), 0.0) * RET_DK ** -0.5
            at = B_DEC + h * KEYS_ALL + KEY_AT[k]
            c2[:len(keys), at:at + KEY_COLS[k]] = decay
    below = np.where(np.arange(P)[:, None] >= np.arange(P)[None, :], 0.0, -1e30)
    c2[:, B_MASK:B_MASK + P] = below
    c2[:, B_MASK + 2 * P:B_MASK + 3 * P] = below
    c2[:META, B_MASK + 5 * P:B_MASK + 5 * P + META] = below[:META, :META]
    for n, w in enumerate(POOL_WINDOWS):
        rows = slice(64 * (n % 2), 64 * (n % 2) + 64)
        c2[rows, B_CNT + (n // 2) * TOK:B_CNT + (n // 2 + 1) * TOK] = 1.0 / np.minimum(np.arange(TOK) + 1, w)
    return con.reshape(P, 3 * P), bias, c2


def chunks(w, halves=1):
    K, M = w.shape
    w = w.reshape(halves, K // halves // P, P, M // P, P).transpose(3, 0, 2, 1, 4)
    return np.ascontiguousarray(w.reshape(M // P * halves, P, K // halves))


def paired(gate, up):
    K = gate.shape[0]
    return np.stack([gate.reshape(K, KF, P), up.reshape(K, KF, P)], 2).reshape(K, 2 * FF)


def hybrid_columns(w):
    parts = np.split(w, np.cumsum([192, 192, 384, 384, 256, 384, 384, 384]), axis=1)
    q, k, v, g, u, qf, kf, vf, logits = parts

    def halves(a):
        a = a.reshape(D, RET_HEADS, 2, HALF_DK)
        t = np.zeros((D, 2, RET_HEADS, 32), w.dtype)
        t[..., :HALF_DK] = a.transpose(0, 2, 1, 3)
        return t.reshape(D, 2 * P)

    def padded(a):
        t = np.zeros((D, RET_HEADS, P), w.dtype)
        t[..., :RET_DV] = a.reshape(D, RET_HEADS, RET_DV)
        return t

    g = padded(g)
    g[:, 0, LOGIT_ROW:LOGIT_ROW + FOX_HEADS] = logits
    g = g.reshape(D, RET_HEADS * P)
    return np.concatenate([g[:, :P], qf, kf, vf, halves(q), halves(k), padded(v).reshape(D, -1), g[:, P:], u], axis=1)


def hybrid_rows(w):
    t = np.zeros((RET_HEADS, P, D), w.dtype)
    t[:, :RET_DV] = w[:RET_HEADS * RET_DV].reshape(RET_HEADS, RET_DV, D)
    return np.concatenate([t.reshape(-1, D), w[RET_HEADS * RET_DV:]], axis=0)


def tiles(v):
    return v.reshape(-1, P).T


def kernel(**inputs):
    import concourse.bacc as bacc
    from concourse.bass_utils import run_bass_kernel_spmd

    a = {k: np.asarray(v) for k, v in inputs.items()}
    f32 = np.float32
    ffn_in = [paired(*np.split(a["ffn_w_in"][l, i], 2, axis=1)) for l in range(2) for i in range(2)]
    ffn_in += [paired(a["w_ffn1_2"][l], a["w_ffn3_2"][l]) for l in range(LAYERS_2)]
    ffn_out = [a["ffn_w_out"][l, i] for l in range(2) for i in range(2)] + [a["w_ffn2_2"][l] for l in range(LAYERS_2)]
    weights = {}
    for f in range(6):
        weights[f"in{f}"] = chunks(ffn_in[f])
        weights[f"out{f}"] = chunks(ffn_out[f], 2)
    y_cols, u_cols = np.split(a["rg_w_in"][0], 2, axis=1)
    weights["rg_u"], weights["rg_y"] = chunks(u_cols), chunks(y_cols)
    gate = a["rg_gate_w"][0].reshape(2, GATE_BLOCKS, 2, P, 2, P)
    weights["rg_gate"] = np.ascontiguousarray(gate.transpose(1, 3, 0, 4, 2, 5).reshape(GATE_BLOCKS, P, 8 * P))
    weights["rg_out"] = chunks(a["rg_w_out"][0])
    weights["kv"] = chunks(a["kv_w"])
    q = a["attn_w_q"][0].reshape(D, GROUPS, PAIRS, P).transpose(0, 2, 1, 3)
    weights["q"] = chunks(q.reshape(D, GROUPS * PAIRS * P))
    weights["o"] = chunks(a["attn_w_o"][0])
    for l in range(LAYERS_2):
        weights[f"mix{l}"] = chunks(hybrid_columns(a["w_in_2"][l]))
        weights[f"mixo{l}"] = chunks(hybrid_rows(a["w_out_2"][l]))

    gains = [a["ln_g"].reshape(-1), a["ln_emb_g_2"]]
    shifts = [a["ln_b"].reshape(-1), a["ln_emb_b_2"]]
    for l in range(LAYERS_2):
        gains += [a["ln1_g_2"][l], a["ln2_g_2"][l]]
        shifts += [a["ln1_b_2"][l], a["ln2_b_2"][l]]
    par = np.zeros((P, N_PAR), f32)
    par[:, C_G:C_B] = tiles(np.concatenate(gains))
    par[:, C_B:C_CW] = tiles(np.concatenate(shifts))
    par[:, C_CW:C_CB] = tiles(a["rg_conv_w"][0].reshape(-1))
    par[:, C_CB:C_GB] = tiles(a["rg_conv_b"][0])
    par[:, C_GB:C_LAM] = tiles(a["rg_gate_b"][0].reshape(-1))
    par[:, C_LAM:C_GN] = tiles(a["rg_lam"][0])
    par[:RET_DV, C_GN:C_PS] = a["ret_gn_g_2"].reshape(-1, RET_DV).T
    par[:, C_PS:C_BF] = tiles(a["pool_scale_2"].reshape(-1))
    par[LOGIT_ROW:LOGIT_ROW + FOX_HEADS, C_BF:] = a["b_f_2"].T
    poolw = np.zeros((P, LAYERS_2, 2, P), f32)
    for l in range(LAYERS_2):
        for n in range(len(POOL_WINDOWS)):
            s = slice(64 * (n % 2), 64 * (n % 2) + 64)
            poolw[s, l, n // 2, s] = a["pool_w_2"][l, n]
    con, bias, con2 = constants()
    feature_major = lambda v: np.ascontiguousarray(v.reshape(-1, KD, P).transpose(2, 1, 0))
    arrays = {"x": feature_major(a["x"][0]), "meta": feature_major(a["meta_2"]), "par": par, "con": con,
              "bias": bias, "con2": con2, "poolw": poolw}
    arrays.update({f"w_{n}": w for n, w in weights.items()})

    nc = bacc.Bacc("TRN2", target_bir_lowering=False, num_devices=1)
    d = {n: nc.dram_tensor(n, v.shape, mybir.dt.float32, kind="ExternalInput").ap() for n, v in arrays.items()}
    out = nc.dram_tensor("out", (P, KD, SEQ), mybir.dt.float32, kind="ExternalOutput").ap()
    build(nc, d["x"], d["meta"], d["par"], d["con"], d["bias"], d["con2"], d["poolw"],
          {n: d[f"w_{n}"] for n in weights}, out)
    got = run_bass_kernel_spmd(nc, [arrays], core_ids=[0]).results[0]["out"]
    return np.ascontiguousarray(got.transpose(2, 1, 0).reshape(1, SEQ, D))
```

```python
import numpy as np
import concourse.bass as bass
from concourse import mybir

P = 128
D = 1024
KD = D // P
SEQ = 256
META = 16
TOK = SEQ + META
FF = 2816
KF = FF // P
HALF_F = KF // 2
RNN = 1280
KR = RNN // P
GATE_BLOCKS = 5
RG_ORDER = ([("u", m) for m in range(3)] + [x for b in range(3) for x in (("u", 2 * b + 3), ("u", 2 * b + 4), ("gate", b))]
            + [("u", 9), ("gate", 3), ("y", 0), ("gate", 4)] + [("y", m) for m in range(1, KR)])
U_BEHIND = {("u", 2): (0,), ("u", 3): (1,), ("u", 4): (2,), ("u", 5): (3,), ("u", 6): (4, 5), ("u", 7): (6,), ("u", 8): (7,),
            ("u", 9): (8,), ("gate", 3): (9,)}
RG_VECTOR = [("y", m) for m in range(1, 6)]
H_PARTS = ((0, 5), (5, 8), (8, 10))
CONV = 4
HEADS = 16
GROUPS = 3
PAIRS = HEADS // 2
HD = 64
DILATIONS = ((128, 1), (512, 4), (2048, 16))
SCORES = P + SEQ
RET_HEADS, RET_DK, RET_DV = 4, 48, 96
HALF_DK = RET_DK // 2
POOL_WINDOWS = (2, 4, 8, 16)
POOL_PAD = max(POOL_WINDOWS)
FOX_HEADS, FOX_W = 6, 384
LOGIT_ROW = RET_DV
LOGIT_ROWS = 2 * FOX_HEADS
LAYERS_2 = 2
ALPHA = float(4.0 ** 0.25)
LN_EPS = 1e-5
SLOTS = 4
FIRST = 2
AHEAD = 2
CHUNK = HALF_F * P
QT = (112, 96, 64)
QT_AT = (0, 112, 208)
KEY_COLS = tuple(TOK - a for a in QT_AT)
KEY_AT = (0, TOK, TOK + KEY_COLS[1])
KEYS_ALL = sum(KEY_COLS)
FOX_COLS = tuple(a + n for a, n in zip(QT_AT, QT))
FOX_AT = (0, FOX_COLS[0], FOX_COLS[0] + FOX_COLS[1])
FOX_SCORES = sum(FOX_COLS)
MIX_K = RET_HEADS + 2 + 3
WIN_TILES = 22
ROT0, VR0, GATE0, POOL0, FOX0 = 0, 4, 7, 11, 13

N_LN = 11
C_G, C_B = 0, N_LN * KD
C_CW = 2 * N_LN * KD
C_CB = C_CW + CONV * KR
C_GB = C_CB + KR
C_LAM = C_GB + 2 * KR
C_GN = C_LAM + KR
C_PS = C_GN + LAYERS_2 * RET_HEADS
C_BF = C_PS + LAYERS_2 * 2
N_PAR = C_BF + LAYERS_2

B_EXP = 0
B_SEL = B_EXP + RET_HEADS * P
B_ONE = B_SEL + FOX_HEADS * P
B_COS = B_ONE + TOK
B_SIN = B_COS + TOK
B_DEC = B_SIN + TOK
B_MASK = B_DEC + RET_HEADS * KEYS_ALL
B_CNT = B_MASK + FOX_SCORES
B_HEAD = B_CNT + 2 * TOK
B_LO = B_HEAD + RET_HEADS * RET_HEADS
N_B = B_LO + 1


class Stage:

    def __init__(self, name, chunks, tiles, units):
        self.name, self.chunks, self.tiles, self.units = name, chunks, tiles, units
        self.cols = tiles * P
        self.n0 = self.u0 = 0


def plan():
    ffn = lambda f: [Stage(f"in{f}", 2 * KF, KD, KF), Stage(f"out{f}", 2 * KD, HALF_F, KD)]
    s = ffn(0)
    s += [Stage("rg", len(RG_ORDER), KD, len(RG_ORDER)), Stage("rg_out", KD, KR, KD)]
    s += ffn(1) + [Stage("kv", 2 * KD, KD, 2 * KD)] + ffn(2)
    s += [Stage("q", GROUPS * PAIRS, KD, GROUPS * PAIRS), Stage("o", KD, KD, KD)] + ffn(3)
    for l in range(LAYERS_2):
        s += [Stage(f"mix{l}", WIN_TILES, KD, WIN_TILES), Stage(f"mixo{l}", KD, MIX_K, KD)] + ffn(4 + l)
    n, u = 0, SLOTS
    for st in s:
        st.n0, st.u0 = n, u
        n += st.chunks
        u += st.units
    for a, b in zip(s, s[1:]):
        a.next = b
    s[-1].next = None
    return s


def build(nc, x_in, meta_in, par_in, con_in, bias_in, con2_in, poolw_in, weights, out):
    fp32, fp32r = mybir.dt.float32, mybir.dt.float32r
    ALU, ACT = mybir.AluOpType, mybir.ActivationFunctionType
    AX = mybir.AxisListType
    stages = plan()
    by_name = {st.name: st for st in stages}

    first = -(-nc.sbuf_base // 32) * 32
    slab_bytes = nc.sbuf_usable_end - first - 64
    slab = nc.sbuf_tensor("slab", [P, slab_bytes // 4], fp32)
    slab.__enter__()
    cursor = [first]

    def place(name, free, dtype=fp32):
        t = nc.alloc_sbuf_tensor_at(name, [P, *free], dtype, offset=cursor[0])
        cursor[0] += -(-4 * int(np.prod(free)) // 32) * 32
        assert cursor[0] <= first + slab_bytes, name
        return t

    raw = [place(f"raw{i}", [CHUNK]) for i in range(SLOTS)]
    whi = [place(f"whi{i}", [CHUNK], fp32r) for i in range(SLOTS)]
    wlo = [place(f"wlo{i}", [CHUNK], fp32r) for i in range(SLOTS)]
    x_hi = place("x_hi", [KD, TOK], fp32r)
    x_lo = place("x_lo", [KD, TOK], fp32r)
    ax = place("ax", [KD, TOK])
    r_at = cursor[0]
    r = place("r", [KD, TOK])
    sq_at = cursor[0]
    sq = place("sq", [KD, TOK])
    hhi_at = cursor[0]
    h_hi = place("h_hi", [KF, TOK], fp32r)
    hlo_at = cursor[0]
    h_lo = place("h_lo", [KF, TOK], fp32r)
    con = place("con", [3 * P])
    ident, ones_d, ones_head = con[:, 0:P], con[:, P:2 * P], con[:, 2 * P:3 * P]
    par = place("par", [N_PAR])
    ab = place("ab", [N_LN * KD])
    eps = place("eps", [1])
    sums = place("sums", [2, TOK])
    msq = place("msq", [3])
    var_t = place("var_t", [3])
    std_t = place("std_t", [3])
    rstd_t = place("rstd_t", [3])
    spare = place("spare", [1])
    frow = place("frow", [2, TOK])
    sgate = place("sgate", [2, TOK])
    prod = place("prod", [2, TOK])
    spc = place("spc", [KR])
    nspc = place("nspc", [KR])
    lser = place("lser", [5, KR])
    mix_at = cursor[0]

    uc = place("uc", [KR, SEQ])
    dec = place("dec", [KR, SEQ])
    tnh = place("tnh", [KR, SEQ])
    ybr = place("ybr", [KR, SEQ])
    cursor[0] = mix_at
    kT = place("kT", [KD, SEQ])
    v_tok = place("v_tok", [2, D])
    qT = place("qT", [2, GROUPS, SEQ])
    dist = place("dist", [GROUPS, SCORES])
    s_at = place("s_at", [2, GROUPS, SCORES])
    nmax = place("nmax", [2, 2])
    den = place("den", [2, 2])
    rden = place("rden", [2, 2])
    pT = place("pT", [2, SCORES])
    cursor[0] = mix_at
    con2 = place("con2", [N_B])
    poolw = place("poolw", [LAYERS_2, 2, P])
    gsb = place("gsb", [RET_HEADS, TOK])
    qf = place("qf", [3, TOK])
    kf = place("kf", [3, TOK])
    vf_tok = place("vf_tok", [3, FOX_W])
    cursor[0] = sq_at
    upad = place("upad", [2, CONV - 1 + SEQ])
    a2 = place("a2", [KR // 2, SEQ])
    cursor[0] = sq_at
    vr = place("vr", [3, TOK])
    cursor[0] = sq_at
    osb = place("osb", [RET_HEADS, TOK])
    vf = place("vf", [3, TOK])
    cursor[0] = r_at
    up = place("up", [2, POOL_PAD + TOK])
    w_a = place("w_a", [2, POOL_PAD + TOK])
    w_b = place("w_b", [2, POOL_PAD + TOK])
    std4 = place("std4", [TOK])
    cursor[0] = hhi_at + 10 * TOK * 4
    s_fox = place("s_fox", [3, FOX_SCORES])
    pT_fox = place("pT_fox", [2, KEYS_ALL])
    nmax_f = place("nmax_f", [2, 3])
    den_f = place("den_f", [2, 3])
    rden_f = place("rden_f", [2, 3])
    assert cursor[0] <= hlo_at
    cursor[0] = hlo_at + 10 * TOK * 4
    rot_in = place("rot_in", [4, TOK])
    rtmp = place("rtmp", [2, TOK])
    rot = place("rot", [4, TOK])
    sqh = place("sqh", [2, TOK])
    assert cursor[0] <= hlo_at + KF * TOK * 4
    cursor[0] = hlo_at + 10 * TOK * 4
    vr_tok = place("vr_tok", [3, RET_HEADS * RET_DV])
    cursor[0] = hlo_at + 16 * TOK * 4
    sel_r = place("sel_r", [FOX_HEADS * P], fp32r)
    c_parts = place("c_parts", [TOK], fp32r)
    assert cursor[0] <= hlo_at + 20 * TOK * 4

    psum = nc.psum_tensor("psum", [P, 8, 512], fp32)
    ps = psum.__enter__()

    sems = []

    def sem(name):
        s = nc.semaphore(name)
        sems.append(s)
        return s.__enter__()

    x_landed = [sem(f"x_landed{i}") for i in range(2)]
    par_landed = sem("par_landed")
    inputs_in = sem("inputs_in")
    zeros = sem("zeros")
    bias_landed = sem("bias_landed")
    con2_landed = sem("con2_landed")
    raw_landed = [sem(f"raw_landed{i}") for i in range(SLOTS)]
    w_hi_done = sem("w_hi_done")
    w_lo_done = sem("w_lo_done")
    chunk_used = sem("chunk_used")
    acc_free = sem("acc_free")
    x_hi_done = sem("x_hi_done")
    x_ready = sem("x_ready")
    ax_done = sem("ax_done")
    gate_done = sem("gate_done")
    h_hi_done = sem("h_hi_done")
    h_ready = sem("h_ready")
    mean_done = sem("mean_done")
    shift_done = sem("shift_done")
    shifted = sem("shifted")
    ax_shifted = sem("ax_shifted")
    xc_done = sem("xc_done")
    emb_squares = sem("emb_squares")
    sums_done = sem("sums_done")
    stat_done = sem("stat_done")
    msq_done = sem("msq_done")
    sq_done = sem("sq_done")
    var_ready = sem("var_ready")
    std_done = sem("std_done")
    rstd_done = sem("rstd_done")
    spread = sem("spread")
    xn_done = sem("xn_done")
    y_done = sem("y_done")
    out_landed = sem("out_landed")
    dve_step = sem("dve_step")
    act_step = sem("act_step")
    ser_e = sem("ser_e")
    spc_done = sem("spc_done")
    u_raw = sem("u_raw")
    pad_zero = sem("pad_zero")
    conv_done = sem("conv_done")
    u_hi_done = sem("u_hi_done")
    u_ready = sem("u_ready")
    tanh_done = sem("tanh_done")
    iu_done = sem("iu_done")
    dec_done = sem("dec_done")
    a2_done = sem("a2_done")
    v_arg = sem("v_arg")
    v_root = sem("v_root")
    gelu_done = sem("gelu_done")
    rg_prod = sem("rg_prod")
    rg_hi = sem("rg_hi")
    rg_ready = sem("rg_ready")
    vT_done = sem("vT_done")
    v_copied = sem("v_copied")
    scored = sem("scored")
    biased = sem("biased")
    nmax_done = sem("nmax_done")
    probs = sem("probs")
    probs_ready = sem("probs_ready")
    pT_done = sem("pT_done")
    pT_copied = sem("pT_copied")
    pv_done = sem("pv_done")
    at_hi = sem("at_hi")
    at_ready = sem("at_ready")
    fx_done = sem("fx_done")
    fe_done = sem("fe_done")
    c_done = sem("c_done")
    sel_done = sem("sel_done")
    vt2_done = sem("vt2_done")
    vt2_copied = sem("vt2_copied")
    rot_done = sem("rot_done")
    up_zero = sem("up_zero")
    pool_done = sem("pool_done")
    pool_mm = sem("pool_mm")
    pool_hi = sem("pool_hi")
    pool_ready = sem("pool_ready")
    ret_s = sem("ret_s")
    ret_d = sem("ret_d")
    ret_o = sem("ret_o")
    ret_osb = sem("ret_osb")
    ret_mean = sem("ret_mean")
    ret_xc = sem("ret_xc")
    ret_sq = sem("ret_sq")
    ret_var = sem("ret_var")
    ret_std = sem("ret_std")
    ret_rstd = sem("ret_rstd")
    ret_bc = sem("ret_bc")
    silu2 = sem("silu2")
    ret_hi = sem("ret_hi")
    ret_ready = sem("ret_ready")

    block_guard = nc.Block()
    block = block_guard.__enter__()

    def steps(eng, count, body, start=0, done=0):
        full = (count - AHEAD) // SLOTS
        for s in range(SLOTS * done, SLOTS * start):
            body(s // SLOTS, s % SLOTS)
        if full - start > 1:
            with eng.Fori(start, full) as i:
                for j in range(SLOTS):
                    body(i, j)
        else:
            full = start
        for s in range(SLOTS * full, count):
            body(s // SLOTS, s % SLOTS)

    def at(st, i, j):
        return SLOTS * i + (st.n0 + j), (st.n0 + j) % SLOTS, i + (st.n0 + j) // SLOTS

    def ahead(st, i, j):
        cols = st.cols
        if isinstance(i, int) and SLOTS * i + j + AHEAD >= st.chunks:
            if st.next is None:
                return None
            cols = st.next.cols
        return *at(st, i, j + AHEAD), cols

    def early_split(st, i, j):
        return (st.name == "o" or st.name.startswith("mixo")) and isinstance(i, int) and SLOTS * i + j < 2

    norms = [("out0", SEQ, "x"), ("rg_out", SEQ, "x"), ("out1", SEQ, "x"), ("out2", SEQ, "x"),
             ("o", SEQ, "x"), ("out3", SEQ, "y"), ("emb", TOK, "x"), ("mixo0", TOK, "x"),
             ("out4", TOK, "x"), ("mixo1", SEQ, "x"), ("out5", SEQ, "y")]
    norm_no = {name: n for n, (name, _, _) in enumerate(norms)}
    version, versions = {"start": 0}, 1
    for name, _, kind in norms:
        if kind == "x":
            version[name] = versions
            versions += 1
    tok0 = lambda T: TOK - T
    x_of = {}
    now = "start"
    for st in stages:
        x_of[st.name] = version[now]
        if st.name in norm_no:
            now = st.name if st.name in version else "emb"
    tokens = {st.name: SEQ if st.n0 < by_name["mix0"].n0 or st.n0 > by_name["mix1"].n0 else TOK for st in stages}
    h_at = lambda st: META if st.name == "mixo1" else 0
    token_starts = lambda T: [tok0(T) + min(t * P, T - P) for t in range(-(-T // P))]
    two_banks = lambda s: s % 2
    norm_stages = [x[0] for x in norms if x[0] != "emb"]
    behind_norm = {a.next.name for a in stages if a.name in norm_no and a.next}
    acc = lambda bank, T: ps[:, bank, 0:T]
    h_base = [KF * f for f in range(6)]

    @block.sync
    def _(sp):
        def load(st, i, j, first=False):
            n, slot, _ = at(st, i, j)
            if not first:
                sp.wait_ge(w_lo_done, n - SLOTS + 1)
            sp.dma_start(raw[slot][:, 0:st.cols], weights[st.name][SLOTS * i + j]).then_inc(raw_landed[slot], 16)

        for st in stages:
            start = 0
            if st.n0 == 0:
                for j in range(SLOTS):
                    load(st, 0, j, first=True)
                    if j < 2:
                        half = slice(KD // 2 * j, KD // 2 * (j + 1))
                        sp.dma_start(r[:, half, META:TOK], x_in[:, half, :]).then_inc(x_landed[j], 16)
                    if j == 1:
                        sp.dma_start(par[:, :], par_in).then_inc(par_landed, 16)
                sp.dma_start(con[:, :], con_in).then_inc(inputs_in, 16)
                sp.dma_start(r[:, :, 0:META], meta_in).then_inc(inputs_in, 16)
                start = 1
            if st.name == "in1":
                sp.wait_ge(rg_ready, len(H_PARTS))
                sp.dma_start(dist[:, :, :], bias_in).then_inc(bias_landed, 16)
            if st.name == "in3":
                sp.wait_ge(at_ready, PAIRS)
                for j in range(SLOTS):
                    load(st, 0, j)
                    part = slice(N_B * j // SLOTS, N_B * (j + 1) // SLOTS)
                    sp.dma_start(con2[:, part], con2_in[:, part]).then_inc(con2_landed, 16)
                sp.dma_start(poolw[:, :, :, ], poolw_in).then_inc(con2_landed, 16)
                start = 1
            full = st.chunks // SLOTS
            if full - start > 1:
                with sp.Fori(start, full) as i:
                    for j in range(SLOTS):
                        load(st, i, j)
            else:
                full = start
            for s in range(SLOTS * full, st.chunks):
                load(st, s // SLOTS, s % SLOTS)
        for k in range(KD):
            sp.wait_ge(y_done, KD + k + 1)
            sp.dma_start(out[:, k, :], r[:, k, META:TOK]).then_inc(out_landed, 16)
        sp.wait_ge(out_landed, 16 * KD)

    @block.tensor
    def _(pe):
        def products(slot, tile, hi, lo, bank, T, start, stop, rows=P):
            w = slice(tile * P, (tile + 1) * P)
            nc.tensor.matmul(acc(bank, T), whi[slot][0:rows, w], hi, start=start, stop=False)
            nc.tensor.matmul(acc(bank, T), whi[slot][0:rows, w], lo, start=False, stop=False)
            return nc.tensor.matmul(acc(bank, T), wlo[slot][0:rows, w], hi, start=False, stop=stop)

        def x_tile(k, T):
            return x_hi[:, k, tok0(T):TOK], x_lo[:, k, tok0(T):TOK]

        def from_x(st, i, j, bank, behind, arriving=False):
            T = tokens[st.name]
            n, slot, _ = at(st, i, j)
            pe.wait_ge(acc_free, behind)
            pe.wait_ge(w_lo_done, n + 1)
            for k in range(KD):
                if arriving:
                    pe.wait_ge(x_ready, k + 1)
                last = products(slot, k, *x_tile(k, T), bank, T, k == 0, k == KD - 1)
            last.then_inc(chunk_used, 1)

        def first_chunks(st):
            T = tokens[st.name]
            pe.wait_ge(w_lo_done, st.n0 + FIRST)
            for k in range(KD):
                pe.wait_ge(x_ready, KD * x_of[st.name] + k + 1)
                for j in range(FIRST):
                    last = products((st.n0 + j) % SLOTS, k, *x_tile(k, T), j, T, k == 0, k == KD - 1)
                    if k == KD - 1:
                        last.then_inc(chunk_used, 1)

        def all_from_x(st, behind):
            pe.wait_ge(acc_free, st.u0)
            if st.n0:
                first_chunks(st)
            else:
                for j in range(FIRST):
                    from_x(st, 0, j, j, st.u0, arriving=True)
            for j in range(FIRST, SLOTS):
                from_x(st, 0, j, j, behind(0, j))
            steps(pe, st.chunks, lambda i, j: from_x(st, i, j, j, behind(i, j)), start=1, done=1)

        def from_h(st, i, j, tiles, ready=None, begun=None):
            first = isinstance(i, int) and i == 0
            todo = [k for k in range(tiles) if not (begun and first and j < 2 and k in begun)]
            if len(todo) == tiles:
                pe.wait_ge(acc_free, SLOTS * i + (st.u0 + j - 3))
                pe.wait_ge(w_lo_done, at(st, i, j)[0] + 1)
            for n, k in enumerate(todo):
                if ready and j == 0 and first:
                    ready(k)
                last = h_products(st, i, j, k, len(todo) == tiles and n == 0, n == len(todo) - 1)
            last.then_inc(chunk_used, 1)
            shift(st, i, j)

        def h_products(st, i, j, k, start, stop):
            T = tokens[st.name]
            t = slice(h_at(st), h_at(st) + T)
            rows = RET_DV if st.name.startswith("mixo") and k < RET_HEADS else P
            return products(at(st, i, j)[1], k, h_hi[0:rows, k, t], h_lo[0:rows, k, t], j, T, start, stop, rows)

        def begin(st, j, k):
            if k == 0:
                pe.wait_ge(acc_free, st.u0)
                pe.wait_ge(w_lo_done, st.n0 + j + 1)
            h_products(st, 0, j, k, k == 0, False)

        def keep_warm(count):
            for _ in range(count):
                nc.tensor.matmul(acc(7, SEQ), h_hi[:, 0, 0:P], h_hi[:, 0, 0:SEQ], start=True, stop=True)

        def shift(st, i, j):
            if isinstance(i, int) and i == 0 and j == (2 if st.chunks == 2 * KD else 1):
                T = tokens[st.name]
                pe.wait_ge(inputs_in, 32)
                pe.wait_ge(acc_free, st.u0 + 1)
                nc.tensor.matmul(acc(7, T), ones_d, r[:, 0, tok0(T):TOK], start=True, stop=True).then_inc(shift_done, 1)

        def ffn(f):
            st = by_name[f"in{f}"]
            all_from_x(st, lambda i, j: 2 * i + (st.u0 + j // 2 - 1))
            so = by_name[f"out{f}"]
            T = tokens[so.name]

            def half(i, j):
                n, slot, _ = at(so, i, j)
                if j % 2 == 0:
                    pe.wait_ge(acc_free, 2 * i + (so.u0 + j // 2 - 1))
                pe.wait_ge(w_lo_done, n + 1)
                for t in range(HALF_F):
                    k = (j % 2) * HALF_F + t
                    if t == 0 or k >= KF - 2:
                        pe.wait_ge(h_ready, h_base[f] + (HALF_F if k == 0 else KF - 2 if t == 0 else k + 1))
                    last = products(slot, t, h_hi[:, k, 0:T], h_lo[:, k, 0:T], j // 2, T, k == 0, k == KF - 1)
                last.then_inc(chunk_used, 1)
                shift(so, i, j)

            steps(pe, so.chunks, half, start=1)

        def layer_norm(name):
            n = norm_no[name]
            T = norms[n][1]
            t = slice(tok0(T), TOK)
            starts = token_starts(T)
            started = []

            def means(tile, first=False, last=False):
                return nc.tensor.matmul(acc(4, T), ones_d, tile[:, t], start=first, stop=last)

            def token_means(tile, col, last=False):
                for m, c in enumerate(starts):
                    ins = nc.tensor.matmul(ps[:, 5, col + m:col + m + 1], tile[:, c:c + P], ones_d[:, 0:1],
                                           start=not started, stop=last and m == len(starts) - 1, skip_group_check=True)
                    started.append(1)
                return ins

            if name == "emb":
                pe.wait_ge(xc_done, 4 * n)
                for k in range(KD):
                    pe.wait_ge(y_done, k + 1)
                    ins = means(r[:, k, :], k == 0, k == KD - 1)
                ins.then_inc(mean_done, 1)
                pe.wait_ge(emb_squares, 1)
                ins = token_means(sums[:, 1, :], 4, True)
            else:
                pe.wait_ge(sums_done, norm_stages.index(name) + 1)
                means(sums[:, 0, :], first=True)
                token_means(sums[:, 0, :], 0)
                token_means(sums[:, 1, :], 4)
                pe.wait_ge(acc_free, by_name[name].u0 + by_name[name].units)
                means(r[:, KD - 1, :], last=True).then_inc(mean_done, 1)
                token_means(r[:, KD - 1, :], 0)
                pe.wait_ge(sq_done, KD * (n + 1))
                ins = token_means(sq[:, KD - 1, :], 4, True)
            ins.then_inc(stat_done, 1)
            keep_warm(6)
            pe.wait_ge(rstd_done, n + 1)
            for m, c in enumerate(starts):
                ins = nc.tensor.matmul(ps[:, 6, c - starts[0]:c - starts[0] + P], rstd_t[:, m:m + 1].broadcast_to([P, P]),
                                       ident, start=True, stop=True)
            ins.then_inc(spread, 1)
            keep_warm(12)

        def recurrent():
            st, so = by_name["rg"], by_name["rg_out"]
            pe.wait_ge(acc_free, st.u0)
            first_chunks(st)
            dense = [s for s, (kind, _) in enumerate(RG_ORDER) if kind != "gate"]
            for s in range(FIRST, st.chunks):
                kind, b = RG_ORDER[s]
                i, j = s // SLOTS, s % SLOTS
                if kind != "gate":
                    c = dense.index(s)
                    from_x(st, i, j, c % 4, st.u0 + (dense[c - 4] + 1 if c >= 4 else 0))
                    continue
                n, slot, _ = at(st, i, j)
                pe.wait_ge(w_lo_done, n + 1)
                if b:
                    pe.wait_ge(acc_free, st.u0 + RG_ORDER.index(("gate", b - 1)) + 1)
                pe.wait_ge(u_ready, 2 * b + 2)
                for m in range(4):
                    for k in range(2):
                        c = KR + 2 * b + k
                        last = products(slot, 2 * m + k, h_hi[:, c, 0:SEQ], h_lo[:, c, 0:SEQ], 4 + m, SEQ, k == 0, k == 1)
                last.then_inc(chunk_used, 1)

            pe.wait_ge(rg_ready, 1)
            early = range(*H_PARTS[0])
            for j in range(2):
                for k in early:
                    begin(so, j, k)

            def ready(k):
                for n, (first, _) in enumerate(H_PARTS):
                    if k == first:
                        pe.wait_ge(rg_ready, n + 1)

            steps(pe, so.chunks, lambda i, j: from_h(so, i, j, KR, ready=ready, begun=early))

        def keys_values():
            st = by_name["kv"]
            all_from_x(st, lambda i, j: SLOTS * i + (st.u0 + j - 3))
            pe.wait_ge(acc_free, st.u0 + st.units)
            for t in range(2):
                for m in range(KD):
                    last = nc.tensor.transpose(ps[:, 4 + 2 * t + m // 4, (m % 4) * P:(m % 4 + 1) * P],
                                               sq[:, m, t * P:(t + 1) * P], ident)
            last.then_inc(vT_done, 1)

        def attention():
            st = by_name["q"]
            pe.wait_ge(acc_free, st.u0)
            pe.wait_ge(v_copied, 4)

            def query(s):
                if s == 0:
                    first_chunks(st)
                if s >= FIRST:
                    from_x(st, s // SLOTS, s % SLOTS, two_banks(s), st.u0 + s - 1)

            def scores(a):
                hp, rows = a // 2, slice(HD * (a % 2), HD * (a % 2 + 1))
                pe.wait_ge(acc_free, st.u0 + GROUPS * (hp + 1))
                if a:
                    pe.wait_ge(biased, a)
                for g in range(GROUPS):
                    nc.tensor.matmul(ps[:, 2 + g, 0:P], qT[rows, hp % 2, g, 0:P], kT[rows, hp, 0:P], start=True, stop=True)
                    last = nc.tensor.matmul(ps[:, 2 + g, P:SCORES], qT[rows, hp % 2, g, P:SEQ], kT[rows, hp, :],
                                            start=True, stop=True)
                last.then_inc(scored, 1)

            def transposed(a):
                pe.wait_ge(probs_ready, a + 1)
                if a:
                    pe.wait_ge(pT_copied, a)
                for n in range(SCORES // P):
                    last = nc.tensor.transpose(ps[:, 5, n * P:(n + 1) * P], s_at[:, a % 2, 0, n * P:(n + 1) * P], ident)
                last.then_inc(pT_done, 1)

            def values(a):
                hp, e = a // 2, a % 2
                o = ps[HD * e:HD * (e + 1), 6 + hp % 2, :]
                pe.wait_ge(pT_copied, a + 1)
                if hp >= 2:
                    pe.wait_ge(at_ready, hp - 1)
                col = slice(HD * a, HD * (a + 1))
                nc.tensor.matmul(o[:, 0:SEQ], v_tok[:, 0, col], pT[:, a % 2, 0:SEQ], start=True, stop=False)
                nc.tensor.matmul(o[:, P:SEQ], v_tok[:, 1, col], pT[:, a % 2, SEQ:SEQ + P],
                                 start=False, stop=True).then_inc(pv_done, 1)

            so, early = by_name["o"], range(PAIRS - 2)
            for hp in range(PAIRS + 2):
                a, b, behind = 2 * hp - 2, 2 * hp - 1, 2 * hp - 3
                if 1 <= hp <= PAIRS:
                    scores(a)
                if hp < PAIRS:
                    query(3 * hp)
                if hp == PAIRS:
                    pe.wait_ge(at_ready, PAIRS - 2)
                    for k in early:
                        begin(so, 0, k)
                if 1 <= hp <= PAIRS:
                    scores(b)
                if hp >= 2:
                    transposed(behind)
                if hp < PAIRS:
                    query(3 * hp + 1)
                if hp == PAIRS:
                    for k in early[:3]:
                        begin(so, 1, k)
                if hp >= 2:
                    values(behind)
                if 1 <= hp <= PAIRS:
                    transposed(a)
                if hp < PAIRS:
                    query(3 * hp + 2)
                if hp == PAIRS:
                    for k in early[3:]:
                        begin(so, 1, k)
                if 1 <= hp <= PAIRS:
                    values(a)
            steps(pe, so.chunks, lambda i, j: from_h(so, i, j, KD, ready=lambda k: pe.wait_ge(at_ready, k + 1), begun=early))

        def hybrid(l):
            st = by_name[f"mix{l}"]
            pe.wait_ge(acc_free, st.u0)
            pe.wait_ge(con2_landed, 16 * (SLOTS + 1))
            f0 = FOX_HEADS * l

            def tile(s):
                if s == 0:
                    first_chunks(st)
                if s >= FIRST:
                    from_x(st, s // SLOTS, s % SLOTS, two_banks(s), st.u0 + s - 1)

            def token_tiles(t):
                return slice(QT_AT[t], QT_AT[t] + QT[t])

            score_bank = lambda h: 2 if h % 2 == 0 else 6

            def fox_scores(h):
                rows = slice(HD * (h % 2), HD * (h % 2 + 1))
                if h == 0:
                    pe.wait_ge(c_done, l + 1)
                    pe.wait_ge(sel_done, l + 1)
                    pe.wait_ge(acc_free, st.u0 + FOX0 + 6)
                    pe.wait_ge(pool_ready, 2 * l + 2)
                if h == 1:
                    pe.wait_ge(ret_ready, RET_HEADS * (l + 1))
                if h >= 2:
                    pe.wait_ge(biased, HEADS + f0 + h - 1)
                b = score_bank(h)
                for q, (bank, c) in enumerate(((b, 0), (b, FOX_AT[1]), (b + 1, 0))):
                    n = FOX_COLS[q]
                    o = ps[0:QT[q], bank, c:c + n]
                    nc.tensor.matmul(o, qf[rows, h // 2, token_tiles(q)], kf[rows, h // 2, 0:n], start=True, stop=False)
                    parts = slice(LOGIT_ROW, LOGIT_ROW + LOGIT_ROWS)
                    last = nc.tensor.matmul(o, sel_r[parts, h * P:h * P + QT[q]], c_parts[parts, 0:n], start=False, stop=True)
                last.then_inc(scored, 1)

            def fox_transposed(h):
                pe.wait_ge(probs_ready, HEADS + f0 + h + 1)
                pe.wait_ge(pT_copied, HEADS + f0 + h)
                b = h % 3
                for k in range(3):
                    for q in range(k, 3):
                        to, c = KEY_AT[k] + QT_AT[q] - QT_AT[k], FOX_AT[q] + QT_AT[k]
                        last = nc.tensor.transpose(ps[0:QT[k], 4, to:to + QT[q]], s_fox[0:QT[q], b, c:c + QT[k]],
                                                   con[0:QT[q], 0:QT[q]])
                last.then_inc(pT_done, 1)

            def by_values(o, v, col, weights_t):
                for k in range(3):
                    last = nc.tensor.matmul(o[:, QT_AT[k]:TOK], v[0:QT[k], k, col],
                                            weights_t[0:QT[k], KEY_AT[k]:KEY_AT[k] + KEY_COLS[k]], start=k == 0, stop=k == 2)
                return last

            def fox_values(h):
                o = ps[HD * (h % 2):HD * (h % 2 + 1), 5, :]
                pe.wait_ge(pT_copied, HEADS + f0 + h + 1)
                pe.wait_ge(at_ready, PAIRS + 3 * l + h // 2)
                by_values(o, vf_tok, slice(HD * h, HD * (h + 1)), pT_fox[:, h % 2, :]).then_inc(pv_done, 1)

            def transposes(src, tiles, dst_bank):
                for t in range(3):
                    for m in range(tiles):
                        last = nc.tensor.transpose(ps[0:QT[t], dst_bank[t][0], dst_bank[t][1] + m * P:dst_bank[t][1] + (m + 1) * P],
                                                   src[:, m, token_tiles(t)], ident)
                return last

            vT_bank = (5, 6, 7)
            out_bank = (4, 5, 6, 7)

            def ret_scores(h):
                n = RET_HEADS * l + h
                rows = slice(32 * h, 32 * h + 32)
                if h == 0:
                    pe.wait_ge(rot_done, 4 * (l + 1))
                if h >= 2:
                    pe.wait_ge(ret_d, n - 1)
                for k in range(3):
                    o = ps[0:QT[k], 2 + h % 2, KEY_AT[k]:KEY_AT[k] + KEY_COLS[k]]
                    for half in range(2):
                        last = nc.tensor.matmul(o, rot[rows, 2 + half, token_tiles(k)], rot[rows, half, QT_AT[k]:TOK],
                                                start=half == 0, stop=half == 1)
                last.then_inc(ret_s, 1)

            def ret_values(h):
                n = RET_HEADS * l + h
                pe.wait_ge(ret_d, n + 1)
                if h == 0:
                    pe.wait_ge(vt2_copied, 2 * l + 1)
                o = ps[0:RET_DV, out_bank[h], :]
                by_values(o, vr_tok, slice(RET_DV * h, RET_DV * (h + 1)), s_fox[:, h % 2, 0:KEYS_ALL]).then_inc(ret_o, 1)

            def ret_means(h):
                pe.wait_ge(ret_osb, RET_HEADS * l + h + 1)
                nc.tensor.matmul(ps[0:RET_DV, out_bank[h], 0:TOK], ones_head[0:RET_DV, 0:RET_DV], osb[0:RET_DV, h, :],
                                 start=True, stop=True).then_inc(ret_mean, 1)

            def ret_variance(h):
                pe.wait_ge(ret_sq, RET_HEADS * l + h + 1)
                heads = con2[0:RET_DV, B_HEAD + RET_HEADS * h:B_HEAD + RET_HEADS * (h + 1)]
                nc.tensor.matmul(ps[0:RET_HEADS, 2, 0:TOK], heads, sqh[0:RET_DV, h % 2, :],
                                 start=h == 0, stop=h == RET_HEADS - 1).then_inc(ret_var, 1)

            def ret_spread(h):
                pe.wait_ge(ret_rstd, l + 1)
                nc.tensor.matmul(ps[0:RET_DV, out_bank[h], 0:TOK], con2[0:RET_HEADS, B_EXP + h * P:B_EXP + h * P + RET_DV],
                                 std4[0:RET_HEADS, :], start=True, stop=True).then_inc(ret_bc, 1)

            def pool_products():
                pe.wait_ge(pool_done, l + 1)
                pe.wait_ge(ret_std, l + 1)
                for m in range(2):
                    last = nc.tensor.matmul(acc(2 + m, TOK), poolw[:, l, m, :], w_b[:, m, POOL_PAD:], start=True, stop=True)
                last.then_inc(pool_mm, 1)

            for s in range(WIN_TILES):
                tile(s)
                n = s - GATE0
                if n == 0:
                    pe.wait_ge(acc_free, st.u0 + VR0 + 3)
                    transposes(vr, 3, [(b, 0) for b in vT_bank]).then_inc(vt2_done, 1)
                if 1 <= n <= RET_HEADS:
                    ret_scores(n - 1)
                if 2 <= n < 2 + RET_HEADS:
                    ret_values(n - 2)
                if 3 <= n < 3 + RET_HEADS:
                    ret_means(n - 3)
                if 5 <= n < 5 + RET_HEADS:
                    ret_variance(n - 5)
                if n == 11:
                    for h in range(RET_HEADS):
                        ret_spread(h)
                if n == 11:
                    pool_products()
                if n == 13:
                    fox_scores(0)
            so, early = by_name[f"mixo{l}"], range(MIX_K - 1)

            def begin_output(tiles):
                for j, k in tiles:
                    begin(so, j, k)

            own_tiles = [(j, k) for j in range(2) for k in range(MIX_K - 3)]
            fox_scores(1)
            for h in range(FOX_HEADS):
                if 1 <= h < FOX_HEADS - 2:
                    fox_scores(h + 2)
                if h == 0:
                    pe.wait_ge(acc_free, st.u0 + WIN_TILES)
                    transposes(vf, 3, ((4, 0), (5, 0), (1, 0))).then_inc(vt2_done, 1)
                else:
                    fox_values(h - 1)
                if h == 0:
                    fox_scores(2)
                begin_output(own_tiles[2 * h:2 * h + 2])
                if h == 0:
                    pe.wait_ge(vt2_copied, 2 * l + 2)
                fox_transposed(h)
                if h == FOX_HEADS - 2:
                    pe.wait_ge(at_ready, PAIRS + 3 * l + 1)
                    begin_output([(j, MIX_K - 3) for j in range(2)])
            pe.wait_ge(at_ready, PAIRS + 3 * l + 2)
            begin_output([(j, MIX_K - 2) for j in range(2)])
            fox_values(FOX_HEADS - 1)

            ready = lambda k: pe.wait_ge(at_ready, PAIRS + 3 * l + k - (MIX_K - 3) + 1)
            steps(pe, so.chunks, lambda i, j: from_h(so, i, j, MIX_K, ready=ready, begun=early))

        pe.wait_ge(zeros, 1)
        for _ in range(8):
            nc.tensor.matmul(acc(7, SEQ), sums[:, 0, 0:P], sums[:, 0, 0:SEQ], start=True, stop=True)
        ffn(0)
        layer_norm("out0")
        recurrent()
        layer_norm("rg_out")
        ffn(1)
        layer_norm("out1")
        keys_values()
        ffn(2)
        layer_norm("out2")
        attention()
        layer_norm("o")
        ffn(3)
        layer_norm("out3")
        layer_norm("emb")
        for l in range(LAYERS_2):
            hybrid(l)
            layer_norm(f"mixo{l}")
            ffn(4 + l)
            layer_norm(f"out{4 + l}")

    @block.scalar
    def _(act):
        own = [0]

        def link(ins):
            own[0] += 1
            ins.then_inc(act_step, 1)
            act.wait_ge(act_step, own[0])

        def round_chunk(n, slot, rnd, cols, count=1):
            act.wait_ge(raw_landed[slot], 16 * rnd + 16)
            if not isinstance(n, int) or n >= SLOTS:
                act.wait_ge(chunk_used, n - SLOTS + 1)
            nc.scalar.activation(whi[slot][:, 0:cols], raw[slot][:, 0:cols], ACT.Copy).then_inc(w_hi_done, count)

        def next_chunk(st, i, j, count=1):
            a = ahead(st, i, j)
            if a:
                round_chunk(*a, count)

        def round_ahead(st, i, j, count=1):
            if early_split(st, i, j):
                return
            if st.name in behind_norm and isinstance(i, int) and i == 0:
                if j < 2:
                    next_chunk(st, i, j + 2)
                n, t = last_norm
                for k in range((0, 0, 2, 5)[j], (0, 2, 5, KD)[j]):
                    nc.scalar.activation(ax[:, k, t], r[:, k, t], ACT.Identity, scale=ALPHA,
                                         bias=ab[:, KD * n + k:KD * n + k + 1]).then_inc(ax_done, 1)
            else:
                next_chunk(st, i, j, count)

        last_norm = []

        def before_norm(st):
            nc.scalar.activation(spare[:, :], eps[:, :], ACT.Sqrt)
            if st.next:
                round_chunk(*ahead(st.next, 0, 0))

        def start():
            round_chunk(0, 0, 0, stages[0].cols)
            for k in range(KD):
                act.wait_ge(x_landed[k // (KD // 2)], 16)
                nc.scalar.activation(x_hi[:, k, META:TOK], r[:, k, META:TOK], ACT.Copy).then_inc(x_hi_done, 1)
                if k == 1:
                    round_chunk(1, 1, 0, stages[0].cols)

            act.wait_ge(par_landed, 16)
            nc.scalar.activation(ab[:, :], par[:, C_B:C_B + N_LN * KD], ACT.Copy, scale=ALPHA)
            link(nc.scalar.activation(lser[:, 0, :], par[:, C_LAM:C_LAM + KR], ACT.Abs))
            nc.scalar.activation(lser[:, 1, :], lser[:, 0, :], ACT.Exp, scale=-1.0).then_inc(ser_e, 1)

        def first_ax(half):
            for k in range(KD // 2 * half, KD // 2 * (half + 1)):
                nc.scalar.activation(ax[:, k, META:TOK], r[:, k, META:TOK], ACT.Copy, scale=ALPHA).then_inc(ax_done, 1)

        def ffn(f):
            st = by_name[f"in{f}"]
            T = tokens[st.name]

            def step(i, j):
                round_ahead(st, i, j)
                if f == 0 and isinstance(i, int) and i and j % 2:
                    first_ax(j // 2)
                if j % 2 == 0:
                    p = 2 * i + j // 2
                    act.wait_ge(chunk_used, SLOTS * i + (st.n0 + j + 1))
                    act.wait_ge(acc_free, 2 * i + (st.u0 + j // 2 - 1))
                    nc.scalar.activation(sgate[:, j // 2, 0:T], acc(j, T), ACT.Silu).then_inc(gate_done, 1)

            steps(act, st.chunks, step, start=1)
            so = by_name[f"out{f}"]

            def out_step(i, j):
                round_ahead(so, i, j)
                if j % 2:
                    if isinstance(i, int) and SLOTS * i + j == so.chunks - 1:
                        before_norm(so)
                    square(so, 2 * i, j // 2)

            steps(act, so.chunks, out_step, start=1)

        def square(st, i, j):
            T = tokens[st.name]
            t = slice(tok0(T), TOK)
            if isinstance(i, int) and i + j == 0:
                return
            if isinstance(i, int) and i + j == 1:
                act.wait_ge(shifted, norm_stages.index(st.name) + 1)
                nc.scalar.activation(sq[:, 0, t], r[:, 0, t], ACT.Square).then_inc(sq_done, 1)
            act.wait_ge(acc_free, i + (st.u0 + j + 1))
            nc.scalar.activation(sq[:, i + j, t], r[:, i + j, t], ACT.Square).then_inc(sq_done, 1)

        def squares(st):
            def step(i, j):
                m = SLOTS * i + j
                round_ahead(st, i, j)
                if m == st.chunks - 1:
                    before_norm(st)
                if m:
                    square(st, 0, m - 1)

            steps(act, st.chunks, step)
            square(st, 0, st.chunks - 1)

        def layer_norm(name):
            n = norm_no[name]
            _, T, kind = norms[n]
            t = slice(tok0(T), TOK)
            nt = len(token_starts(T))
            if name == "emb":
                for k in range(KD):
                    act.wait_ge(xc_done, 4 * n + k // 2 + 1)
                    nc.scalar.activation(sq[:, k, :], r[:, k, :], ACT.Square).then_inc(sq_done, 1)
            act.wait_ge(stat_done, n + 1)
            if name == "emb":
                nc.scalar.activation(std_t[:, 0:nt], ps[:, 5, 4:4 + nt], ACT.Sqrt, bias=eps[:, 0:1]).then_inc(std_done, 1)
            else:
                ns = norm_stages.index(name)
                nc.scalar.activation(msq[:, 0:nt], ps[:, 5, 0:nt], ACT.Square).then_inc(msq_done, 1)
                act.wait_ge(var_ready, ns + 1)
                nc.scalar.activation(std_t[:, 0:nt], var_t[:, 0:nt], ACT.Sqrt, bias=eps[:, 0:1]).then_inc(std_done, 1)
            nxt = None if name == "out3" else by_name["out3" if name == "emb" else name].next
            if nxt:
                round_chunk(*ahead(nxt, 0, 1))
            b = lambda k: par[:, C_B + KD * n + k:C_B + KD * n + k + 1]
            for k in range(KD):
                act.wait_ge(xn_done, KD * n + k + 1)
                if kind == "x":
                    nc.scalar.activation(x_hi[:, k, t], r[:, k, t], ACT.Identity, bias=b(k)).then_inc(x_hi_done, 1)
                else:
                    nc.scalar.activation(r[:, k, t], r[:, k, t], ACT.Identity, bias=b(k)).then_inc(y_done, 1)
            last_norm[:] = n, t

        def recurrent():
            st = by_name["rg"]
            col = lambda c, k: par[:, c + k:c + k + 1]

            def round_u(m):
                act.wait_ge(conv_done, m + 1)
                nc.scalar.activation(h_hi[:, KR + m, 0:SEQ], uc[:, m, :], ACT.Copy).then_inc(u_hi_done, 1)

            def tanh(m):
                nc.scalar.activation(tnh[:, m, :], dec[:, m, :], ACT.Tanh, scale=spc[:, m:m + 1]).then_inc(tanh_done, 1)

            def decay(m):
                act.wait_ge(tanh_done, m + 1)
                nc.scalar.activation(dec[:, m, :], dec[:, m, :], ACT.Exp, scale=nspc[:, m:m + 1]).then_inc(dec_done, 1)

            def decay_squared(half):
                act.wait_ge(dec_done, 5 * half + 5)
                if half:
                    act.wait_ge(v_arg, 1)
                nc.scalar.activation(a2[:, :, :], dec[:, 5 * half:5 * half + 5, :], ACT.Square).then_inc(a2_done, 1)

            def root(half):
                c = slice(5 * half, 5 * half + 5)
                act.wait_ge(v_arg, half + 1)
                nc.scalar.activation(tnh[:, c, :], tnh[:, c, :], ACT.Sqrt).then_inc(v_root, 1)

            def gelu(part):
                first, end = H_PARTS[part]
                act.wait_ge(acc_free, st.u0 + RG_ORDER.index(("y", end - 1)) + 1)
                nc.scalar.activation(ybr[:, first:end, :], ybr[:, first:end, :], ACT.Gelu_apprx_tanh).then_inc(gelu_done, 1)

            def round_result(part):
                first, end = H_PARTS[part]
                act.wait_ge(rg_prod, part + 1)
                nc.scalar.activation(h_hi[:, first:end, 0:SEQ], dec[:, first:end, :], ACT.Copy).then_inc(rg_hi, 1)

            act.wait_ge(pad_zero, 1)
            for s, (kind, m) in enumerate(RG_ORDER):
                if (kind, m) not in RG_VECTOR:
                    behind = s and RG_ORDER[s - 1] == RG_VECTOR[-1]
                    round_ahead(st, s // SLOTS, s % SLOTS, 1 + len(RG_VECTOR) if behind else 1)
                for u in U_BEHIND.get((kind, m), ()):
                    round_u(u)
                if s and RG_ORDER[s - 1][0] == "gate":
                    b = RG_ORDER[s - 1][1]
                    act.wait_ge(spc_done, 1)
                    act.wait_ge(acc_free, st.u0 + s)
                    tanh(2 * b)
                    tanh(2 * b + 1)
                if kind == "y":
                    for n in {1: (0, 1), 2: (2, 3, 4), 3: (5, 6, 7), 4: (8, 9)}.get(m, ()):
                        decay(n)
                    if m in (2, 4):
                        decay_squared(m // 2 - 1)
                    if m in (5, 6):
                        root(m - 5)
                    if m == 6:
                        gelu(0)
                    if m == 8:
                        round_result(0)
                        gelu(1)
                act.wait_ge(chunk_used, st.n0 + s + 1)
                if kind == "u":
                    bank = acc((m % 4), SEQ)
                    if m >= 2:
                        act.wait_ge(conv_done, m - 1)
                    nc.scalar.activation(upad[:, m % 2, CONV - 1:], bank, ACT.Copy).then_inc(u_raw, 1)
                    nc.scalar.activation(uc[:, m, :], bank, ACT.Identity, scale=col(C_CW, (CONV - 1) * KR + m),
                                         bias=col(C_CB, m)).then_inc(acc_free, 1)
                elif kind == "gate":
                    for d in range(2):
                        nc.scalar.activation(dec[:, 2 * m + d, :], acc(4 + d, SEQ), ACT.Sigmoid, bias=col(C_GB, 2 * m + d))
                    for d in range(2):
                        last = nc.scalar.activation(ybr[:, 2 * m + d, :], acc(6 + d, SEQ), ACT.Sigmoid,
                                                    bias=col(C_GB, KR + 2 * m + d))
                    last.then_inc(acc_free, 1)
                else:
                    act.wait_ge(iu_done, m // 2 + 1)
                    nc.scalar.activation(ybr[:, m, :], acc((KR + m) % 4, SEQ), ACT.Copy).then_inc(acc_free, 1)
            gelu(2)
            round_result(1)
            round_result(2)
            squares(by_name["rg_out"])

        def keys_values():
            st = by_name["kv"]
            for s in range(2 * KD):
                round_ahead(st, s // SLOTS, s % SLOTS)
                act.wait_ge(chunk_used, st.n0 + s + 1)
                dst = kT[:, s, :] if s < KD else sq[:, s - KD, 0:SEQ]
                nc.scalar.activation(dst, acc(s % SLOTS, SEQ), ACT.Copy).then_inc(acc_free, 1)
            act.wait_ge(vT_done, 1)
            for t in range(2):
                for half in range(2):
                    nc.scalar.activation(v_tok[:, t, 512 * half:512 * half + 512], ps[:, 4 + 2 * t + half, :],
                                         ACT.Copy).then_inc(v_copied, 1)

        def attention():
            st = by_name["q"]

            def query(s):
                round_ahead(st, s // SLOTS, s % SLOTS)
                act.wait_ge(chunk_used, st.n0 + s + 1)
                hp = s // GROUPS
                if hp >= 2:
                    act.wait_ge(scored, 2 * hp - 2)
                nc.scalar.activation(qT[:, hp % 2, s % GROUPS, :], acc(two_banks(s), SEQ), ACT.Copy,
                                     scale=float(HD) ** -0.5).then_inc(acc_free, 1)

            def exps(a):
                act.wait_ge(nmax_done, a + 1)
                b = a % 2
                nc.scalar.activation(s_at[:, b, :, 0:P], s_at[:, b, :, 0:P], ACT.Exp,
                                     bias=nmax[:, b, 0:1], accum_out=den[:, b, 0:1])
                nc.scalar.activation(s_at[:, b, :, P:], s_at[:, b, :, P:], ACT.Exp,
                                     bias=nmax[:, b, 1:2], accum_out=den[:, b, 1:2]).then_inc(probs, 1)

            def copy_transposed(a):
                act.wait_ge(pT_done, a + 1)
                if a >= 2:
                    act.wait_ge(pv_done, a - 1)
                nc.scalar.activation(pT[:, a % 2, :], ps[:, 5, 0:SCORES], ACT.Copy).then_inc(pT_copied, 1)

            def round_output(hp):
                act.wait_ge(pv_done, 2 * hp + 2)
                nc.scalar.activation(h_hi[:, hp, 0:SEQ], acc(6 + hp % 2, SEQ), ACT.Copy).then_inc(at_hi, 1)

            for hp in range(PAIRS + 2):
                a, b, behind = 2 * hp - 2, 2 * hp - 1, 2 * hp - 3
                if 1 <= hp <= PAIRS:
                    exps(a)
                if hp < PAIRS:
                    query(3 * hp)
                if hp >= 2:
                    copy_transposed(behind)
                if hp < PAIRS:
                    query(3 * hp + 1)
                if hp >= 2:
                    round_output(hp - 2)
                if 1 <= hp <= PAIRS:
                    copy_transposed(a)
                if hp < PAIRS:
                    query(3 * hp + 2)
                if hp == PAIRS:
                    next_chunk(by_name["o"], 0, 0)
                if 1 <= hp <= PAIRS:
                    exps(b)
                if hp == PAIRS:
                    next_chunk(by_name["o"], 0, 1)
            squares(by_name["o"])

        def hybrid(l):
            st = by_name[f"mix{l}"]
            f0 = FOX_HEADS * l
            lr = slice(LOGIT_ROW, LOGIT_ROW + LOGIT_ROWS)

            def tile(s):
                src = acc(two_banks(s), TOK)
                act.wait_ge(chunk_used, st.n0 + s + 1)
                if s < VR0:
                    dst, scale = rot_in[:, s - ROT0, :], 1.0
                elif s < GATE0:
                    dst, scale = vr[:, s - VR0, :], 1.0
                elif s < POOL0:
                    if s == GATE0:
                        bf = par[lr, C_BF + l:C_BF + l + 1]
                        nc.scalar.activation(sgate[lr, 0, :], ps[lr, two_banks(s), 0:TOK], ACT.Identity, bias=bf).then_inc(fx_done, 1)
                        link(nc.scalar.activation(sgate[lr, 1, :], ps[lr, two_banks(s), 0:TOK], ACT.Abs, bias=bf))
                        nc.scalar.activation(sgate[lr, 1, :], sgate[lr, 1, :], ACT.Exp, scale=-1.0).then_inc(fe_done, 1)
                    dst, scale = gsb[:, s - GATE0, :], 1.0
                elif s < FOX0:
                    if s == POOL0:
                        act.wait_ge(up_zero, l + 1)
                    dst, scale = up[:, s - POOL0, POOL_PAD:], 1.0
                elif s < FOX0 + 3:
                    dst, scale = qf[:, s - FOX0, :], float(HD) ** -0.5
                elif s < FOX0 + 6:
                    dst, scale = kf[:, s - FOX0 - 3, :], 1.0
                else:
                    dst, scale = vf[:, s - FOX0 - 6, :], 1.0
                nc.scalar.activation(dst, src, ACT.Copy, scale=scale).then_inc(acc_free, 1)

            def exps(h):
                act.wait_ge(nmax_done, HEADS + f0 + h + 1)
                b = h % 2
                for q, (c, n, m) in enumerate(zip(FOX_AT, FOX_COLS, QT)):
                    last = nc.scalar.activation(s_fox[0:m, h % 3, c:c + n], s_fox[0:m, h % 3, c:c + n], ACT.Exp,
                                                bias=nmax_f[0:m, b, q:q + 1], accum_out=den_f[0:m, b, q:q + 1])
                last.then_inc(probs, 1)

            def copy_transposed(h):
                act.wait_ge(pT_done, HEADS + f0 + h + 1)
                if h >= 2:
                    act.wait_ge(pv_done, HEADS + f0 + h - 1)
                for k in range(3):
                    c = slice(KEY_AT[k], KEY_AT[k] + KEY_COLS[k])
                    last = nc.scalar.activation(pT_fox[0:QT[k], h % 2, c], ps[0:QT[k], 4, c], ACT.Copy)
                last.then_inc(pT_copied, 1)

            def round_output(hp):
                act.wait_ge(pv_done, HEADS + f0 + 2 * hp + 2)
                nc.scalar.activation(h_hi[:, RET_HEADS + 2 + hp, :], acc(5, TOK), ACT.Copy).then_inc(at_hi, 1)

            def copy_values(n, dst, banks):
                cols = FOX_W
                act.wait_ge(vt2_done, 2 * l + n + 1)
                for t in range(3):
                    last = nc.scalar.activation(dst[0:QT[t], t, 0:cols], ps[0:QT[t], banks[t], 0:cols], ACT.Copy)
                last.then_inc(vt2_copied, 1)

            out_bank = (4, 5, 6, 7)
            hd = slice(0, RET_DV)
            for s in range(WIN_TILES):
                round_ahead(st, s // SLOTS, s % SLOTS)
                n = s - GATE0
                if n == 1:
                    act.wait_ge(rot_done, 4 * (l + 1))
                    copy_values(0, vr_tok, (5, 6, 7))
                if 3 <= n < 3 + RET_HEADS:
                    h = n - 3
                    act.wait_ge(ret_o, RET_HEADS * l + h + 1)
                    nc.scalar.activation(osb[hd, h, :], ps[hd, out_bank[h], 0:TOK], ACT.Copy).then_inc(ret_osb, 1)
                if 5 <= n < 5 + RET_HEADS:
                    h = n - 5
                    act.wait_ge(ret_xc, RET_HEADS * l + h + 1)
                    if h >= 2:
                        act.wait_ge(ret_var, RET_HEADS * l + h - 1)
                    nc.scalar.activation(sqh[hd, h % 2, :], osb[hd, h, :], ACT.Square).then_inc(ret_sq, 1)
                if n == 6:
                    act.wait_ge(acc_free, st.u0 + POOL0)
                    nc.scalar.activation(gsb[:, :, :], gsb[:, :, :], ACT.Silu).then_inc(silu2, 1)
                if n == 7:
                    act.wait_ge(ret_s, RET_HEADS * (l + 1))
                    nc.scalar.activation(sel_r[lr, :], con2[lr, B_SEL:B_SEL + FOX_HEADS * P], ACT.Copy).then_inc(sel_done, 1)
                if n == 9:
                    act.wait_ge(ret_var, RET_HEADS * (l + 1))
                    nc.scalar.activation(std4[0:RET_HEADS, :], ps[0:RET_HEADS, 2, 0:TOK], ACT.Sqrt,
                                         bias=eps[0:RET_HEADS, 0:1]).then_inc(ret_std, 1)
                if n == 12:
                    act.wait_ge(pool_mm, l + 1)
                    for m in range(2):
                        nc.scalar.activation(h_hi[:, RET_HEADS + m, :], acc(2 + m, TOK), ACT.Copy,
                                             scale=par[:, C_PS + 2 * l + m:C_PS + 2 * l + m + 1]).then_inc(pool_hi, 1)
                tile(s)
            exps(0)
            copy_values(1, vf_tok, (4, 5, 1))
            for h in range(FOX_HEADS):
                if h + 1 < FOX_HEADS:
                    exps(h + 1)
                if h >= 2 and h % 2 == 0:
                    round_output(h // 2 - 1)
                if h == FOX_HEADS - 1:
                    for j in range(2):
                        next_chunk(by_name[f"mixo{l}"], 0, j)
                copy_transposed(h)
            round_output(2)
            squares(by_name[f"mixo{l}"])

        start()
        ffn(0)
        layer_norm("out0")
        recurrent()
        layer_norm("rg_out")
        ffn(1)
        layer_norm("out1")
        keys_values()
        ffn(2)
        layer_norm("out2")
        attention()
        layer_norm("o")
        ffn(3)
        layer_norm("out3")
        layer_norm("emb")
        for l in range(LAYERS_2):
            hybrid(l)
            layer_norm(f"mixo{l}")
            ffn(4 + l)
            layer_norm(f"out{4 + l}")

    @block.vector
    def _(dve):
        own = [0]

        def link(ins):
            own[0] += 1
            ins.then_inc(dve_step, 1)
            dve.wait_ge(dve_step, own[0])

        V = nc.vector
        f = lambda ap: ap.bitcast(fp32)

        def rest_of_chunk(n, slot, rnd, cols):
            dve.wait_ge(w_hi_done, n + 1)
            V.tensor_tensor(wlo[slot][:, 0:cols], raw[slot][:, 0:cols], f(whi[slot][:, 0:cols]),
                            ALU.subtract).then_inc(w_lo_done, 1)

        def rest_ahead(st, i, j):
            if early_split(st, i, j):
                return
            if st.name in behind_norm and isinstance(i, int) and i == 0:
                if j >= 2:
                    return
                j += 2
            a = ahead(st, i, j)
            if a:
                rest_of_chunk(*a)

        def log1p(part, e, s, s2, p):
            if part == 0:
                link(V.tensor_scalar(s, e, 2.0, None, ALU.add))
                link(V.reciprocal(s, s))
            elif part == 1:
                link(V.tensor_tensor(s, s, e, ALU.mult))
                link(V.tensor_tensor(s2, s, s, ALU.mult))
                link(V.tensor_scalar(p, s2, 1.0 / 17, None, ALU.mult))
            else:
                for odd in ((15, 13), (11, 9), (7, 5), (3,))[part - 2]:
                    link(V.scalar_tensor_tensor(p, p, 1.0 / odd, s2, ALU.add, ALU.mult))

        def start():
            V.memset(sums[:, :, :], 0.0).then_inc(zeros, 1)
            link(V.memset(eps[:, :], LN_EPS))
            dve.sem_inc(acc_free, SLOTS)
            rest_of_chunk(0, 0, 0, stages[0].cols)
            for k in range(KD):
                dve.wait_ge(x_hi_done, k + 1)
                V.tensor_tensor(x_lo[:, k, META:TOK], r[:, k, META:TOK], f(x_hi[:, k, META:TOK]),
                                ALU.subtract).then_inc(x_ready, 1)
                if k == 1:
                    rest_of_chunk(1, 1, 0, stages[0].cols)

        def parameters(part):
            s, s2, p = lser[:, 2, :], lser[:, 3, :], lser[:, 4, :]
            dve.wait_ge(ser_e, 1)
            for n in ((0,), (1, 2), (3, 4), (5,))[part]:
                log1p(n, lser[:, 1, :], s, s2, p)
            if part == 3:
                link(V.scalar_tensor_tensor(s, p, 1.0, s, ALU.add, ALU.mult))
                link(V.tensor_scalar(s2, par[:, C_LAM:C_LAM + KR], -1.0, 0.0, ALU.mult, ALU.max))
                link(V.scalar_tensor_tensor(s, s, 2.0, s2, ALU.mult, ALU.add))
                link(V.tensor_scalar(nspc[:, :], s, -8.0, None, ALU.mult))
                V.tensor_scalar(spc[:, :], s, 8.0, None, ALU.mult).then_inc(spc_done, 1)

        def ffn(fn):
            st = by_name[f"in{fn}"]
            T = tokens[st.name]
            h0 = h_base[fn]

            def step(i, j):
                rest_ahead(st, i, j)
                if fn == 0 and isinstance(i, int) and i:
                    parameters(j)
                if j % 2:
                    b = j // 2
                    p = 2 * i + b
                    dve.wait_ge(chunk_used, SLOTS * i + (st.n0 + j + 1))
                    dve.wait_ge(gate_done, 2 * i + (KF * fn + b + 1))
                    V.tensor_tensor(prod[:, b, 0:T], sgate[:, b, 0:T], acc(j, T), ALU.mult).then_inc(acc_free, 1)
                    dve.wait_ge(acc_free, 2 * i + (st.u0 + b + 1))
                    V.tensor_copy(h_hi[:, p, 0:T], prod[:, b, 0:T]).then_inc(h_hi_done, 1)
                    dve.wait_ge(h_hi_done, 2 * i + (h0 + b + 1))
                    V.tensor_tensor(h_lo[:, p, 0:T], prod[:, b, 0:T], f(h_hi[:, p, 0:T]),
                                    ALU.subtract).then_inc(h_ready, 1)

            steps(dve, st.chunks, step, start=1)
            so = by_name[f"out{fn}"]
            new_sums(so)

            def out_step(i, j):
                rest_ahead(so, i, j)
                if j % 2:
                    add_tile(so, 2 * i, j // 2, j // 2, SLOTS * i + (so.n0 + j + 1), 0.5 if fn < 4 else 1.0)

            steps(dve, so.chunks, out_step, start=1)

        def new_sums(st):
            dve.wait_ge(ax_done, KD * (x_of[st.name] + 1))
            link(V.memset(sums[:, :, :], 0.0))

        def add_tile(st, i, j, bank, chunks_used, scale):
            T = tokens[st.name]
            t = slice(tok0(T), TOK)
            m = i + j
            first = isinstance(i, int) and m == 0
            last = isinstance(i, int) and m == KD - 1

            def less_shift(tile, signal):
                return V.scalar_tensor_tensor(tile, acc(7, T), float(-KD), tile, ALU.mult, ALU.add).then_inc(signal, 1)

            def add_square(late):
                dve.wait_ge(sq_done, i + (KD * norm_no[st.name] + j - late + 1))
                return V.tensor_tensor(sums[:, 1, t], sums[:, 1, t], sq[:, i + (j - late), t], ALU.add)

            if isinstance(i, int) and m == 1:
                dve.wait_ge(shift_done, norm_stages.index(st.name) + 1)
                less_shift(r[:, 0, t], shifted)
                dve.wait_ge(shifted, norm_stages.index(st.name) + 1)
                V.tensor_tensor(sums[:, 0, t], sums[:, 0, t], r[:, 0, t], ALU.add)
            if not first:
                less_shift(ax[:, m, t], ax_shifted)
                dve.wait_ge(ax_shifted, i + ((KD - 1) * norm_stages.index(st.name) + j))
            if last:
                link(add_square(2))
                add_square(1).then_inc(sums_done, 1)
            elif not first and not (isinstance(i, int) and m == 1):
                add_square(2)
            if last and st.next:
                rest_of_chunk(*ahead(st.next, 0, 0))
            dve.wait_ge(chunk_used, chunks_used)
            V.scalar_tensor_tensor(r[:, m, t], acc(bank, T), scale, ax[:, m, t], ALU.mult, ALU.add).then_inc(acc_free, 1)
            if not first and not last:
                dve.wait_ge(acc_free, i + (st.u0 + j + 1))
                V.tensor_tensor(sums[:, 0, t], sums[:, 0, t], r[:, m, t], ALU.add)

        def add_to_ax(st):
            new_sums(st)

            def step(i, j):
                rest_ahead(st, i, j)
                add_tile(st, SLOTS * i, j, j, SLOTS * i + (st.n0 + j + 1), 1.0)

            steps(dve, st.chunks, step)

        def layer_norm(name):
            n = norm_no[name]
            _, T, kind = norms[n]
            t = slice(tok0(T), TOK)
            nt = len(token_starts(T))

            def centre(k):
                mean = acc(4, T).unsqueeze(1).broadcast_to([P, 2, T])
                V.tensor_tensor(r[:, k:k + 2, t], r[:, k:k + 2, t], mean, ALU.subtract).then_inc(xc_done, 1)

            dve.wait_ge(mean_done, n + 1)
            if name == "emb":
                for k in range(0, KD, 2):
                    centre(k)
                for k in range(2, KD, 2):
                    dve.wait_ge(sq_done, KD * n + k + 2)
                    link(V.tensor_tensor(sq[:, 0:2, :], sq[:, 0:2, :], sq[:, k:k + 2, :], ALU.add))
                V.tensor_tensor(sums[:, 1, :], sq[:, 0, :], sq[:, 1, :], ALU.add).then_inc(emb_squares, 1)
            else:
                centre(0)
                ns = norm_stages.index(name)
                dve.wait_ge(msq_done, ns + 1)
                V.tensor_tensor(var_t[:, 0:nt], ps[:, 5, 4:4 + nt], msq[:, 0:nt], ALU.subtract).then_inc(var_ready, 1)
            dve.wait_ge(std_done, n + 1)
            V.reciprocal(rstd_t[:, 0:nt], std_t[:, 0:nt]).then_inc(rstd_done, 1)
            if name != "emb":
                centre(2)
                centre(4)
            dve.wait_ge(spread, n + 1)
            dve.wait_ge(xc_done, 4 * n + 3)
            v = version.get(name, 0)
            for k in range(KD + 1):
                if k == 2 and name != "emb":
                    centre(6)
                if k == 6:
                    dve.wait_ge(xc_done, 4 * n + 4)
                if k < KD:
                    V.scalar_tensor_tensor(r[:, k, t], r[:, k, t], par[:, C_G + KD * n + k:C_G + KD * n + k + 1],
                                           acc(6, T), ALU.mult, ALU.mult).then_inc(xn_done, 1)
                if k and kind == "x":
                    c = C_B + KD * n + k - 1
                    dve.wait_ge(x_hi_done, KD * v + k)
                    V.scalar_tensor_tensor(x_lo[:, k - 1, t], r[:, k - 1, t], par[:, c:c + 1], f(x_hi[:, k - 1, t]),
                                           ALU.add, ALU.subtract).then_inc(x_ready, 1)
            if name != "out3":
                nxt = by_name["out3" if name == "emb" else name].next
                if nxt:
                    rest_of_chunk(*ahead(nxt, 0, 1))

        def recurrent():
            st = by_name["rg"]
            V.memset(upad[:, :, 0:CONV - 1], 0.0).then_inc(pad_zero, 1)

            def rest_of_u(m):
                dve.wait_ge(u_hi_done, m + 1)
                V.tensor_tensor(h_lo[:, KR + m, 0:SEQ], uc[:, m, :], f(h_hi[:, KR + m, 0:SEQ]), ALU.subtract).then_inc(u_ready, 1)

            def convolve(m):
                dve.wait_ge(u_raw, m + 1)
                dve.wait_ge(acc_free, st.u0 + RG_ORDER.index(("u", m)) + 1)
                for j in range(CONV - 1):
                    ins = V.scalar_tensor_tensor(uc[:, m, :], upad[:, m % 2, j:j + SEQ],
                                                 par[:, C_CW + j * KR + m:C_CW + j * KR + m + 1], uc[:, m, :], ALU.mult, ALU.add)
                    if j < CONV - 2:
                        link(ins)
                ins.then_inc(conv_done, 1)

            def gate_input(b):
                dve.wait_ge(acc_free, st.u0 + RG_ORDER.index(("gate", b)) + 1)
                c = slice(2 * b, 2 * b + 2)
                V.tensor_tensor(uc[:, c, :], uc[:, c, :], ybr[:, c, :], ALU.mult).then_inc(iu_done, 1)

            def root_argument(half):
                c = slice(5 * half, 5 * half + 5)
                dve.wait_ge(a2_done, half + 1)
                V.scalar_tensor_tensor(tnh[:, c, :], a2[:, :, :], 1.0, tnh[:, c, :], ALU.add, ALU.mult).then_inc(v_arg, 1)

            def scan(half):
                c = slice(5 * half, 5 * half + 5)
                dve.wait_ge(v_root, half + 1)
                link(V.tensor_tensor(uc[:, c, :], uc[:, c, :], tnh[:, c, :], ALU.mult))
                for m in range(5 * half, 5 * half + 5):
                    V.tensor_tensor_scan(tnh[:, m, :], dec[:, m, :], uc[:, m, :], 0.0, ALU.mult, ALU.add).then_inc(dve_step, 1)
                    own[0] += 1

            def product(part):
                c = slice(*H_PARTS[part])
                dve.wait_ge(dve_step, own[0])
                dve.wait_ge(gelu_done, part + 1)
                V.tensor_tensor(dec[:, c, :], tnh[:, c, :], ybr[:, c, :], ALU.mult).then_inc(rg_prod, 1)

            def rest_of_result(part):
                first, end = H_PARTS[part]
                dve.wait_ge(rg_hi, part + 1)
                V.tensor_tensor(h_lo[:, first:end, 0:SEQ], dec[:, first:end, :], f(h_hi[:, first:end, 0:SEQ]),
                                ALU.subtract).then_inc(rg_ready, 1)

            for s, (kind, m) in enumerate(RG_ORDER):
                if (kind, m) in RG_VECTOR:
                    n, slot, rnd, cols = ahead(st, s // SLOTS, s % SLOTS)
                    dve.wait_ge(raw_landed[slot], 16 * rnd + 16)
                    dve.wait_ge(chunk_used, n - SLOTS + 1)
                    link(V.tensor_copy(whi[slot][:, 0:cols], raw[slot][:, 0:cols]))
                    V.tensor_tensor(wlo[slot][:, 0:cols], raw[slot][:, 0:cols], f(whi[slot][:, 0:cols]),
                                    ALU.subtract).then_inc(w_lo_done, 1)
                else:
                    rest_ahead(st, s // SLOTS, s % SLOTS)
                if s and RG_ORDER[s - 1][0] == "gate":
                    gate_input(RG_ORDER[s - 1][1])
                for u in U_BEHIND.get((kind, m), ()):
                    rest_of_u(u)
                if kind == "u":
                    convolve(m)
                if kind == "y":
                    if m in (3, 5):
                        root_argument(m // 2 - 1)
                    if m == 6:
                        scan(0)
                    if m == 7:
                        product(0)
                    if m == 8:
                        rest_of_result(0)
                        scan(1)
                    if m == 9:
                        product(1)
            product(2)
            rest_of_result(1)
            rest_of_result(2)
            add_to_ax(by_name["rg_out"])

        def keys_values():
            st = by_name["kv"]
            steps(dve, st.chunks, lambda i, j: rest_ahead(st, i, j), start=1)

        def attention():
            st = by_name["q"]

            def rest(s):
                rest_ahead(st, s // SLOTS, s % SLOTS)

            def bias_max(a):
                slope = float(2.0 ** (-8.0 * (a + 1) / HEADS))
                b = a % 2
                dve.wait_ge(scored, a + 1)
                if a >= 2:
                    dve.wait_ge(pT_done, a - 1)
                V.scalar_tensor_tensor(s_at[:, b, :, :], dist[:, :, :], slope, ps[:, 2:2 + GROUPS, 0:SCORES],
                                       ALU.mult, ALU.add).then_inc(biased, 1)
                dve.wait_ge(biased, a + 1)
                V.tensor_reduce(nmax[:, b, 0:1], s_at[:, b, :, 0:P], AX.XY, ALU.max, negate=True)
                V.tensor_reduce(nmax[:, b, 1:2], s_at[:, b, :, P:], AX.XY, ALU.max, negate=True).then_inc(nmax_done, 1)

            def sum_groups(a):
                b = a % 2
                dve.wait_ge(probs, a + 1)
                V.reciprocal(rden[:, b, :], den[:, b, :])
                s = s_at[:, b, 0, :]
                link(V.tensor_tensor(s, s, s_at[:, b, 1, :], ALU.add))
                link(V.tensor_tensor(s, s, s_at[:, b, 2, :], ALU.add))
                V.tensor_scalar(s_at[:, b, 0, 0:P], s_at[:, b, 0, 0:P], rden[:, b, 0:1], None, ALU.mult)
                V.tensor_scalar(s_at[:, b, 0, P:], s_at[:, b, 0, P:], rden[:, b, 1:2], None, ALU.mult).then_inc(probs_ready, 1)

            def rest_of_output(hp):
                dve.wait_ge(at_hi, hp + 1)
                V.tensor_tensor(h_lo[:, hp, 0:SEQ], acc(6 + hp % 2, SEQ), f(h_hi[:, hp, 0:SEQ]), ALU.subtract).then_inc(at_ready, 1)

            dve.wait_ge(bias_landed, 16)
            for hp in range(PAIRS + 2):
                a, b, behind = 2 * hp - 2, 2 * hp - 1, 2 * hp - 3
                if 1 <= hp <= PAIRS:
                    bias_max(a)
                if hp >= 2:
                    sum_groups(behind)
                if 1 <= hp <= PAIRS:
                    sum_groups(a)
                if hp < PAIRS:
                    rest(3 * hp)
                if 1 <= hp <= PAIRS:
                    bias_max(b)
                if hp >= PAIRS:
                    rest_of_chunk(*ahead(by_name["o"], 0, hp - PAIRS))
                if hp >= 2:
                    rest_of_output(hp - 2)
                if hp < PAIRS:
                    rest(3 * hp + 1)
                    rest(3 * hp + 2)
            add_to_ax(by_name["o"])

        def hybrid(l):
            st = by_name[f"mix{l}"]
            f0 = FOX_HEADS * l
            lr = slice(LOGIT_ROW, LOGIT_ROW + LOGIT_ROWS)
            k2 = lambda c, n: con2[:, c:c + n]

            def rest(s):
                rest_ahead(st, s // SLOTS, s % SLOTS)

            def cumulative_logits(part):
                e, s, s2, p = sgate[lr, 1, :], prod[lr, 0, :], prod[lr, 1, :], frow[lr, 0, :]
                if part == 0:
                    dve.wait_ge(fe_done, l + 1)
                if part < 6:
                    log1p(part, e, s, s2, p)
                    return
                if part == 7:
                    link(V.tensor_copy(c_parts[lr, :], frow[lr, 1, :]))
                    V.scalar_tensor_tensor(c_parts[lr, :], f(c_parts[lr, :]), con2[lr, B_LO:B_LO + 1], frow[lr, 1, :],
                                           ALU.mult, ALU.add).then_inc(c_done, 1)
                    return
                link(V.scalar_tensor_tensor(s, p, 1.0, s, ALU.add, ALU.mult))
                link(V.tensor_scalar(s2, sgate[lr, 0, :], 0.0, None, ALU.min))
                link(V.scalar_tensor_tensor(s, s, -2.0, s2, ALU.mult, ALU.add))
                link(V.tensor_tensor_scan(frow[lr, 1, :], con2[lr, B_ONE:B_ONE + TOK], s, 0.0, ALU.mult, ALU.add))

            def mask_max(h):
                b = h % 2
                n_all = HEADS + f0 + h
                bank = 2 if b == 0 else 6
                dve.wait_ge(scored, n_all + 1)
                if h >= 3:
                    dve.wait_ge(pT_done, n_all - 2)
                for q, at in enumerate(((bank, 0), (bank, FOX_AT[1]), (bank + 1, 0))):
                    c, n, m = FOX_AT[q], FOX_COLS[q], QT[q]
                    ins = V.tensor_tensor(s_fox[0:m, h % 3, c:c + n], ps[0:m, at[0], at[1]:at[1] + n],
                                          con2[0:m, B_MASK + c:B_MASK + c + n], ALU.add)
                ins.then_inc(biased, 1)
                dve.wait_ge(biased, n_all + 1)
                for q, (c, n, m) in enumerate(zip(FOX_AT, FOX_COLS, QT)):
                    ins = V.tensor_reduce(nmax_f[0:m, b, q:q + 1], s_fox[0:m, h % 3, c:c + n], AX.X, ALU.max, negate=True)
                ins.then_inc(nmax_done, 1)

            def normalise(h):
                b = h % 2
                dve.wait_ge(probs, HEADS + f0 + h + 1)
                for q in range(3):
                    ins = V.reciprocal(rden_f[0:QT[q], b, q:q + 1], den_f[0:QT[q], b, q:q + 1])
                link(ins)
                for q, (c, n, m) in enumerate(zip(FOX_AT, FOX_COLS, QT)):
                    s = s_fox[0:m, h % 3, c:c + n]
                    ins = V.tensor_scalar(s, s, rden_f[0:m, b, q:q + 1], None, ALU.mult)
                ins.then_inc(probs_ready, 1)

            def rest_of_output(hp):
                dve.wait_ge(at_hi, PAIRS + 3 * l + hp + 1)
                k = RET_HEADS + 2 + hp
                V.tensor_tensor(h_lo[:, k, :], acc(5, TOK), f(h_hi[:, k, :]), ALU.subtract).then_inc(at_ready, 1)

            def rotate(which):
                x1, x2 = rot_in[:, 2 * which, :], rot_in[:, 2 * which + 1, :]
                cos, sin = k2(B_COS, TOK), k2(B_SIN, TOK)
                dve.wait_ge(acc_free, st.u0 + ROT0 + 2 * which + 2)
                for half, (p, q, op) in enumerate(((cos, sin, ALU.subtract), (sin, cos, ALU.add))):
                    V.tensor_tensor(rtmp[:, 0, :], x1, p, ALU.mult)
                    link(V.tensor_tensor(rtmp[:, 1, :], x2, q, ALU.mult))
                    ins = V.tensor_tensor(rot[:, 2 * which + half, :], rtmp[:, 0, :], rtmp[:, 1, :], op)
                    ins.then_inc(rot_done, 1)
                    dve.wait_ge(rot_done, 4 * l + 2 * which + half + 1)

            def pool(part):
                dve.wait_ge(acc_free, st.u0 + FOX0)
                end = POOL_PAD + TOK
                both = slice(0, 2)
                tok = slice(POOL_PAD, end)
                if part == 1:
                    cnt = con2[:, B_CNT:B_CNT + 2 * TOK].rearrange("p (m t) -> p m t", m=2)
                    link(V.tensor_tensor(w_b[:, :, tok], w_b[:, :, tok], cnt, ALU.mult))
                    V.tensor_tensor(w_b[:, :, tok], w_b[:, :, tok], up[:, :, tok], ALU.subtract).then_inc(pool_done, 1)
                    return
                link(V.tensor_tensor(w_a[:, both, 1:end], up[:, both, 1:end], up[:, both, 0:end - 1], ALU.add))
                link(V.tensor_tensor(w_b[:, both, 3:end], w_a[:, both, 3:end], w_a[:, both, 1:end - 2], ALU.add))
                link(V.tensor_tensor(w_a[:, 1, 7:end], w_b[:, 1, 7:end], w_b[:, 1, 3:end - 4], ALU.add))
                link(V.tensor_tensor(w_b[:, 1, 15:end], w_a[:, 1, 15:end], w_a[:, 1, 7:end - 8], ALU.add))
                half = P // 2
                for m in range(2):
                    V.tensor_copy(w_b[0:half, m, tok], w_a[0:half, m, tok]).then_inc(dve_step, 1)
                    own[0] += 1
                dve.wait_ge(dve_step, own[0])

            def decay(h):
                n = RET_HEADS * l + h
                dve.wait_ge(ret_s, n + 1)
                if h >= 2:
                    dve.wait_ge(ret_o, n - 1)
                c = B_DEC + h * KEYS_ALL
                for k in range(3):
                    at = slice(KEY_AT[k], KEY_AT[k] + KEY_COLS[k])
                    ins = V.tensor_tensor(s_fox[0:QT[k], h % 2, at], ps[0:QT[k], 2 + h % 2, at],
                                          k2(c, KEYS_ALL)[0:QT[k], at], ALU.mult)
                ins.then_inc(ret_d, 1)

            out_bank = (4, 5, 6, 7)
            hd = slice(0, RET_DV)

            def centre(h):
                dve.wait_ge(ret_mean, RET_HEADS * l + h + 1)
                V.tensor_tensor(osb[hd, h, :], osb[hd, h, :], ps[hd, out_bank[h], 0:TOK], ALU.subtract).then_inc(ret_xc, 1)

            def gated(h):
                n = RET_HEADS * l + h
                dve.wait_ge(ret_bc, n + 1)
                dve.wait_ge(silu2, l + 1)
                c = C_GN + n
                link(V.scalar_tensor_tensor(osb[hd, h, :], osb[hd, h, :], par[hd, c:c + 1], ps[hd, out_bank[h], 0:TOK], ALU.mult, ALU.mult))
                link(V.tensor_tensor(osb[hd, h, :], osb[hd, h, :], gsb[hd, h, :], ALU.mult))
                V.tensor_copy(h_hi[hd, h, :], osb[hd, h, :]).then_inc(ret_hi, 1)
                dve.wait_ge(ret_hi, n + 1)
                V.tensor_tensor(h_lo[hd, h, :], osb[hd, h, :], f(h_hi[hd, h, :]), ALU.subtract).then_inc(ret_ready, 1)

            for s in range(WIN_TILES):
                rest(s)
                n = s - GATE0
                if s in (ROT0 + 2, ROT0 + 4):
                    rotate(s // 2 - 1)
                if n == 0:
                    dve.wait_ge(ax_done, KD * (x_of[st.name] + 1))
                    V.memset(up[:, :, 0:POOL_PAD], 0.0).then_inc(up_zero, 1)
                if 1 <= n < 9:
                    cumulative_logits(n - 1)
                if 2 <= n < 2 + RET_HEADS:
                    decay(n - 2)
                if 4 <= n < 4 + RET_HEADS:
                    centre(n - 4)
                if n in (8, 9):
                    pool(n - 8)
                if n == 10:
                    dve.wait_ge(ret_std, l + 1)
                    V.reciprocal(std4[0:RET_HEADS, :], std4[0:RET_HEADS, :]).then_inc(ret_rstd, 1)
                if n == 12:
                    for m in range(2):
                        dve.wait_ge(pool_hi, 2 * l + m + 1)
                        V.scalar_tensor_tensor(h_lo[:, RET_HEADS + m, :], acc(2 + m, TOK),
                                               par[:, C_PS + 2 * l + m:C_PS + 2 * l + m + 1], f(h_hi[:, RET_HEADS + m, :]),
                                               ALU.mult, ALU.subtract).then_inc(pool_ready, 1)
                if 11 <= n < 11 + RET_HEADS:
                    gated(n - 11)
            mask_max(0)
            for h in range(FOX_HEADS):
                if h + 1 < FOX_HEADS:
                    mask_max(h + 1)
                if h >= 3 and h % 2:
                    rest_of_output(h // 2 - 1)
                normalise(h)
            for j in range(2):
                rest_of_chunk(*ahead(by_name[f"mixo{l}"], 0, j))
            rest_of_output(2)
            add_to_ax(by_name[f"mixo{l}"])

        start()
        ffn(0)
        layer_norm("out0")
        recurrent()
        layer_norm("rg_out")
        ffn(1)
        layer_norm("out1")
        keys_values()
        ffn(2)
        layer_norm("out2")
        attention()
        layer_norm("o")
        ffn(3)
        layer_norm("out3")
        layer_norm("emb")
        for l in range(LAYERS_2):
            hybrid(l)
            layer_norm(f"mixo{l}")
            ffn(4 + l)
            layer_norm(f"out{4 + l}")

    block_guard.__exit__(None, None, None)
    for s in reversed(sems):
        s.__exit__(None, None, None)
    psum.__exit__(None, None, None)
    slab.__exit__(None, None, None)


def constants():
    con = np.zeros((P, 3, P), np.float32)
    con[:, 0] = np.eye(P)
    con[:, 1] = 1.0 / D
    con[:RET_DV, 2] = 1.0 / RET_DV

    far = -1e33
    t = np.arange(SEQ)
    dist = t[:, None] - t[None, :]
    bias = np.full((P, GROUPS, SCORES), far, np.float32)
    for g, (window, dilation) in enumerate(DILATIONS):
        seen = (dist >= 0) & (dist <= window) & (dist % dilation == 0)
        b = np.where(seen, -dist, far)
        bias[:, g, :P] = b[:P, :P]
        bias[:, g, P:] = b[P:]

    c2 = np.zeros((P, N_B), np.float32)
    for h in range(RET_HEADS):
        c2[h, B_EXP + h * P:B_EXP + (h + 1) * P] = 1.0
        c2[:RET_DV, B_HEAD + RET_HEADS * h + h] = 1.0 / RET_DV
    for h in range(FOX_HEADS):
        c2[[LOGIT_ROW + h, LOGIT_ROW + FOX_HEADS + h], B_SEL + h * P:B_SEL + (h + 1) * P] = -1.0
        c2[LOGIT_ROW + FOX_HEADS + h, B_LO] = -1.0
    c2[:, B_ONE:B_ONE + TOK] = 1.0
    pos = np.arange(TOK, dtype=np.float32)
    freq = np.float32(10000.0) ** (-np.arange(HALF_DK, dtype=np.float32) / np.float32(HALF_DK))
    ang = (freq[:, None] * pos[None, :]).astype(np.float32)
    for h in range(RET_HEADS):
        c2[32 * h:32 * h + HALF_DK, B_COS:B_COS + TOK] = np.cos(ang)
        c2[32 * h:32 * h + HALF_DK, B_SIN:B_SIN + TOK] = np.sin(ang)
        log_gamma = np.log(1.0 - 2.0 ** (-5.0 - h))
        for k in range(3):
            keys = np.arange(QT_AT[k], QT_AT[k] + QT[k])
            away = np.arange(QT_AT[k], TOK)[None, :] - keys[:, None]
            decay = np.where(away >= 0, np.exp(log_gamma * np.maximum(away, 0)), 0.0) * RET_DK ** -0.5
            at = B_DEC + h * KEYS_ALL + KEY_AT[k]
            c2[:len(keys), at:at + KEY_COLS[k]] = decay
    for q in range(3):
        queries = np.arange(QT_AT[q], QT_AT[q] + QT[q])
        hidden = np.where(queries[:, None] >= np.arange(FOX_COLS[q])[None, :], 0.0, -1e30)
        c2[:QT[q], B_MASK + FOX_AT[q]:B_MASK + FOX_AT[q] + FOX_COLS[q]] = hidden
    for n, w in enumerate(POOL_WINDOWS):
        rows = slice(64 * (n % 2), 64 * (n % 2) + 64)
        c2[rows, B_CNT + (n // 2) * TOK:B_CNT + (n // 2 + 1) * TOK] = 1.0 / np.minimum(np.arange(TOK) + 1, w)
    return con.reshape(P, 3 * P), bias, c2


def chunks(w, halves=1):
    K, M = w.shape
    w = w.reshape(halves, K // halves // P, P, M // P, P).transpose(3, 0, 2, 1, 4)
    return np.ascontiguousarray(w.reshape(M // P * halves, P, K // halves))


def paired(gate, up):
    K = gate.shape[0]
    return np.stack([gate.reshape(K, KF, P), up.reshape(K, KF, P)], 2).reshape(K, 2 * FF)


def hybrid_columns(w):
    parts = np.split(w, np.cumsum([192, 192, 384, 384, 256, 384, 384, 384]), axis=1)
    q, k, v, g, u, qf, kf, vf, logits = parts

    def halves(a):
        a = a.reshape(D, RET_HEADS, 2, HALF_DK)
        t = np.zeros((D, 2, RET_HEADS, 32), w.dtype)
        t[..., :HALF_DK] = a.transpose(0, 2, 1, 3)
        return t.reshape(D, 2 * P)

    def padded(a):
        t = np.zeros((D, RET_HEADS, P), w.dtype)
        t[..., :RET_DV] = a.reshape(D, RET_HEADS, RET_DV)
        return t

    g = padded(g)
    g[:, 0, LOGIT_ROW:LOGIT_ROW + LOGIT_ROWS] = np.tile(logits, 2)
    return np.concatenate([halves(q), halves(k), v, g.reshape(D, RET_HEADS * P), u, qf, kf, vf], axis=1)


def hybrid_rows(w):
    t = np.zeros((RET_HEADS, P, D), w.dtype)
    t[:, :RET_DV] = w[:RET_HEADS * RET_DV].reshape(RET_HEADS, RET_DV, D)
    return np.concatenate([t.reshape(-1, D), w[RET_HEADS * RET_DV:]], axis=0)


def tiles(v):
    return v.reshape(-1, P).T


def kernel(**inputs):
    import concourse.bacc as bacc
    from concourse.bass_utils import run_bass_kernel_spmd

    a = {k: np.asarray(v) for k, v in inputs.items()}
    f32 = np.float32
    ffn_in = [paired(*np.split(a["ffn_w_in"][l, i], 2, axis=1)) for l in range(2) for i in range(2)]
    ffn_in += [paired(a["w_ffn1_2"][l], a["w_ffn3_2"][l]) for l in range(LAYERS_2)]
    ffn_out = [a["ffn_w_out"][l, i] for l in range(2) for i in range(2)] + [a["w_ffn2_2"][l] for l in range(LAYERS_2)]
    weights = {}
    for f in range(6):
        weights[f"in{f}"] = chunks(ffn_in[f])
        weights[f"out{f}"] = chunks(ffn_out[f], 2)
    y_cols, u_cols = np.split(a["rg_w_in"][0], 2, axis=1)
    gate = a["rg_gate_w"][0].reshape(2, GATE_BLOCKS, 2, P, 2, P)
    gate = gate.transpose(1, 3, 0, 4, 2, 5).reshape(GATE_BLOCKS, P, 8 * P)
    parts = {"u": chunks(u_cols), "gate": gate, "y": chunks(y_cols)}
    weights["rg"] = np.stack([parts[kind][m] for kind, m in RG_ORDER])
    weights["rg_out"] = chunks(a["rg_w_out"][0])
    weights["kv"] = chunks(a["kv_w"])
    q = a["attn_w_q"][0].reshape(D, GROUPS, PAIRS, P).transpose(0, 2, 1, 3)
    weights["q"] = chunks(q.reshape(D, GROUPS * PAIRS * P))
    weights["o"] = chunks(a["attn_w_o"][0])
    for l in range(LAYERS_2):
        weights[f"mix{l}"] = chunks(hybrid_columns(a["w_in_2"][l]))
        weights[f"mixo{l}"] = chunks(hybrid_rows(a["w_out_2"][l]))

    gains = [a["ln_g"].reshape(-1), a["ln_emb_g_2"]]
    shifts = [a["ln_b"].reshape(-1), a["ln_emb_b_2"]]
    for l in range(LAYERS_2):
        gains += [a["ln1_g_2"][l], a["ln2_g_2"][l]]
        shifts += [a["ln1_b_2"][l], a["ln2_b_2"][l]]
    par = np.zeros((P, N_PAR), f32)
    par[:, C_G:C_B] = tiles(np.concatenate(gains))
    par[:, C_B:C_CW] = tiles(np.concatenate(shifts))
    par[:, C_CW:C_CB] = tiles(a["rg_conv_w"][0].reshape(-1))
    par[:, C_CB:C_GB] = tiles(a["rg_conv_b"][0])
    par[:, C_GB:C_LAM] = tiles(a["rg_gate_b"][0].reshape(-1))
    par[:, C_LAM:C_GN] = tiles(a["rg_lam"][0])
    par[:RET_DV, C_GN:C_PS] = a["ret_gn_g_2"].reshape(-1, RET_DV).T
    par[:, C_PS:C_BF] = tiles(a["pool_scale_2"].reshape(-1))
    par[LOGIT_ROW:LOGIT_ROW + LOGIT_ROWS, C_BF:] = np.tile(a["b_f_2"].T, (2, 1))
    poolw = np.zeros((P, LAYERS_2, 2, P), f32)
    for l in range(LAYERS_2):
        for n in range(len(POOL_WINDOWS)):
            s = slice(64 * (n % 2), 64 * (n % 2) + 64)
            poolw[s, l, n // 2, s] = a["pool_w_2"][l, n]
    con, bias, con2 = constants()
    feature_major = lambda v: np.ascontiguousarray(v.reshape(-1, KD, P).transpose(2, 1, 0))
    arrays = {"x": feature_major(a["x"][0]), "meta": feature_major(a["meta_2"]), "par": par, "con": con,
              "bias": bias, "con2": con2, "poolw": poolw}
    arrays.update({f"w_{n}": w for n, w in weights.items()})

    nc = bacc.Bacc("TRN2", target_bir_lowering=False, num_devices=1)
    d = {n: nc.dram_tensor(n, v.shape, mybir.dt.float32, kind="ExternalInput").ap() for n, v in arrays.items()}
    out = nc.dram_tensor("out", (P, KD, SEQ), mybir.dt.float32, kind="ExternalOutput").ap()
    build(nc, d["x"], d["meta"], d["par"], d["con"], d["bias"], d["con2"], d["poolw"],
          {n: d[f"w_{n}"] for n in weights}, out)
    got = run_bass_kernel_spmd(nc, [arrays], core_ids=[0]).results[0]["out"]
    return np.ascontiguousarray(got.transpose(2, 1, 0).reshape(1, SEQ, D))
```
